# Optimizing a Trainium2 kernel written in Bass

```python
import jax
import jax.numpy as jnp
from jax import lax
import numpy as np

D_MODEL = 1024
BATCH = 1
SEQ = 512
DEPTH = 2
DEC_BATCH = 1
DEC_SEQ = 64
PAST_LEN = 512

CHUNK = 64
N_META = 16
Q_BLOCK = 128
N_EVEN = (DEPTH + 1) // 2
N_ODD = DEPTH // 2
HG_HEADS = 4
HG_DK = 128
HG_DV = 128
HG_QK = HG_HEADS * HG_DK
HG_VO = HG_HEADS * HG_DV
FOX_HEADS = 4
FOX_DH = 128
FOX_W = FOX_HEADS * FOX_DH
FOX_FORGET_INIT = 2.0
EVEN_IN = 2 * HG_QK + 2 * HG_VO + 3 * FOX_W + FOX_HEADS
EVEN_OUT = HG_VO + FOX_W
MLA_HEADS = 8
MLA_Q_LORA = 512
MLA_KV_LORA = 256
MLA_NOPE = 128
MLA_ROPE = 64
MLA_V = 128
ODD_IN = MLA_Q_LORA + MLA_KV_LORA + MLA_ROPE
ROPE_BASE = 10000.0
N_EXPERTS = 16
N_GROUPS = 4
EXPERTS_PER_GROUP = N_EXPERTS // N_GROUPS
TOP_K = 2
D_EXPERT = 256
ALPHA = (2 * DEPTH) ** 0.25
BETA = (8 * DEPTH) ** -0.25
LN_EPS = 1e-5
RMS_EPS = 1e-6

kernel_name = 'hybrid_streaming_encoder_step'

def layer_norm(x, g, b):
    xf = x.astype(jnp.float32)
    mu = jnp.mean(xf, axis=-1, keepdims=True)
    var = jnp.mean(jnp.square(xf - mu), axis=-1, keepdims=True)
    return ((xf - mu) * lax.rsqrt(var + LN_EPS) * g + b).astype(x.dtype)

def rms_norm(x, g):
    xf = x.astype(jnp.float32)
    return (xf * lax.rsqrt(jnp.mean(xf * xf, axis=-1, keepdims=True) + RMS_EPS) * g).astype(x.dtype)

def rope(x, pos):
    half = MLA_ROPE // 2
    inv = ROPE_BASE ** (-jnp.arange(half, dtype=jnp.float32) / half)
    ang = pos.astype(jnp.float32)[:, None] * inv[None, :]
    shape = (pos.shape[0],) + (1,) * (x.ndim - 3) + (half,)
    cos = jnp.cos(ang).reshape(shape)
    sin = jnp.sin(ang).reshape(shape)
    xf = x.astype(jnp.float32)
    x1, x2 = xf[..., :half], xf[..., half:]
    return jnp.concatenate([x1 * cos - x2 * sin, x1 * sin + x2 * cos], axis=-1).astype(x.dtype)

def block_attention(q, k, v, grp_q, grp_k, scale, bias_q=None, bias_k=None):
    B, Tq, H, Dk = q.shape
    qb = min(Q_BLOCK, Tq)
    nb = -(-Tq // qb)
    pad = nb * qb - Tq
    has_bias = bias_q is not None
    q_blocks = jnp.swapaxes(jnp.pad(q, ((0, 0), (0, pad), (0, 0), (0, 0))).reshape(B, nb, qb, H, Dk), 0, 1)
    g_blocks = jnp.pad(grp_q, (0, pad), constant_values=jnp.iinfo(jnp.int32).max).reshape(nb, qb)
    if has_bias:
        b_blocks = jnp.swapaxes(jnp.pad(bias_q, ((0, 0), (0, pad), (0, 0))).reshape(B, nb, qb, H), 0, 1)
        bias_kt = jnp.swapaxes(bias_k, 1, 2)[:, :, None, :]
        xs = (q_blocks, g_blocks, b_blocks)
    else:
        xs = (q_blocks, g_blocks)

    def one(blk):
        qi, gi = blk[0], blk[1]
        s = jnp.einsum('bqhd,bkhd->bhqk', qi, k).astype(jnp.float32) * scale
        if has_bias:
            s = s + jnp.swapaxes(blk[2], 1, 2)[..., None] - bias_kt
        visible = (grp_k[None, :] <= gi[:, None])[None, None]
        p = jax.nn.softmax(jnp.where(visible, s, -jnp.inf), axis=-1).astype(v.dtype)
        return jnp.einsum('bhqk,bkhd->bqhd', p, v)

    o = lax.map(one, xs)
    return jnp.swapaxes(o, 0, 1).reshape(B, nb * qb, H, -1)[:, :Tq]

def hgrn2_scan(q, lf, k, v, s0, chunk):
    B, T, H, DK = q.shape
    n = T // chunk

    def blocks(a):
        return jnp.moveaxis(a.reshape(B, n, chunk, H, a.shape[-1]), 1, 0)

    tri = jnp.tril(jnp.ones((chunk, chunk), dtype=bool))[None, :, :, None, None]

    def step(S, blk):
        qc, lfc, kc, vc = blk
        vc = vc.astype(jnp.float32)
        b = jnp.cumsum(lfc, axis=1)
        decay = jnp.exp(jnp.where(tri, b[:, :, None] - b[:, None, :], -jnp.inf))
        A = jnp.einsum('btshd,bshd->bhts', decay * qc[:, :, None].astype(jnp.float32), kc)
        o = jnp.einsum('bhts,bshv->bthv', A, vc) + jnp.einsum('bthd,bhdv->bthv', qc * jnp.exp(b), S)
        b_last = b[:, -1]
        S_new = jnp.exp(b_last)[..., None] * S + jnp.einsum('bshd,bshv->bhdv', kc * jnp.exp(b_last[:, None] - b), vc)
        return S_new, o

    S, o = lax.scan(step, s0.astype(jnp.float32), (blocks(q), blocks(lf), blocks(k), blocks(v)))
    return jnp.moveaxis(o, 0, 1).reshape(B, T, H, -1).astype(q.dtype), S

def hgrn2_segments(q, lf, k, v, s0, segments):
    outs = []
    s = s0
    start = 0
    for length, chunk in segments:
        sl = slice(start, start + length)
        o, s = hgrn2_scan(q[:, sl], lf[:, sl], k[:, sl], v[:, sl], s, chunk)
        outs.append(o)
        start += length
    return jnp.concatenate(outs, axis=1), s

def even_mixer(x, hg_s0, fox_k_past, fox_v_past, fox_lf_past, pos_q, pos_k, segments,
               lb, w_in, hg_norm_g, fox_fb, w_out):
    B, T, _ = x.shape
    z = jnp.einsum('btd,de->bte', x, w_in)
    c0 = HG_QK
    c1 = c0 + HG_QK
    c2 = c1 + HG_VO
    c3 = c2 + HG_VO
    c4 = c3 + FOX_W
    c5 = c4 + FOX_W
    c6 = c5 + FOX_W
    hq, hf, hi, hg, fq, fk, fv, ffg = jnp.split(z, [c0, c1, c2, c3, c4, c5, c6], axis=-1)
    zf = hf.astype(jnp.float32)
    lf_hg = jnp.log(lb + (1.0 - lb) * jax.nn.sigmoid(zf))
    k_hg = (1.0 - lb) * jax.nn.sigmoid(-zf)
    hd = lambda a: a.reshape(B, T, HG_HEADS, -1)
    o_hg, s_new = hgrn2_segments(hd(hq), hd(lf_hg), hd(k_hg), hd(hi), hg_s0, segments)
    o_hg = rms_norm(o_hg, hg_norm_g).reshape(B, T, HG_VO) * jax.nn.sigmoid(hg)
    fh = lambda a: a.reshape(B, T, FOX_HEADS, FOX_DH)
    q_f, k_new, v_new = fh(fq), fh(fk), fh(fv)
    lf_new = jax.nn.log_sigmoid((ffg + fox_fb).astype(jnp.float32))
    if fox_k_past is None:
        k_all, v_all, lf_all = k_new, v_new, lf_new
    else:
        k_all = jnp.concatenate([fox_k_past.astype(k_new.dtype), k_new], axis=1)
        v_all = jnp.concatenate([fox_v_past.astype(v_new.dtype), v_new], axis=1)
        lf_all = jnp.concatenate([fox_lf_past.astype(jnp.float32), lf_new], axis=1)
    F = jnp.cumsum(lf_all, axis=1)
    o_fox = block_attention(q_f, k_all, v_all, pos_q, pos_k, FOX_DH ** -0.5, F[:, -T:], F)
    mixed = jnp.concatenate([o_hg, o_fox.reshape(B, T, FOX_W).astype(o_hg.dtype)], axis=-1)
    y = jnp.einsum('bte,ed->btd', mixed, w_out)
    return y, s_new, k_new, v_new, lf_new

def odd_mixer(x, ckv_past, kpe_past, pos_q, grp_q, grp_k,
              w_in, q_norm_g, kv_norm_g, w_uq, w_uk, w_uv, w_out):
    B, T, _ = x.shape
    z = jnp.einsum('btd,de->bte', x, w_in)
    cq, ckv, kpe = jnp.split(z, [MLA_Q_LORA, MLA_Q_LORA + MLA_KV_LORA], axis=-1)
    cq = rms_norm(cq, q_norm_g)
    ckv = rms_norm(ckv, kv_norm_g)
    kpe = rope(kpe, pos_q)
    q = jnp.einsum('btc,ce->bte', cq, w_uq).reshape(B, T, MLA_HEADS, MLA_NOPE + MLA_ROPE)
    q = jnp.concatenate([q[..., :MLA_NOPE], rope(q[..., MLA_NOPE:], pos_q)], axis=-1)
    if ckv_past is None:
        ckv_all, kpe_all = ckv, kpe
    else:
        ckv_all = jnp.concatenate([ckv_past.astype(ckv.dtype), ckv], axis=1)
        kpe_all = jnp.concatenate([kpe_past.astype(kpe.dtype), kpe], axis=1)
    k_nope = jnp.einsum('bsc,chd->bshd', ckv_all, w_uk)
    v = jnp.einsum('bsc,chd->bshd', ckv_all, w_uv)
    k_rot = jnp.broadcast_to(kpe_all[:, :, None, :], k_nope.shape[:3] + (MLA_ROPE,)).astype(k_nope.dtype)
    k = jnp.concatenate([k_nope, k_rot], axis=-1)
    o = block_attention(q.astype(k.dtype), k, v, grp_q, grp_k, (MLA_NOPE + MLA_ROPE) ** -0.5)
    y = jnp.einsum('bte,ed->btd', o.reshape(B, T, MLA_HEADS * MLA_V), w_out)
    return y, ckv, kpe

def moe(x, router_w, router_bias, w_gate, w_up, w_down):
    B, T, D = x.shape
    scores = jax.nn.sigmoid(jnp.einsum('btd,de->bte', x, router_w).astype(jnp.float32))
    grouped = (scores + router_bias.astype(jnp.float32)).reshape(B, T, N_GROUPS, EXPERTS_PER_GROUP)
    group_score = jnp.sum(lax.top_k(grouped, TOP_K)[0], axis=-1)
    best = jnp.argmax(group_score, axis=-1)
    in_group = (jnp.arange(N_GROUPS) == best[..., None])[..., None]
    masked = jnp.where(in_group, grouped, -jnp.inf).reshape(B, T, N_EXPERTS)
    _, idx = lax.top_k(masked, TOP_K)
    w = jnp.take_along_axis(scores, idx, axis=-1)
    w = w / jnp.sum(w, axis=-1, keepdims=True)
    combine = jnp.sum(jax.nn.one_hot(idx, N_EXPERTS, dtype=jnp.float32) * w[..., None], axis=-2).astype(x.dtype)
    y = jnp.zeros_like(x)
    for e in range(N_EXPERTS):
        h = jax.nn.silu(x @ w_gate[e]) * (x @ w_up[e])
        y = y + (h @ w_down[e]).astype(x.dtype) * combine[..., e:e + 1]
    return y

def trunk(x, hg_s0, fox_k_c, fox_v_c, fox_lf_c, mla_ckv_c, mla_kpe_c, pos_q, pos_k, grp_q, grp_k, segments, p):
    lb_table = jnp.cumsum(jax.nn.softmax(p['hg_lb_logits'].astype(jnp.float32), axis=0), axis=0)
    hg_new, fk_new, fv_new, flf_new, ckv_new, kpe_new = [], [], [], [], [], []
    for l in range(DEPTH):
        if l % 2 == 0:
            e = l // 2
            if fox_k_c is None:
                past = (None, None, None)
            else:
                past = (fox_k_c[e], fox_v_c[e], fox_lf_c[e])
            y, s, kr, vr, lr = even_mixer(x, hg_s0[e], past[0], past[1], past[2], pos_q, pos_k, segments,
                                          lb_table[l], p['even_w_in'][e], p['hg_norm_g'][e],
                                          p['fox_forget_bias'][e], p['even_w_out'][e])
            hg_new.append(s)
            fk_new.append(kr)
            fv_new.append(vr)
            flf_new.append(lr)
        else:
            o = l // 2
            if mla_ckv_c is None:
                past = (None, None)
            else:
                past = (mla_ckv_c[o], mla_kpe_c[o])
            y, c, kp = odd_mixer(x, past[0], past[1], pos_q, grp_q, grp_k,
                                 p['mla_w_in'][o], p['mla_q_norm_g'][o], p['mla_kv_norm_g'][o],
                                 p['mla_w_uq'][o], p['mla_w_uk'][o], p['mla_w_uv'][o], p['mla_w_out'][o])
            ckv_new.append(c)
            kpe_new.append(kp)
        x = layer_norm(ALPHA * x + y.astype(x.dtype), p['ln_mix_g'][l], p['ln_mix_b'][l])
        f = moe(x, p['router_w'], p['router_bias'], p['moe_w_gate'][l], p['moe_w_up'][l], p['moe_w_down'][l])
        x = layer_norm(ALPHA * x + f, p['ln_ffn_g'][l], p['ln_ffn_b'][l])
    return (x, jnp.stack(hg_new), jnp.stack(fk_new), jnp.stack(fv_new), jnp.stack(flf_new),
            jnp.stack(ckv_new), jnp.stack(kpe_new))

def setup_inputs(seed: int = 0) -> dict:
    key = jax.random.key(seed)
    ks = jax.random.split(key, 32)
    nrm = lambda k, shape, scale: jax.random.normal(k, shape, jnp.float32) * scale
    return {
        'x_prompt': nrm(ks[0], (BATCH, SEQ, D_MODEL), 1.0),
        'x_sample': nrm(ks[1], (DEC_BATCH, DEC_SEQ, D_MODEL), 1.0),
        'state_hgrn2': nrm(ks[2], (N_EVEN, DEC_BATCH, HG_HEADS, HG_DK, HG_DV), 0.5),
        'cache_fox_k': nrm(ks[3], (N_EVEN, DEC_BATCH, PAST_LEN, FOX_HEADS, FOX_DH), 1.0),
        'cache_fox_v': nrm(ks[4], (N_EVEN, DEC_BATCH, PAST_LEN, FOX_HEADS, FOX_DH), 1.0),
        'cache_fox_logf': jax.nn.log_sigmoid(FOX_FORGET_INIT + nrm(ks[5], (N_EVEN, DEC_BATCH, PAST_LEN, FOX_HEADS), 1.0)),
        'cache_mla_ckv': nrm(ks[6], (N_ODD, DEC_BATCH, PAST_LEN, MLA_KV_LORA), 1.0),
        'cache_mla_kpe': nrm(ks[7], (N_ODD, DEC_BATCH, PAST_LEN, MLA_ROPE), 1.0),
        'meta_tokens': nrm(ks[8], (N_META, D_MODEL), 1.0),
        'even_w_in': nrm(ks[9], (N_EVEN, D_MODEL, EVEN_IN), D_MODEL ** -0.5),
        'hg_lb_logits': nrm(ks[10], (DEPTH + 1, HG_QK), 0.5),
        'hg_norm_g': 1.0 + nrm(ks[11], (N_EVEN, HG_HEADS, HG_DV), 0.05),
        'fox_forget_bias': FOX_FORGET_INIT + nrm(ks[12], (N_EVEN, FOX_HEADS), 0.1),
        'even_w_out': nrm(ks[13], (N_EVEN, EVEN_OUT, D_MODEL), BETA * EVEN_OUT ** -0.5),
        'mla_w_in': nrm(ks[14], (N_ODD, D_MODEL, ODD_IN), D_MODEL ** -0.5),
        'mla_q_norm_g': 1.0 + nrm(ks[15], (N_ODD, MLA_Q_LORA), 0.05),
        'mla_kv_norm_g': 1.0 + nrm(ks[16], (N_ODD, MLA_KV_LORA), 0.05),
        'mla_w_uq': nrm(ks[17], (N_ODD, MLA_Q_LORA, MLA_HEADS * (MLA_NOPE + MLA_ROPE)), MLA_Q_LORA ** -0.5),
        'mla_w_uk': nrm(ks[18], (N_ODD, MLA_KV_LORA, MLA_HEADS, MLA_NOPE), MLA_KV_LORA ** -0.5),
        'mla_w_uv': nrm(ks[19], (N_ODD, MLA_KV_LORA, MLA_HEADS, MLA_V), MLA_KV_LORA ** -0.5),
        'mla_w_out': nrm(ks[20], (N_ODD, MLA_HEADS * MLA_V, D_MODEL), BETA * (MLA_HEADS * MLA_V) ** -0.5),
        'ln_mix_g': 1.0 + nrm(ks[21], (DEPTH, D_MODEL), 0.05),
        'ln_mix_b': nrm(ks[22], (DEPTH, D_MODEL), 0.02),
        'ln_ffn_g': 1.0 + nrm(ks[23], (DEPTH, D_MODEL), 0.05),
        'ln_ffn_b': nrm(ks[24], (DEPTH, D_MODEL), 0.02),
        'router_w': nrm(ks[25], (D_MODEL, N_EXPERTS), D_MODEL ** -0.5),
        'router_bias': nrm(ks[26], (N_EXPERTS,), 0.01),
        'moe_w_gate': nrm(ks[27], (DEPTH, N_EXPERTS, D_MODEL, D_EXPERT), D_MODEL ** -0.5),
        'moe_w_up': nrm(ks[28], (DEPTH, N_EXPERTS, D_MODEL, D_EXPERT), D_MODEL ** -0.5),
        'moe_w_down': nrm(ks[29], (DEPTH, N_EXPERTS, D_EXPERT, D_MODEL), BETA * D_EXPERT ** -0.5),
    }

def reference(x_prompt, x_sample, state_hgrn2, cache_fox_k, cache_fox_v, cache_fox_logf, cache_mla_ckv, cache_mla_kpe,
              meta_tokens, even_w_in, hg_lb_logits, hg_norm_g, fox_forget_bias, even_w_out,
              mla_w_in, mla_q_norm_g, mla_kv_norm_g, mla_w_uq, mla_w_uk, mla_w_uv, mla_w_out,
              ln_mix_g, ln_mix_b, ln_ffn_g, ln_ffn_b, router_w, router_bias, moe_w_gate, moe_w_up, moe_w_down):
    p = {
        'even_w_in': even_w_in, 'hg_lb_logits': hg_lb_logits, 'hg_norm_g': hg_norm_g,
        'fox_forget_bias': fox_forget_bias, 'even_w_out': even_w_out,
        'mla_w_in': mla_w_in, 'mla_q_norm_g': mla_q_norm_g, 'mla_kv_norm_g': mla_kv_norm_g,
        'mla_w_uq': mla_w_uq, 'mla_w_uk': mla_w_uk, 'mla_w_uv': mla_w_uv, 'mla_w_out': mla_w_out,
        'ln_mix_g': ln_mix_g, 'ln_mix_b': ln_mix_b, 'ln_ffn_g': ln_ffn_g, 'ln_ffn_b': ln_ffn_b,
        'router_w': router_w, 'router_bias': router_bias,
        'moe_w_gate': moe_w_gate, 'moe_w_up': moe_w_up, 'moe_w_down': moe_w_down,
    }
    B, T = x_prompt.shape[0], x_prompt.shape[1]
    meta = jnp.broadcast_to(meta_tokens[None].astype(x_prompt.dtype), (B, N_META, D_MODEL))
    xp = jnp.concatenate([meta, x_prompt], axis=1)
    pos_p = jnp.arange(N_META + T, dtype=jnp.int32)
    grp_p = jnp.where(pos_p < N_META, -1, (pos_p - N_META) // CHUNK).astype(jnp.int32)
    s0_p = jnp.zeros((N_EVEN, B, HG_HEADS, HG_DK, HG_DV), jnp.float32)
    hp, hg_p, fk_p, fv_p, flf_p, ckv_p, kpe_p = trunk(
        xp, s0_p, None, None, None, None, None, pos_p, pos_p, grp_p, grp_p,
        ((N_META, N_META), (T, CHUNK)), p)
    y_prompt = hp[:, N_META:]
    Tn = x_sample.shape[1]
    P = cache_fox_k.shape[2]
    pos_s = P + jnp.arange(Tn, dtype=jnp.int32)
    pos_sk = jnp.arange(P + Tn, dtype=jnp.int32)
    hs, hg_s, fk_s, fv_s, flf_s, ckv_s, kpe_s = trunk(
        x_sample, state_hgrn2, cache_fox_k, cache_fox_v, cache_fox_logf, cache_mla_ckv, cache_mla_kpe,
        pos_s, pos_sk, pos_s // CHUNK, pos_sk // CHUNK, ((Tn, Tn),), p)
    return (y_prompt, hs, hg_p, fk_p, fv_p, flf_p, ckv_p, kpe_p, hg_s, fk_s, fv_s, flf_s, ckv_s, kpe_s)


_drawn_inputs = setup_inputs


def setup_inputs(seed=0):
    import zlib

    import numpy as np

    out = dict(_drawn_inputs(seed))
    spreads = {}
    factors = {'cache_mla_kpe': 4.63, 'mla_q_norm_g': 8.0}
    for name, (base, spread) in spreads.items():
        noise = np.random.default_rng([zlib.crc32(name.encode()), seed]).standard_normal(out[name].shape)
        drawn = base * np.exp(spread * noise) if base else spread * noise
        out[name] = jnp.asarray(drawn.astype(out[name].dtype))
    for name, factor in factors.items():
        out[name] = (out[name] * factor).astype(out[name].dtype)
    return out
```

```python
from contextlib import ExitStack

import numpy as np

import concourse.bass as bass
from concourse import mybir

F32 = mybir.dt.float32
BF16 = mybir.dt.bfloat16
I32 = mybir.dt.int32
ALU = mybir.AluOpType
ACT = mybir.ActivationFunctionType
AX = mybir.AxisListType.X

D = 1024
KD = D // 128
SEQ, NS, NM, PAST = 512, 64, 16, 512
TILES = [128, 128, 128, 128, NS + NM]
NT = len(TILES)
TOK = sum(TILES)
PAD = 128 * NT
META0 = SEQ + NS
HH, FH, MH = 4, 4, 8
DH = 128
QL, KVL, NOPE, ROPE = 512, 256, 128, 64
NE, DE = 16, 256
ALPHA = 4.0 ** 0.25
LN_EPS, RMS_EPS = 1e-5, 1e-6
LEVELS = [64, 32, 16, 8, 4, 2, 1]
NL = len(LEVELS)
NEG = -1e30
SLOT = 2048
NOV = 9
NSLOTS = (NE + NOV) * 128
UNIT_TILES = [4, 0, 1, 2, 3]
SC_FOX = DH ** -0.5
SC_MLA = (NOPE + ROPE) ** -0.5


def shape_constants():
    s = np.arange(128)[:, None]
    t = np.arange(128)[None, :]
    parts = {}
    parts["ident"] = (s == t).astype(np.float32)
    parts["iota"] = np.broadcast_to(t.astype(np.float32), (128, 128))
    reset = np.ones((128, PAD), np.float32)
    reset[:, 0:SEQ:128] = 0
    reset[:, SEQ] = 0
    reset[:, META0] = 0
    parts["reset"] = reset
    pos = np.zeros((NT, 128), np.float32)
    for i in range(4):
        pos[i] = NM + 128 * i + np.arange(128)
    pos[4, :NS] = PAST + np.arange(NS)
    pos[4, NS:NS + NM] = np.arange(NM)
    inv = np.float32(10000.0) ** (-np.arange(32, dtype=np.float32) / np.float32(32))
    ang = pos[:, :, None] * inv.astype(np.float32)[None, None, :]
    parts["cos"] = np.cos(ang).astype(np.float32).transpose(1, 0, 2).reshape(128, NT * 32)
    parts["sin"] = np.sin(ang).astype(np.float32).transpose(1, 0, 2).reshape(128, NT * 32)
    valid = np.ones((128, NT), np.float32)
    valid[NS + NM:, 4] = 0
    parts["valid"] = valid
    parts["prio4"] = np.broadcast_to(4.0 - np.arange(4), (128, 4))
    parts["prio16"] = np.broadcast_to(16.0 - np.arange(16), (128, 16))
    parts["base"] = np.broadcast_to(128.0 * np.arange(16), (128, 16))
    s3 = s[:, :, None]
    lev = []
    for L in LEVELS:
        lev.append((s // (2 * L) == t // (2 * L)) & (s % (2 * L) < L) & (t % (2 * L) >= L))
    lev.append(s == t)
    parts["lev"] = np.stack(lev, 1).reshape(128, 8 * 128).astype(np.float32)
    unmasked = np.zeros((128, 384))
    parts["m_causal"] = np.concatenate([unmasked, np.where(t <= s, 0, NEG)], 1)
    parts["m_group"] = np.concatenate([unmasked, np.where((s < 64) & (t >= 64), NEG, 0)], 1)
    c80 = np.arange(80)[None, :]
    parts["m_meta"] = np.broadcast_to(np.where(c80 < NS, NEG, 0), (128, 80))
    parts["m_past"] = np.broadcast_to(np.where(s < NS, 0, NEG), (128, PAST))
    same = (s < NS) == (c80 < NS)
    parts["m_own_fox"] = np.where(same & (c80 <= s), 0, NEG)
    parts["m_own_mla"] = np.where(same, 0, NEG)
    parts["before"] = (s < t).astype(np.float32)
    parts["ones"] = np.ones((128, 128), np.float32)
    parts["tok"] = np.stack([np.broadcast_to(np.arange(NT), (128, NT)),
                             np.broadcast_to(s, (128, NT))], 2).reshape(128, 2 * NT)
    where, n = {}, 0
    for name, a in parts.items():
        where[name] = (n, n + a.shape[1])
        n += a.shape[1]
    blob = np.concatenate([np.ascontiguousarray(a, np.float32) for a in parts.values()], 1)
    return blob, where


class Signal:

    def __init__(self, sem, keys, step=1):
        self.sem = sem
        self.at = {k: (n + 1) * step for n, k in enumerate(keys)}
        self.total = len(self.at) * step

    def __getitem__(self, key):
        return self.sem, self.at[key]


class Chain:

    def __init__(self, eng, sem):
        self.eng, self.sem, self.n = eng, sem, 0

    def __call__(self, ins):
        ins.then_inc(self.sem, 1)
        self.n += 1
        self.eng.wait_ge(self.sem, self.n)

    def mark(self, ins):
        ins.then_inc(self.sem, 1)
        self.n += 1
        return self.n

    def wait(self, n):
        self.eng.wait_ge(self.sem, n)


def build_step(nc, const_where, consts, a, o):
    (y_prompt, y_sample, hg_prompt, fk_prompt, fv_prompt, flf_prompt, ckv_prompt, kpe_prompt,
     hg_sample, fk_sample, fv_sample, flf_sample, ckv_sample, kpe_sample) = o

    x_rows = [nc.dram_tensor(f"x_rows{s}", [TOK, D], F32).ap() for s in range(3)]
    y_all = nc.dram_tensor("y_rows", [NSLOTS, D], F32).ap()
    y_rows = [y_all, y_all]

    ctx = ExitStack()
    with ctx:
        def sb(name, shape, dt=F32):
            return ctx.enter_context(nc.sbuf_tensor(name, shape, dt))

        def sem(name):
            return ctx.enter_context(nc.semaphore(name))

        def signal(name, keys, step=1):
            return Signal(sem(name), keys, step)

        n_f32 = const_where["lev"][0]
        n_all = consts.shape[1]
        cst = sb("cst", [128, n_f32])
        cstb = sb("cstb", [128, n_all - n_f32], BF16)
        identb = sb("identb", [128, 128], BF16)
        iotab = sb("iotab", [128, 128], BF16)

        def const(name):
            lo, hi = const_where[name]
            return cst[:, lo:hi] if lo < n_f32 else cstb[:, lo - n_f32:hi - n_f32]

        ident, reset = const("ident"), const("reset")
        cos = const("cos").rearrange("p (i d) -> p i d", i=NT)
        sin = const("sin").rearrange("p (i d) -> p i d", i=NT)
        lev = const("lev").rearrange("p (l t) -> p l t", l=8)
        tok2 = const("tok").rearrange("p (i c) -> p i c", c=2)

        xT = sb("xT", [128, KD, TOK])
        mixT = sb("mixT", [128, 4, TOK])
        ring = sb("ring", [128, 6 * SLOT])
        xr = sb("xr", [128, 2, D])
        rb = sb("rb", [128, 2, D])
        lng = sb("lng", [128, 2, D])
        rw = sb("rw", [128, KD, NE])
        small = sb("small", [128, 768])
        ints = sb("ints", [128, 64], I32)
        ARENA = 22528
        arena = sb("arena", [128, ARENA])

        cursor = [0]

        def col(n):
            c = cursor[0]
            cursor[0] += n
            assert cursor[0] <= 768
            return small[:, c:c + n]

        psum = [ctx.enter_context(nc.psum_tensor(f"pair{p}", [128, 1024], F32)) for p in range(4)]

        class Region:
            def __init__(self, start=0):
                self.n = start

            def take(self, words):
                v = arena[:, self.n:self.n + words]
                self.n += words
                assert self.n <= ARENA, self.n
                return v

        r0 = Region()
        fq = r0.take(4 * TOK).rearrange("p (h t) -> p h t", h=4)
        fkT = r0.take(4 * TOK).rearrange("p (h t) -> p h t", h=4)
        hg_start = r0.n
        hv = r0.take(NT * 512).rearrange("p (i n) -> p i n", i=NT)
        hgate = r0.take(NT * 512).rearrange("p (i n) -> p i n", i=NT)
        qk = r0.take(2 * 2 * PAD).rearrange("p (b s t) -> p b s t", b=2, s=2)
        bn = r0.take(2 * 2 * PAD).rearrange("p (b s t) -> p b s t", b=2, s=2)
        x_in = arena[:, r0.n:r0.n + NT * D].rearrange("p (i n) -> p i n", i=NT)
        qe = r0.take(2 * PAD).rearrange("p (b t) -> p b t", b=2)
        kd = r0.take(2 * PAD).rearrange("p (b t) -> p b t", b=2)
        gbuf = r0.take(2 * NL * 128).rearrange("p (b l t) -> p b l t", b=2, l=NL)
        am = lng[:, 0, :]
        junk = lng[:, 1, :]
        asb = r0.take(2 * 128).rearrange("p (b t) -> p b t", b=2)
        kdT = r0.take(2 * 128).rearrange("p (b t) -> p b t", b=2)
        og = r0.take(2 * 128).rearrange("p (b t) -> p b t", b=2)
        sp_ = r0.take(4 * 128).rearrange("p (h t) -> p h t", h=4)
        ss_ = r0.take(4 * 128).rearrange("p (h t) -> p h t", h=4)
        ft = rb[:, :, :].rearrange("p b n -> p (b n)")[:, 0:3 * PAD].rearrange("p (b t) -> p b t", b=3)
        hgn = xr[:, 0, 0:512]
        consts_in = arena[:, 0:n_all - n_f32]
        r1 = Region(hg_start)
        fv = r1.take(NT * 512).rearrange("p (i n) -> p i n", i=NT)
        kpT = r1.take(4 * PAST).rearrange("p (h t) -> p h t", h=4)
        vp = r1.take(4 * 512).rearrange("p (j n) -> p j n", j=4)
        fks = r1.take(2 * 512).rearrange("p (b n) -> p b n", b=2)
        kps = r1.take(4 * 512).rearrange("p (b n) -> p b n", b=4)
        nfb = r1.take(2 * 592).rearrange("p (s t) -> p s t", s=2)
        lf = r1.take(PAST + TOK)
        ff = r1.take(PAST + TOK)
        l1, l2 = r1.take(TOK), r1.take(TOK)
        sel4 = r1.take(4 * 128).rearrange("p (h t) -> p h t", h=4)
        ATT = 2 * 592 + 2 * 128 + 2 * 640
        r1.n = max(r1.n, ARENA - ATT)
        probs = r1.take(2 * 592).rearrange("p (b t) -> p b t", b=2)
        diag = r1.take(2 * 128).rearrange("p (b t) -> p b t", b=2)
        pT = r1.take(2 * 640).rearrange("p (b t) -> p b t", b=2)
        r2 = Region()
        cqT = r2.take(4 * TOK).rearrange("p (k t) -> p k t", k=4)
        ckT = r2.take(2 * TOK).rearrange("p (k t) -> p k t", k=2)
        ckpT = r2.take(2 * PAST).rearrange("p (k t) -> p k t", k=2)
        peT, pepT = r2.take(TOK), r2.take(PAST)
        qpT = r2.take(4 * TOK).rearrange("p (k t) -> p k t", k=4)
        qnT = r2.take(4 * TOK).rearrange("p (k t) -> p k t", k=4)
        knT = r2.take(4 * TOK).rearrange("p (k t) -> p k t", k=4)
        knpT = r2.take(4 * PAST).rearrange("p (k t) -> p k t", k=4)
        r3 = Region(r2.n)
        mv_ = r2.take(9 * 512).rearrange("p (j n) -> p j n", j=9)
        assert r2.n <= ARENA - ATT
        cqb = r3.take(2 * 512).rearrange("p (b n) -> p b n", b=2)
        cvb = r3.take(2 * 256).rearrange("p (b n) -> p b n", b=2)
        kpb = r3.take(2 * 128).rearrange("p (b n) -> p b n", b=2)
        qpb = r3.take(2 * 512).rearrange("p (b n) -> p b n", b=2)
        assert r3.n <= r2.n
        r3 = Region(r2.n - 4608 - 4 * PAST)
        pst = r3.take(4 * 384).rearrange("p (b n) -> p b n", b=4)
        rtmp = arena[:, ARENA - ATT:ARENA - ATT + 1024].rearrange("p (b n) -> p b n", b=4)
        qng = arena[:, ARENA - ATT + 1024:ARENA - ATT + 1024 + 768]
        r4 = Region()
        wexp = r4.take(6 * SLOT)
        xg = r4.take(2 * D).rearrange("p (b n) -> p b n", b=2)
        xgT = r4.take(2 * D).rearrange("p (b k n) -> p b k n", b=2, k=KD)
        yb = r4.take(2 * D).rearrange("p (b n) -> p b n", b=2)
        eg = r4.take(2 * 256).rearrange("p (b n) -> p b n", b=2)
        hb = r4.take(2 * 256).rearrange("p (b n) -> p b n", b=2)
        hT = r4.take(2 * 256).rearrange("p (b n) -> p b n", b=2)
        oneh = r4.take(2 * 5 * 64).bitcast(BF16).rearrange("p (b i t) -> p b i t", b=2, i=NT)
        r5 = Region()
        yg = r5.take(4 * D).rearrange("p (b n) -> p b n", b=4)

        lb, omlb, tl = col(4), col(4), col(12).rearrange("p (j c) -> p j c", j=3)
        mx4, se4 = col(4), col(4)
        eps_rms, eps_ln, one = col(1), col(1), col(1)
        ebl = col(12).rearrange("p (b c) -> p b c", b=2)
        hstat = col(4)
        fb4 = col(1)
        amax, nmax, rsum, rinv = col(2), col(2), col(2), col(2)
        lst = col(24).rearrange("p (b c) -> p b c", b=2)
        lmv = col(4).rearrange("p (b c) -> p b c", b=2)
        lrs = col(4).rearrange("p (b c) -> p b c", b=2)
        mst = col(8).rearrange("p (b c) -> p b c", b=2)
        rbias = col(16)
        lg = col(NT * NE).rearrange("p (i e) -> p i e", i=NT)
        sc_ = col(NT * NE).rearrange("p (i e) -> p i e", i=NT)
        mk = col(NT * NE).rearrange("p (i e) -> p i e", i=NT)
        sel1 = col(NT * NE).rearrange("p (i e) -> p i e", i=NT)
        gs = col(NT * 4).rearrange("p (i e) -> p i e", i=NT)
        gs2 = col(NT * 4).rearrange("p (i e) -> p i e", i=NT)
        t5a, t5b = col(NT), col(NT)
        wts = col(2 * NT).rearrange("p (c i) -> p c i", c=2)
        posf = col(2 * NT).rearrange("p (c i) -> p c i", c=2)
        rk1 = col(NT * NE).rearrange("p (i e) -> p i e", i=NT)
        cnt, ovn, ovend = col(16), col(16), col(16)
        cur = col(4)
        RW = arena[:, ARENA - 1024:ARENA]

        def rtile(n):
            return RW[:, n * 80:(n + 1) * 80].rearrange("p (i e) -> p i e", i=NT)

        maskb = sb("maskb", [128, NT * NE], BF16)
        posi = ints[:, 0:10].rearrange("p (c i) -> p c i", c=2)
        sloti = ints[:, 16:32]
        ovi = ints[:, 32:36]

        order = {0: [], 1: [], 2: [], 3: []}
        pair_of = {}
        alt = [0]

        def ticket(key, pair=None):
            if pair is None:
                pair = alt[0] % 2
                alt[0] += 1
            order[pair].append(key)
            pair_of[key] = pair

        HG_ORDER = [("q", 0), ("f", 0), ("q", 1), ("f", 1), ("U", 0), ("q", 2), ("flush", 0), ("f", 2),
                    ("U", 1), ("q", 3), ("flush", 1), ("f", 3), ("U", 2), ("fq", 0), ("flush", 2),
                    ("fq", 1), ("fq", 2), ("fq", 3), ("U", 3), ("fk", 0), ("flush", 3)]
        units = [(h, i) for h in range(HH) for i in UNIT_TILES]
        fox_units = [("fox", h, i) for h in range(FH) for i in range(NT)]
        mla_units = [("mla", h, i) for h in range(MH) for i in range(NT)]
        att_units = fox_units + mla_units
        for i in range(NT):
            ticket(("T", -1, i))
        for i in range(NT):
            ticket(("v", i))
        for i in range(NT):
            ticket(("g", i))
        for kind, n in HG_ORDER:
            if kind == "U":
                for u in range(5 * n, 5 * n + 5):
                    ticket(("A", u), 2)
            elif kind != "flush":
                ticket((kind, n), 0)
        alt[0] = 1
        for i in range(1, NT + 1):
            if i < NT:
                ticket(("fk", i))
            ticket(("fkt", i - 1))
        for i in range(NT):
            ticket(("fv", i))
        ticket(("lf",))
        for j in range(4):
            ticket(("kp", j))
        for n, (_, h, i) in enumerate(fox_units):
            if i == 0:
                ticket(("nf", h, 0))
                ticket(("nf", h, 1))
            ticket(("S", n))
            ticket(("PT", n), 2 + n % 2)

        def plan_out(l):
            for i in range(NT):
                ticket(("wo", l, i))
                ticket(("T", 2 * l, i), 2)
                ticket(("lg", l, i), 3)
            ticket(("rk", l), 0)
            for e in range(0, NE, 1):
                pass
            ticket(("ix", l), 1)

        plan_out(0)
        for i in range(NT):
            ticket(("T", 1, i), 2)
        alt[0] = 0
        for i in range(NT):
            ticket(("mi", i))
            ticket(("mt", i), 2)
        for j in range(4):
            ticket(("pt", j), 3)
        for i in range(NT):
            ticket(("qp", i))
            ticket(("qt", i), 2)
        for g in range(2):
            for h in range(4):
                ticket(("qn", g, h))
                ticket(("kn", g, h))
                ticket(("knp", g, h))
            for j in range(9):
                ticket(("mv", g, j))
            for n in range(20 + 20 * g, 40 + 20 * g):
                ticket(("S", n))
                ticket(("PT", n), 2 + n % 2)
        plan_out(1)

        kdT_bank, o_bank = psum[1][:, 0:128], psum[1][:, 512:640]
        s_bank, ogT_bank = psum[3][:, 0:256], psum[3][:, 512:640]

        class Pairs:

            def __init__(self, what):
                self.of = [signal(f"pair{p}_{what}", order[p]) for p in range(4)]

            def sem(self, key):
                return self.of[pair_of[key]].sem

            def __getitem__(self, key):
                return self.of[pair_of[key]][key]

        pe_full = Pairs("full")
        ps_free = Pairs("free")
        before = {}
        for p in range(4):
            for prev, k in zip(order[p], order[p][1:]):
                before[k] = prev

        def claim(pe, key):
            if key in before:
                pe.wait_ge(*ps_free[before[key]])
            return psum[pair_of[key]]

        def filled(eng, key):
            eng.wait_ge(*pe_full[key])
            return psum[pair_of[key]]

        class Written:

            def __init__(self, key_of):
                self.key_of = key_of

            def __getitem__(self, k):
                return ps_free[self.key_of(k)]

        cst_in = signal("constants_loaded", ["all"], 32)
        cst_b = signal("constants_ready", ["dve"])
        vec_in = signal("vectors_loaded", ["all"], 16 * 6)
        state_in = signal("states_loaded", ["all"], 16)
        past_in = signal("past_fox_loaded", ["all"], 16 * 9)
        pastm_in = signal("past_mla_loaded", ["all"], 16 * 12)
        mg_in = signal("mla_gains_loaded", ["all"], 32)
        x_loaded = signal("x_loaded", ["all"], 16 * 6)
        evac = Written(lambda k: k)
        lb_done = signal("lower_bound_logits_ready", ["max"])
        lb_e = signal("lower_bound_exps_ready", ["exp"])
        v_sb = Written(lambda i: ("v", i))
        g_exp = signal("gate_exp_written", list(range(NT)))
        g_sb = signal("gate_written", list(range(NT)))
        q_sb = Written(lambda h: ("q", h))
        f_exp = signal("f_exp_written", list(range(HH)))
        f_sig = signal("f_written", list(range(HH)))
        f_ln = signal("log_f_written", list(range(HH)))
        b_sb = signal("b_written", list(range(HH)))
        nb_sb = signal("minus_b_written", list(range(HH)))
        eb_sb = signal("exp_b_written", list(range(HH)))
        qe_sb = signal("decayed_q_k_written", list(range(HH)))
        d_sb = signal("decay_exponents_written", list(range(20)))
        de_sb = signal("decays_written", list(range(20)))
        gm_sb = signal("decayed_levels_written", list(range(20)))
        a_sb = signal("A_written", list(range(20)))
        kdT_ps = signal("kd_transposed", list(range(20)))
        kdT_sb = signal("kdT_written", list(range(20)))
        o_ps = signal("o_in_psum", list(range(20)))
        s_ps = signal("S_in_psum", list(range(20)))
        s_sb = signal("S_written", list(range(20)))
        o_rs = signal("o_rms_ready", list(range(20)))
        og_sb = signal("gated_o_written", list(range(20)))
        ogT_ps = signal("gated_o_transposed", list(range(20)))
        ogT_sb = signal("mixed_hg_written", list(range(20)))
        zero_st = signal("overflow_rows_zeroed", ["all"], 16 * NOV)
        st_hg = signal("hg_states_stored", ["all"], 32)
        fk_st = [signal(f"fox_k_stored{b}", [(i, p) for i in range(b, NT, 2)
                                             for p in range(2 if i == 4 else 1)], 16) for b in range(2)]
        fv_st = signal("fox_v_stored", ["all"], 16 * 6)
        fq_sb = Written(lambda h: ("fq", h))
        fk_sb = Written(lambda i: ("fk", i))
        fkt_sb = Written(lambda i: ("fkt", i))
        fv_sb = Written(lambda i: ("fv", i))
        lf_x = signal("forget_logit_written", ["x"])
        lf_l = signal("forget_log_written", ["x"])
        lf_sb = signal("forget_sums_written", ["x"])
        lf_st = signal("logf_stored", ["all"], 48)
        kp_sb = Written(lambda j: ("kp", j))
        N_ATT = len(att_units)
        mx_sb = signal("row_max_ready", list(range(N_ATT)))
        ex_sb = signal("probs_written", list(range(N_ATT)))
        dg_sb = signal("row_scale_written", list(range(N_ATT)))
        pT_a = signal("pT_blocks_written", list(range(N_ATT)))
        pT_b = signal("pT_own_written", list(range(N_ATT)))
        oT_ps = signal("oT_in_psum", list(range(N_ATT)))
        lnk = [(s, i) for s in range(4) for i in range(NT)]
        xr_in = [signal(f"residual_loaded{b}", [(s, i, c) for s in range(4) for i in range(b, NT, 2)
                                                for c in range(2 if (s == 0 and i == 4) else 1)], 16)
                 for b in range(2)]
        r_mv = signal("ln_stats_ready", lnk)
        r_rs = signal("ln_scale_ready", lnk)
        r_n = signal("ln_gain_applied", lnk)
        r_sb = signal("ln_written", lnk)
        x_st = [signal(f"rows_stored{b}", [(s, i) for s in range(4) for i in range(b, NT, 2)], 16)
                for b in range(2)]
        lng_in = signal("ln_params_loaded", list(range(4)), 32)
        lg_sb = Written(lambda k: ("lg", *k))
        r_e = signal("router_exp_written", [0, 1])
        mk_sb = signal("expert_mask_written", [0, 1])
        rt_sb = signal("router_done", [0, 1])
        oh_sb = signal("onehots_written", [(l, e) for l in range(2) for e in range(NE)])
        oh_us = signal("onehots_used", [(l, e) for l in range(2) for e in range(NE)])
        ix_sb = signal("slot_tokens_written", [0, 1])
        mi_a = signal("mla_squares_ready", list(range(NT)))
        mi_sb = signal("mla_latents_written", list(range(NT)))
        mt_sb = Written(lambda i: ("mt", i))
        mi_st = [signal(f"mla_stored{b}", [(i, c) for i in range(b, NT, 2)
                                           for c in range(4 if i == 4 else 2)], 16) for b in range(2)]
        pt_sb = Written(lambda j: ("pt", j))
        qp_sb = signal("q_rope_written", list(range(NT)))
        qt_sb = Written(lambda i: ("qt", i))
        qn_sb = Written(lambda k: ("qn", *k))
        kn_sb = Written(lambda k: ("kn", *k))
        knp_sb = Written(lambda k: ("knp", *k))
        mvs_sb = Written(lambda k: ("mv", *k))
        ALLE = [(l, e) for l in range(2) for e in range(NE)]
        we_in = [signal(f"expert_weights_loaded{b}", [le for le in ALLE if le[1] % 4 == b], 48)
                 for b in range(4)]
        xg_in = [signal(f"expert_rows_loaded{b}", [le for le in ALLE if le[1] % 2 == b], 16) for b in range(2)]
        xgT_ps = signal("expert_rows_transposed", ALLE)
        xgT_sa = signal("expert_rowsT_written_act", ALLE)
        xgT_sd = signal("expert_rowsT_written_dve", ALLE)
        gu_ps = signal("gate_up_in_psum", ALLE)
        eg_sb = signal("gate_exp_ready", ALLE)
        h_sb = signal("hidden_written", ALLE)
        hT_ps = signal("hidden_transposed", ALLE)
        hT_sb = signal("hiddenT_written", ALLE)
        dn_ps = signal("down_in_psum", ALLE)
        y_sa = signal("expert_out_written_act", ALLE)
        y_sd = signal("expert_out_written_dve", ALLE)
        y_st = [signal(f"expert_out_stored{b}", [le for le in ALLE if le[1] % 2 == b], 16) for b in range(2)]
        yg_in = [signal(f"token_rows_gathered{b}", [(l, i, c) for l in range(2) for i in range(b, NT, 2)
                                                    for c in range(2)], 16) for b in range(2)]
        c_dve, c_act, c_pool = sem("dve_steps"), sem("act_steps"), sem("pool_steps")
        ov = [{k: sem(f"ov_{k}{l}") for k in ("cnt", "oh", "ix", "id", "xg", "tx", "xt", "w", "gu", "ex",
                                              "h", "ht", "hs", "dn", "y", "st", "turn")} for l in range(2)]

        w_in_d = a["even_w_in"][0].rearrange("(k p) n -> p k n", p=128)
        mi_d = a["mla_w_in"][0].rearrange("(k p) n -> p k n", p=128)
        items = []

        def item(name, slot, nslots, src, last):
            k, n = src.shape[1], src.shape[2]
            view = ring[:, slot * SLOT:slot * SLOT + k * n].rearrange("p (k n) -> p k n", k=k)
            items.append((name, slot, nslots, src, last, view))

        for name, c, slot, last in (("v", 2, 0, ("v", 4)), ("g", 3, 2, ("g", 4)), ("q", 0, 4, ("q", 3)),
                                    ("f", 1, 0, ("f", 3)), ("fq", 4, 2, ("fq", 3)), ("fk", 5, 4, ("fk", 4)),
                                    ("fv", 6, 0, ("fv", 4))):
            item(name, slot, 2, w_in_d[:, :, 512 * c:512 * c + 512], last)
        wo_d = [a[n][0].rearrange("(k p) n -> p k n", p=128) for n in ("even_w_out", "mla_w_out")]
        item(("wo", 0, 0), 2, 2, wo_d[0][:, :, 0:512], ("wo", 0, 4))
        item(("wo", 0, 1), 4, 2, wo_d[0][:, :, 512:1024], ("wo", 0, 4))
        n_items0 = len(items)
        item("mi0", 0, 2, mi_d[:, :, 0:512], ("mi", 4))
        item("mi1", 2, 2, mi_d[:, :, 512:832], ("mi", 4))
        item("uk", 4, 1, a["mla_w_uk"][0].rearrange("(k p) h d -> p k (h d)", p=128), ("knp", 1, 3))
        item("uv", 5, 1, a["mla_w_uv"][0].rearrange("(k p) h d -> p k (h d)", p=128), ("mv", 1, 8))
        item("uq", 0, 3, a["mla_w_uq"][0].rearrange("(k p) n -> p k n", p=128), ("qn", 1, 3))
        item(("wo", 1, 0), 3, 2, wo_d[1][:, :, 0:512], ("wo", 1, 4))
        item(("wo", 1, 1), 0, 2, wo_d[1][:, :, 512:1024], ("wo", 1, 4))
        w_in = [signal(f"weights_loaded{s}", [it[0] for it in items if it[1] == s], 16) for s in range(6)]
        w_ff = sb("w_ff", [128, KD, 4])

        def weights(pe, name):
            it = next(x for x in items if x[0] == name)
            pe.wait_ge(*w_in[it[1]][name])
            return it[5]

        def earlier_users(n):
            _, slot, ns, *_ = items[n]
            out = []
            for m in range(n - 1, -1, -1):
                if items[m][1] < slot + ns and slot < items[m][1] + items[m][2]:
                    out.append(items[m][4])
            return out

        def expert_place(e):
            base = (ring if e % 4 < 2 else wexp)[:, (e % 2) * 3 * SLOT:(e % 2) * 3 * SLOT + 3 * SLOT]
            gu = base[:, 0:2 * SLOT].rearrange("p (k n) -> p k n", k=KD)
            dn = base[:, 2 * SLOT:3 * SLOT].rearrange("p (k n) -> p k n", k=2)
            return gu, dn

        gate_d = a["moe_w_gate"].rearrange("l e (k p) n -> (l e) p k n", p=128)
        up_d = a["moe_w_up"].rearrange("l e (k p) n -> (l e) p k n", p=128)
        down_d = a["moe_w_down"].rearrange("l e (k p) n -> (l e) p k n", p=128)

        def mixed(k, i):
            src = mixT[:, k, :] if k < 4 else xT[:, k, :]
            return src[:, 128 * i:128 * i + TILES[i]]

        def att_rows(i):
            return (4 if i == 4 else i + 1), TILES[i]

        def row_dst(i, prompt, sample):
            if i < 4:
                return [((0, 128), prompt[NM + 128 * i:NM + 128 * i + 128, :])]
            return [((0, NS), sample[:, :]), ((NS, NS + NM), prompt[0:NM, :])]

        def pairs(view, L):
            part = list(view.ap[0])
            both = bass.AP(view.tensor, view.offset, [part, [2 * L, 64 // L], [PAD + L, 2], [1, L]])
            mid = bass.AP(view.tensor, view.offset + L - 1, [part, [2 * L, 64 // L], [PAD, 2], [0, L]])
            return both, mid

        block = ctx.enter_context(nc.Block())

        @block.sync
        def _(sp):
            def load_item(n):
                name, slot, _, src, _, view = items[n]
                for last in earlier_users(n):
                    sp.wait_ge(*pe_full[last])
                sp.dma_start(view, src).then_inc(w_in[slot].sem, 16)

            def load_expert(l, e):
                gu, dn = expert_place(e)
                s = we_in[e % 4].sem
                sp.dma_start(gu[:, :, 0:DE], gate_d[l * NE + e]).then_inc(s, 16)
                sp.dma_start(gu[:, :, DE:2 * DE], up_d[l * NE + e]).then_inc(s, 16)
                sp.dma_start(dn, down_d[l * NE + e]).then_inc(s, 16)

            for n in range(n_items0):
                load_item(n)
            for l in range(2):
                last_att = 19 if l == 0 else N_ATT - 1
                sp.wait_ge(*oT_ps[last_att])
                if l == 0:
                    sp.wait_ge(*fv_st["all"])
                    for b in range(2):
                        sp.wait_ge(fk_st[b].sem, fk_st[b].total)
                    sp.wait_ge(*st_hg["all"])
                    sp.wait_ge(*lf_st["all"])
                else:
                    for b in range(2):
                        sp.wait_ge(mi_st[b].sem, mi_st[b].total)
                load_expert(l, 2)
                load_expert(l, 3)
                sp.wait_ge(*pe_full[("wo", l, 4)])
                load_expert(l, 0)
                load_expert(l, 1)
                for e in range(NE):
                    if e + 4 < NE:
                        sp.wait_ge(*dn_ps[(l, e)])
                        load_expert(l, e + 4)
                    sp.wait_ge(*y_sa[(l, e)])
                    sp.wait_ge(*y_sd[(l, e)])
                    sp.dma_start(y_rows[l][128 * e:128 * e + 128, :], yb[:, e % 2, :]).then_inc(y_st[e % 2].sem, 16)
                    if l == 0 and e == 13:
                        for n in range(n_items0, n_items0 + 4):
                            load_item(n)
                mk = ov[l]
                sp.wait_ge(*ix_sb[l])
                count = sp.value_load(ovi[0:1, 0:1], min_val=0, max_val=NOV)
                with sp.Fori(0, NOV) as b:
                    with sp.If(count > b):
                        sp.wait_ge(*dn_ps[(l, 14)])
                        sp.wait_ge(mk["id"], b + 1)
                        sp.sem_inc(mk["turn"], 1)
                        ex = sp.value_load(ovi[0:1, 1:2], min_val=0, max_val=NE - 1)
                        gu, dn = expert_place(2)
                        le = ex + l * NE
                        sp.dma_start(gu[:, :, 0:DE], gate_d[bass.ds(le, 1)].rearrange("o p k n -> p (o k) n")
                                     ).then_inc(mk["w"], 16)
                        sp.dma_start(gu[:, :, DE:2 * DE], up_d[bass.ds(le, 1)].rearrange("o p k n -> p (o k) n")
                                     ).then_inc(mk["w"], 16)
                        sp.dma_start(dn, down_d[bass.ds(le, 1)].rearrange("o p k n -> p (o k) n")
                                     ).then_inc(mk["w"], 16)
                        sp.wait_ge(mk["y"], b + 1)
                        sp.dma_start(y_rows[l][bass.ds(b * 128 + NE * 128, 128), :], yb[:, 0, :]
                                     ).then_inc(mk["st"], 16)
                        sp.wait_ge(mk["st"], b * 16 + 16)
                        sp.sem_inc(mk["turn"], 1)
                if l == 0:
                    for n in range(n_items0 + 4, len(items)):
                        load_item(n)
            for s in (st_hg, fv_st, lf_st, *fk_st, *mi_st, *x_st, *y_st):
                sp.wait_ge(s.sem, s.total)

        @block.gpsimd
        def _(pool):
            zrow = xr[:, 1, :]
            pool.memset(zrow, 0.0).then_inc(c_pool, 1)
            pool.wait_ge(c_pool, 1)
            xf = [a["x_prompt"][0], a["x_sample"][0], a["meta_tokens"]]
            st_hg_dst = [hg_prompt[0, 0].rearrange("h k v -> k h v"), hg_sample[0, 0].rearrange("h k v -> k h v")]

            for n in range(NOV):
                pool.dma_start(y_all[128 * (NE + n):128 * (NE + n) + 128, :], zrow).then_inc(zero_st.sem, 16)

            for u, (h, i) in enumerate(units):
                if i == 4:
                    pool.wait_ge(*nb_sb[h])
                    pool.wait_ge(*b_sb[h])
                if u >= 2:
                    pool.wait_ge(*pe_full[("A", u - 2)])
                for n, L in enumerate(LEVELS):
                    both, mid = pairs(bn[:, h % 2, 0, 128 * i:128 * i + 128], L)
                    dst = gbuf[:, u % 2, n, :].rearrange("p (q s r) -> p q s r", s=2, r=L)
                    last = pool.tensor_tensor(dst, both, mid, ALU.subtract)
                last.then_inc(d_sb.sem, 1)
            pool.wait_ge(*s_sb[19])
            pool.dma_start(st_hg_dst[0], sp_).then_inc(st_hg.sem, 16)
            pool.dma_start(st_hg_dst[1], ss_).then_inc(st_hg.sem, 16)
            pool.wait_ge(st_hg.sem, 32)
            pool.wait_ge(*og_sb[19])
            pool.wait_ge(*ogT_ps[19])
            pool.dma_start(vp, a["cache_fox_v"][0, 0].rearrange("(j p) h d -> p j (h d)", p=128)).then_inc(past_in.sem, 16)
            pool.dma_start(kps, a["cache_fox_k"][0, 0].rearrange("(j p) h d -> p j (h d)", p=128)).then_inc(past_in.sem, 16)
            pool.dma_start(lf[0:4, 0:PAST], a["cache_fox_logf"][0, 0].rearrange("t h -> h t"),
                           allow_slow_non_contiguous=True).then_inc(past_in.sem, 16)

            def store_rows(i, tile, prompt, sample, sm):
                for (lo, hi), dst in row_dst(i, prompt, sample):
                    pool.dma_start(dst, tile[lo:hi, :]).then_inc(sm, 16)

            k2 = [fk_prompt[0, 0].rearrange("t h d -> t (h d)"), fk_sample[0, 0].rearrange("t h d -> t (h d)")]
            v2 = [fv_prompt[0, 0].rearrange("t h d -> t (h d)"), fv_sample[0, 0].rearrange("t h d -> t (h d)")]
            for i in range(NT):
                pool.wait_ge(*fk_sb[i])
                store_rows(i, fks[:, i % 2, :], k2[0], k2[1], fk_st[i % 2].sem)
            for i in range(NT):
                pool.wait_ge(*fv_sb[i])
                store_rows(i, fv[:, i, :], v2[0], v2[1], fv_st.sem)
            pool.wait_ge(*lf_sb["x"])
            fp = flf_prompt[0, 0].rearrange("t h -> h t")
            pool.dma_start(fp[:, NM:NM + SEQ], lf[0:4, PAST:PAST + SEQ], allow_slow_non_contiguous=True).then_inc(lf_st.sem, 16)
            pool.dma_start(fp[:, 0:NM], lf[0:4, PAST + META0:PAST + TOK], allow_slow_non_contiguous=True).then_inc(lf_st.sem, 16)
            pool.dma_start(flf_sample[0, 0].rearrange("t h -> h t"), lf[0:4, PAST + SEQ:PAST + META0],
                           allow_slow_non_contiguous=True).then_inc(lf_st.sem, 16)

            def load_residual(s, i):
                b = i % 2
                if i >= 2:
                    pool.wait_ge(*r_mv[(s, i - 2)])
                elif s > 0:
                    pool.wait_ge(*r_mv[(s - 1, 4 - (b == 1))])
                if s == 0:
                    if i < 4:
                        pool.dma_start(xr[:, b, :], xf[0][128 * i:128 * i + 128, :]).then_inc(xr_in[b].sem, 16)
                    else:
                        pool.dma_start(xr[0:NS, b, :], xf[1][:, :]).then_inc(xr_in[b].sem, 16)
                        pool.dma_start(xr[NS:NS + NM, b, :], xf[2][:, :]).then_inc(xr_in[b].sem, 16)
                else:
                    pool.wait_ge(*x_st[b][(s - 1, i)])
                    pool.dma_start(xr[0:TILES[i], b, :], x_rows[s - 1][128 * i:128 * i + TILES[i], :]
                                   ).then_inc(xr_in[b].sem, 16)

            def layer_norm_rows(s):
                gn, bnm = (("ln_mix_g", "ln_mix_b"), ("ln_ffn_g", "ln_ffn_b"))[s % 2]
                if s > 0:
                    pool.wait_ge(*r_sb[(s - 1, 4)])
                pool.dma_start(lng[:, 0, :], a[gn][s // 2].partition_broadcast(128)).then_inc(lng_in.sem, 16)
                pool.dma_start(lng[:, 1, :], a[bnm][s // 2].partition_broadcast(128)).then_inc(lng_in.sem, 16)
                load_residual(s, 0)
                load_residual(s, 1)
                if s % 2 == 1:
                    gather_rows(s // 2, 0)
                    gather_rows(s // 2, 1)
                pool.wait_ge(*lng_in[s])
                for i in range(NT):
                    P = TILES[i]
                    pool.wait_ge(*r_n[(s, i)])
                    pool.tensor_tensor(rb[0:P, i % 2, :], rb[0:P, i % 2, :], lng[0:P, 1, :], ALU.add).then_inc(r_sb.sem, 1)
                    pool.wait_ge(*r_sb[(s, i)])
                    t = rb[:, i % 2, :]
                    if s < 3:
                        pool.dma_start(x_rows[s][128 * i:128 * i + P, :], t[0:P, :]).then_inc(x_st[i % 2].sem, 16)
                    elif i < 4:
                        pool.dma_start(y_prompt[0, 128 * i:128 * i + 128, :], t).then_inc(x_st[i % 2].sem, 16)
                    else:
                        pool.dma_start(y_sample[0], t[0:NS, :]).then_inc(x_st[i % 2].sem, 16)
                    if i + 2 < NT:
                        load_residual(s, i + 2)
                        if s % 2 == 1:
                            gather_rows(s // 2, i + 2)

            def gather_rows(l, i):
                P = TILES[i]
                if i == 0:
                    pool.wait_ge(*zero_st["all"])
                    for b in range(2):
                        pool.wait_ge(y_st[b].sem, (l + 1) * 16 * (NE // 2))
                if i >= 2:
                    pool.wait_ge(*r_mv[(2 * l + 1, i - 2)])
                for c in range(2):
                    pool.indirect_dma_start(
                        yg[0:P, 2 * (i % 2) + c, :], None, y_rows[l],
                        bass.IndirectOffsetOnAxis(ap=posi[0:P, c, i:i + 1], axis=0)).then_inc(yg_in[i % 2].sem, 16)

            def experts(l):
                pool.wait_ge(*ix_sb[l])
                for b in range(2):
                    last = (2 * l, 4 if b == 0 else 3)
                    pool.wait_ge(*x_st[b][last])
                for e in range(NE):
                    if e >= 2:
                        pool.wait_ge(*xgT_ps[(l, e - 2)])
                    pool.indirect_dma_start(
                        xg[:, e % 2, :], None, x_rows[2 * l],
                        bass.IndirectOffsetOnAxis(ap=sloti[:, e:e + 1], axis=0)).then_inc(xg_in[e % 2].sem, 16)
                m = ov[l]
                pool.wait_ge(*xgT_ps[(l, NE - 1)])
                count = pool.value_load(ovi[0:1, 0:1], min_val=0, max_val=NOV)
                with pool.Fori(0, NOV) as b:
                    with pool.If(count > b):
                        pool.wait_ge(m["id"], b + 1)
                        pool.sem_inc(m["turn"], 1)
                        pool.indirect_dma_start(xg[:, 0, :], None, x_rows[2 * l],
                                                bass.IndirectOffsetOnAxis(ap=ovi[:, 2:3], axis=0)
                                                ).then_inc(m["xg"], 16)
                        pool.wait_ge(m["xg"], b * 16 + 16)
                        pool.wait_ge(m["st"], b * 16 + 16)

            pool.wait_ge(*zero_st["all"])
            pool.wait_ge(*g_sb[4])
            layer_norm_rows(0)
            experts(0)
            layer_norm_rows(1)
            pool.dma_start(qng[:, 0:QL], a["mla_q_norm_g"][0].partition_broadcast(128)).then_inc(mg_in.sem, 16)
            pool.dma_start(qng[:, QL:QL + KVL], a["mla_kv_norm_g"][0].partition_broadcast(128)).then_inc(mg_in.sem, 16)
            pool.dma_start(pst[:, :, 0:256], a["cache_mla_ckv"][0, 0].rearrange("(j p) n -> p j n", p=128)).then_inc(pastm_in.sem, 16)
            for c in range(2):
                pool.dma_start(pst[:, :, 256 + 64 * c:320 + 64 * c],
                               a["cache_mla_kpe"][0, 0].rearrange("(j p) n -> p j n", p=128)).then_inc(pastm_in.sem, 16)
            for i in range(NT):
                pool.wait_ge(*mi_sb[i])
                store_rows(i, cvb[:, i % 2, :], ckv_prompt[0, 0], ckv_sample[0, 0], mi_st[i % 2].sem)
                store_rows(i, kpb[:, i % 2, 0:ROPE], kpe_prompt[0, 0], kpe_sample[0, 0], mi_st[i % 2].sem)
            layer_norm_rows(2)
            experts(1)
            layer_norm_rows(3)

        @block.tensor
        def _(pe):
            def transpose_tile(s, i, src):
                P = TILES[i]
                ps = claim(pe, ("T", s, i))
                for k in range(KD):
                    last = pe.transpose(ps[:, 128 * k:128 * k + P], src[0:P, 128 * k:128 * k + 128], ident[0:P, 0:P])
                last.then_inc(pe_full.sem(("T", s, i)), 1)

            def to_tokens(key, i, w, n, chunks=KD, src=None, sl=None):
                P = TILES[i]
                ps = claim(pe, key)
                for k in range(chunks):
                    last = pe.matmul(ps[0:P, 0:n], xT[:, k, 128 * i:128 * i + P], w[:, k, :],
                                     start=(k == 0), stop=(k == chunks - 1))
                last.then_inc(pe_full.sem(key), 1)

            def to_features(key, w, src, ncol):
                ps = claim(pe, key)
                chunks = src.shape[1]
                for lo in range(0, ncol, 512):
                    hi = min(lo + 512, ncol)
                    for k in range(chunks):
                        last = pe.matmul(ps[0:w.shape[2], lo:hi], w[:, k, :], src[:, k, lo:hi],
                                         start=(k == 0), stop=(k == chunks - 1))
                last.then_inc(pe_full.sem(key), 1)

            pe.wait_ge(*cst_in["all"])
            pe.wait_ge(x_loaded.sem, 16 * 6)
            for i in range(NT):
                transpose_tile(-1, i, x_in[:, i, :])
            pe.wait_ge(*evac[("T", -1, 4)])
            pe.wait_ge(*evac[("T", -1, 3)])
            for nm in ("v", "g"):
                w = weights(pe, nm)
                for i in range(NT):
                    to_tokens((nm, i), i, w, 512)

            def unit_a(u):
                h, i = units[u]
                P, c0 = TILES[i], 128 * i
                pe.wait_ge(*gm_sb[u])
                ps = claim(pe, ("A", u))
                n0 = 1 if i == 4 else 0
                for n in range(n0, NL):
                    pe.matmul(ps[0:P, 128 * n:128 * n + P], gbuf[:, u % 2, n, 0:P], gbuf[:, u % 2, n, 0:P],
                              start=True, stop=True)
                pe.matmul(ps[0:P, 896:896 + P], qk[:, h % 2, 0, c0:c0 + P], qk[:, h % 2, 1, c0:c0 + P],
                               start=True, stop=True).then_inc(pe_full.sem(("A", u)), 1)

            def unit_b(u):
                h, i = units[u]
                P, c0, hc = TILES[i], 128 * i, slice(128 * h, 128 * h + 128)
                pe.wait_ge(*qe_sb[h])
                if u > 0:
                    pe.wait_ge(*kdT_sb[u - 1])
                pe.transpose(kdT_bank[0:P, :], kd[:, h % 2, c0:c0 + P], ident).then_inc(kdT_ps.sem, 1)
                pe.wait_ge(*a_sb[u])
                if u > 0:
                    pe.wait_ge(*og_sb[u - 1])
                    pe.wait_ge(*s_sb[u - 1])
                oo = o_bank
                if i == 4:
                    pe.wait_ge(*state_in["all"])
                    pe.matmul(oo[NS:P, :], asb[0:P, u % 2, NS:P], hv[0:P, i, hc], start=True, stop=True)
                    pe.matmul(oo[0:NS, :], asb[0:P, u % 2, 0:NS], hv[0:P, i, hc], start=True, stop=False)
                    last = pe.matmul(oo[0:NS, :], qe[:, h % 2, SEQ:META0], ss_[:, h, :], start=False, stop=True)
                else:
                    pe.matmul(oo[0:P, :], asb[0:P, u % 2, 0:P], hv[0:P, i, hc], start=True, stop=False)
                    last = pe.matmul(oo[0:P, :], qe[:, h % 2, c0:c0 + P], sp_[:, h, :], start=False, stop=True)
                last.then_inc(o_ps.sem, 1)
                pe.wait_ge(*kdT_sb[u])
                if i == 4:
                    pe.matmul(s_bank[:, 0:128], kdT[NS:NS + NM, u % 2, :], hv[NS:NS + NM, 4, hc], start=True, stop=True)
                    last = pe.matmul(s_bank[:, 128:256], kdT[0:NS, u % 2, :], hv[0:NS, 4, hc], start=True, stop=True)
                else:
                    last = pe.matmul(s_bank[:, 0:128], kdT[0:P, u % 2, :], hv[0:P, i, hc], start=True, stop=True)
                last.then_inc(s_ps.sem, 1)

            def unit_c(u):
                P = TILES[units[u][1]]
                pe.wait_ge(*og_sb[u])
                if u > 0:
                    pe.wait_ge(*ogT_sb[u - 1])
                pe.transpose(ogT_bank[:, 0:P], og[0:P, u % 2, :], ident[0:P, 0:P]).then_inc(ogT_ps.sem, 1)

            def fk_step(i):
                to_tokens(("fk", i), i, weights(pe, "fk"), 512)

            for kind, n in HG_ORDER:
                if kind in ("q", "f", "fq"):
                    w = weights(pe, kind)
                    to_features((kind, n), w[:, :, 128 * n:128 * n + 128], xT, TOK)
                elif kind == "fk":
                    fk_step(n)
                elif kind == "U":
                    if n == 0:
                        pe.wait_ge(*v_sb[4])
                        pe.wait_ge(*ps_free[("g", 4)])
                        pe.wait_ge(*ps_free[("g", 3)])
                    for m in range(5):
                        u = 5 * n + m
                        unit_a(u)
                        if m >= 1:
                            unit_b(u - 1)
                        if m >= 2:
                            unit_c(u - 2)
                else:
                    u = 5 * n + 4
                    unit_b(u)
                    unit_c(u - 1)
                    unit_c(u)

            pe.wait_ge(*kdT_sb[19])
            pe.wait_ge(*og_sb[19])
            for i in range(1, NT + 1):
                if i < NT:
                    fk_step(i)
                j = i - 1
                P = TILES[j]
                pe.wait_ge(*fk_sb[j])
                ps = claim(pe, ("fkt", j))
                for h in range(4):
                    last = pe.transpose(ps[:, 128 * h:128 * h + P], fks[0:P, j % 2, 128 * h:128 * h + 128], ident[0:P, 0:P])
                last.then_inc(pe_full.sem(("fkt", j)), 1)
            w = weights(pe, "fv")
            for i in range(NT):
                to_tokens(("fv", i), i, w, 512)
            pe.wait_ge(vec_in.sem, vec_in.total)
            to_features(("lf",), w_ff, xT, TOK)
            pe.wait_ge(past_in.sem, 48)
            for j in range(4):
                ps = claim(pe, ("kp", j))
                for h in range(4):
                    last = pe.transpose(ps[:, 128 * h:128 * h + 128], kps[:, j, 128 * h:128 * h + 128], ident)
                last.then_inc(pe_full.sem(("kp", j)), 1)

            def att_scores(n):
                kind, h, i = att_units[n]
                nb, P = att_rows(i)
                W, c0 = 128 * nb, 128 * i
                ps = claim(pe, ("S", n))
                own, blk = ps[0:P, 432:512], ps[0:P, 512:512 + W]
                if kind == "fox":
                    lq = [fq[:, h, c0:c0 + P]]
                    ko = [fkT[:, h, 512:TOK]]
                    kb = [kpT[:, h, :] if i == 4 else fkT[:, h, 0:W]]
                    m_own, m_diag = const("m_own_fox"), const("m_causal")
                else:
                    hh, r = h % 4, slice(64 * (h % 2), 64 * (h % 2) + 64)
                    lq = [qnT[:, hh, c0:c0 + P], qpT[r, h // 2, c0:c0 + P]]
                    ko = [knT[:, hh, 512:TOK], peT[r, 512:TOK]]
                    kb = [knpT[:, hh, :], pepT[r, :]] if i == 4 else [knT[:, hh, 0:W], peT[r, 0:W]]
                    m_own, m_diag = const("m_own_mla"), const("m_group")
                m_own = m_own if i == 4 else const("m_meta")
                m_blk = const("m_past") if i == 4 else m_diag[:, 512 - W:512]
                for dst, keys, mask in ((own, ko, m_own), (blk, kb, m_blk)):
                    for c, (q_, k_) in enumerate(zip(lq, keys)):
                        pe.matmul(dst, q_, k_, start=(c == 0), stop=False)
                    last = pe.matmul(dst, identb[0:P, 0:P], mask[0:P, :], start=False, stop=True)
                last.then_inc(pe_full.sem(("S", n)), 1)

            def att_transpose(n):
                _, _, i = att_units[n]
                nb, P = att_rows(i)
                pe.wait_ge(*ex_sb[n])
                pe.wait_ge(*dg_sb[n])
                ps = claim(pe, ("PT", n))
                d = diag[0:P, n % 2, 0:P]
                pe.matmul(ps[0:80, 0:P], probs[0:P, n % 2, 0:80], d, start=True, stop=True)
                for j in range(nb):
                    last = pe.matmul(ps[:, 512 + 128 * j:512 + 128 * j + P],
                                     probs[0:P, n % 2, 80 + 128 * j:208 + 128 * j], d, start=True, stop=True)
                last.then_inc(pe_full.sem(("PT", n)), 1)

            def att_values(n):
                kind, h, i = att_units[n]
                nb, P = att_rows(i)
                pe.wait_ge(*pT_a[n])
                pe.wait_ge(*pT_b[n])
                out = psum[pair_of[("PT", n)]][:, 256:256 + P]
                if kind == "fox":
                    hc = slice(128 * h, 128 * h + 128)
                    vo, vb = fv[0:80, 4, hc], [(vp if i == 4 else fv)[:, j, hc] for j in range(nb)]
                else:
                    hc = slice(128 * (h % 4), 128 * (h % 4) + 128)
                    vo, vb = mv_[0:80, 4, hc], [mv_[:, (5 + j) if i == 4 else j, hc] for j in range(nb)]
                pe.matmul(out, vo, pT[0:80, n % 2, 512:512 + P], start=True, stop=False)
                for j in range(nb):
                    last = pe.matmul(out, vb[j], pT[:, n % 2, 128 * j:128 * j + P], start=False, stop=(j == nb - 1))
                last.then_inc(oT_ps.sem, 1)

            def attention(first, last):
                for n in range(first, last + 2):
                    if n < last:
                        kind, h, i = att_units[n]
                        if kind == "fox" and i == 0:
                            for s in range(2):
                                ps = claim(pe, ("nf", h, s))
                                lo = 512 - 512 * s
                                if s == 0:
                                    pe.matmul(ps[:, 0:512], sel4[0:4, h, :], ff[0:4, 512:1024], start=True, stop=True)
                                    m = pe.matmul(ps[:, 512:592], sel4[0:4, h, :], ff[0:4, 1024:PAST + TOK], start=True, stop=True)
                                else:
                                    m = pe.matmul(ps[:, 0:512], sel4[0:4, h, :], ff[0:4, 0:512], start=True, stop=True)
                                m.then_inc(pe_full.sem(("nf", h, s)), 1)
                        att_scores(n)
                    if n - 2 >= first:
                        att_values(n - 2)
                    if first <= n - 1 < last:
                        att_transpose(n - 1)

            pe.wait_ge(*lf_sb["x"])
            pe.wait_ge(*fq_sb[3])
            pe.wait_ge(*fkt_sb[4])
            pe.wait_ge(*kp_sb[3])
            pe.wait_ge(*fv_sb[4])
            pe.wait_ge(*ogT_sb[19])
            pe.wait_ge(*s_sb[19])
            attention(0, 20)

            def out_and_experts(l):
                w0, w1 = weights(pe, ("wo", l, 0)), weights(pe, ("wo", l, 1))
                lastn = 19 if l == 0 else N_ATT - 1
                pe.wait_ge(*ps_free[("PT", lastn)])
                pe.wait_ge(*ps_free[("PT", lastn - 1)])
                for i in range(NT):
                    P = TILES[i]
                    ps = claim(pe, ("wo", l, i))
                    for half, w in ((0, w0), (1, w1)):
                        for k in range(KD):
                            last = pe.matmul(ps[0:P, 512 * half:512 * half + 512], mixed(k, i), w[:, k, :],
                                             start=(k == 0), stop=(k == KD - 1))
                    last.then_inc(pe_full.sem(("wo", l, i)), 1)
                    if i >= 1:
                        after_norm(l, i - 1)
                after_norm(l, NT - 1)
                pe.wait_ge(*mk_sb[l])
                ps = claim(pe, ("rk", l))
                for i in range(NT):
                    m = maskb[:, NE * i:NE * i + NE]
                    for j in range(i):
                        pe.matmul(ps[:, NE * i:NE * i + NE], const("ones"), maskb[:, NE * j:NE * j + NE],
                                  start=(j == 0), stop=False)
                    pe.matmul(ps[:, NE * i:NE * i + NE], const("before"), m, start=(i == 0), stop=True)
                for j in range(NT):
                    last = pe.matmul(ps[:, 80:96], const("ones"), maskb[:, NE * j:NE * j + NE],
                                     start=(j == 0), stop=(j == NT - 1))
                last.then_inc(pe_full.sem(("rk", l)), 1)
                ps = claim(pe, ("ix", l))
                for e in range(NE):
                    pe.wait_ge(*oh_sb[(l, e)])
                    for i in range(NT):
                        last = pe.matmul(ps[:, 2 * e:2 * e + 2], oneh[:, e % 2, i, :], tok2[:, i, :],
                                         start=(i == 0), stop=(i == NT - 1))
                    if e == NE - 1:
                        last.then_inc(pe_full.sem(("ix", l)), 1)
                    else:
                        last.then_inc(oh_us.sem, 1)
                pe.wait_ge(*ps_free[("ix", l)])
                pe.wait_ge(*ps_free[("lg", l, 4)])
                pe.wait_ge(*ps_free[("T", 2 * l, 4)])
                experts(l)

            def after_norm(l, i):
                P = TILES[i]
                pe.wait_ge(*r_sb[(2 * l, i)])
                transpose_tile(2 * l, i, rb[:, i % 2, :])
                pe.wait_ge(*evac[("T", 2 * l, i)])
                ps = claim(pe, ("lg", l, i))
                for k in range(KD):
                    last = pe.matmul(ps[0:P, 0:NE], xT[:, k, 128 * i:128 * i + P], rw[:, k, :],
                                     start=(k == 0), stop=(k == KD - 1))
                last.then_inc(pe_full.sem(("lg", l, i)), 1)

            def prev(le):
                n = ALLE.index(le)
                return ALLE[n - 1] if n else None

            def rows_t(l, e):
                pe.wait_ge(*xg_in[e % 2][(l, e)])
                if e > 0:
                    pe.wait_ge(*xgT_sa[(l, e - 1)])
                    pe.wait_ge(*xgT_sd[(l, e - 1)])
                for k in range(KD):
                    last = pe.transpose(psum[0][:, 128 * k:128 * k + 128], xg[:, e % 2, 128 * k:128 * k + 128], ident)
                last.then_inc(xgT_ps.sem, 1)

            def gate_up(l, e):
                pe.wait_ge(*we_in[e % 4][(l, e)])
                pe.wait_ge(*xgT_sa[(l, e)])
                pe.wait_ge(*xgT_sd[(l, e)])
                if e >= 2:
                    pe.wait_ge(*h_sb[(l, e - 2)])
                gu, _ = expert_place(e)
                bank = psum[1][:, 512 * (e % 2):512 * (e % 2) + 512]
                for k in range(KD):
                    last = pe.matmul(bank, xgT[:, e % 2, k, :], gu[:, k, :], start=(k == 0), stop=(k == KD - 1))
                last.then_inc(gu_ps.sem, 1)

            def hidden_t(l, e):
                pe.wait_ge(*h_sb[(l, e)])
                if e > 0:
                    pe.wait_ge(*hT_sb[(l, e - 1)])
                for k in range(2):
                    last = pe.transpose(psum[3][:, 128 * k:128 * k + 128], hb[:, e % 2, 128 * k:128 * k + 128], ident)
                last.then_inc(hT_ps.sem, 1)

            def down(l, e):
                pe.wait_ge(*hT_sb[(l, e)])
                if e > 0:
                    pe.wait_ge(*y_sa[(l, e - 1)])
                    pe.wait_ge(*y_sd[(l, e - 1)])
                _, dn = expert_place(e)
                for half in range(2):
                    for k in range(2):
                        last = pe.matmul(psum[2][:, 512 * half:512 * half + 512], hT[:, e % 2, 128 * k:128 * k + 128],
                                         dn[:, k, 512 * half:512 * half + 512], start=(k == 0), stop=(k == 1))
                last.then_inc(dn_ps.sem, 1)

            def experts(l):
                rows_t(l, 0)
                for e in range(NE + 1):
                    if e < NE:
                        gate_up(l, e)
                    if e >= 1:
                        hidden_t(l, e - 1)
                    if e + 1 < NE:
                        rows_t(l, e + 1)
                    if e >= 1:
                        down(l, e - 1)
                m = ov[l]
                pe.wait_ge(*y_sa[(l, NE - 1)])
                pe.wait_ge(*y_sd[(l, NE - 1)])
                pe.wait_ge(*ix_sb[l])
                count = pe.value_load(ovi[0:1, 0:1], min_val=0, max_val=NOV)
                with pe.Fori(0, NOV) as b:
                    with pe.If(count > b):
                        pe.wait_ge(m["oh"], b + 1)
                        for c in range(2):
                            for i in range(NT):
                                last = pe.matmul(psum[3][:, 512:514], oneh[:, c, i, :], tok2[:, i, :],
                                                 start=(c == 0 and i == 0), stop=(c == 1 and i == NT - 1))
                        last.then_inc(m["ix"], 1)
                        pe.wait_ge(m["xg"], b * 16 + 16)
                        for k in range(KD):
                            last = pe.transpose(psum[0][:, 128 * k:128 * k + 128], xg[:, 0, 128 * k:128 * k + 128], ident)
                        last.then_inc(m["tx"], 1)
                        pe.wait_ge(m["xt"], b + 1)
                        pe.wait_ge(m["w"], b * 48 + 48)
                        gu, dn = expert_place(2)
                        for k in range(KD):
                            last = pe.matmul(psum[1][:, 0:512], xgT[:, 0, k, :], gu[:, k, :], start=(k == 0), stop=(k == KD - 1))
                        last.then_inc(m["gu"], 1)
                        pe.wait_ge(m["h"], b + 1)
                        for k in range(2):
                            last = pe.transpose(psum[3][:, 128 * k:128 * k + 128], hb[:, 0, 128 * k:128 * k + 128], ident)
                        last.then_inc(m["ht"], 1)
                        pe.wait_ge(m["hs"], b + 1)
                        for half in range(2):
                            for k in range(2):
                                last = pe.matmul(psum[2][:, 512 * half:512 * half + 512], hT[:, 0, 128 * k:128 * k + 128],
                                                 dn[:, k, 512 * half:512 * half + 512], start=(k == 0), stop=(k == 1))
                        last.then_inc(m["dn"], 1)

            out_and_experts(0)
            for i in range(NT):
                pe.wait_ge(*r_sb[(1, i)])
                transpose_tile(1, i, rb[:, i % 2, :])
            wq, wkv = weights(pe, "mi0"), weights(pe, "mi1")

            def latents_t(i):
                P = TILES[i]
                pe.wait_ge(*mi_sb[i])
                ps = claim(pe, ("mt", i))
                for k in range(4):
                    pe.transpose(ps[:, 128 * k:128 * k + P], cqb[0:P, i % 2, 128 * k:128 * k + 128], ident[0:P, 0:P])
                for k in range(2):
                    pe.transpose(ps[:, 512 + 128 * k:512 + 128 * k + P], cvb[0:P, i % 2, 128 * k:128 * k + 128], ident[0:P, 0:P])
                pe.transpose(ps[:, 768:768 + P], kpb[0:P, i % 2, :], ident[0:P, 0:P]).then_inc(pe_full.sem(("mt", i)), 1)

            for i in range(NT):
                P = TILES[i]
                pe.wait_ge(*evac[("T", 1, i)])
                ps = claim(pe, ("mi", i))
                for w, lo, n in ((wq, 0, 512), (wkv, 512, 320)):
                    for k in range(KD):
                        last = pe.matmul(ps[0:P, lo:lo + n], xT[:, k, 128 * i:128 * i + P], w[:, k, :],
                                         start=(k == 0), stop=(k == KD - 1))
                last.then_inc(pe_full.sem(("mi", i)), 1)
                if i >= 1:
                    latents_t(i - 1)
            latents_t(NT - 1)
            pe.wait_ge(pastm_in.sem, 48)
            for j in range(4):
                ps = claim(pe, ("pt", j))
                for k in range(3):
                    last = pe.transpose(ps[:, 128 * k:128 * k + 128], pst[:, j, 128 * k:128 * k + 128], ident)
                last.then_inc(pe_full.sem(("pt", j)), 1)
            uq = weights(pe, "uq")

            def rope_t(i):
                P = TILES[i]
                pe.wait_ge(*qp_sb[i])
                ps = claim(pe, ("qt", i))
                for k in range(4):
                    last = pe.transpose(ps[:, 128 * k:128 * k + P], qpb[0:P, i % 2, 128 * k:128 * k + 128], ident[0:P, 0:P])
                last.then_inc(pe_full.sem(("qt", i)), 1)

            for i in range(NT):
                P = TILES[i]
                pe.wait_ge(*mt_sb[i])
                ps = claim(pe, ("qp", i))
                for k in range(4):
                    rope_cols = uq[:, k, :].rearrange("p (h n) -> p h n", h=MH)[:, :, NOPE:NOPE + ROPE]
                    last = pe.matmul(ps[0:P, 0:512], cqT[:, k, 128 * i:128 * i + P], rope_cols,
                                     start=(k == 0), stop=(k == 3))
                last.then_inc(pe_full.sem(("qp", i)), 1)
                if i >= 1:
                    rope_t(i - 1)
            rope_t(NT - 1)
            uk, uv = weights(pe, "uk"), weights(pe, "uv")
            pe.wait_ge(*pt_sb[3])
            for g in range(2):
                for h in range(4):
                    hd = 4 * g + h
                    to_features(("qn", g, h), uq[:, :, 192 * hd:192 * hd + 128], cqT, TOK)
                    to_features(("kn", g, h), uk[:, :, 128 * hd:128 * hd + 128], ckT, TOK)
                    to_features(("knp", g, h), uk[:, :, 128 * hd:128 * hd + 128], ckpT, PAST)
                for j in range(9):
                    ps = claim(pe, ("mv", g, j))
                    P = TILES[j] if j < 5 else 128
                    src = ckT[:, :, 128 * j:128 * j + P] if j < 5 else ckpT[:, :, 128 * (j - 5):128 * (j - 5) + 128]
                    for k in range(2):
                        last = pe.matmul(ps[0:P, 0:512], src[:, k, :], uv[:, k, 512 * g:512 * g + 512],
                                         start=(k == 0), stop=(k == 1))
                    last.then_inc(pe_full.sem(("mv", g, j)), 1)
                pe.wait_ge(*qt_sb[4])
                pe.wait_ge(*mvs_sb[(g, 8)])
                pe.wait_ge(*qn_sb[(g, 3)])
                pe.wait_ge(*kn_sb[(g, 3)])
                pe.wait_ge(*knp_sb[(g, 3)])
                attention(20 + 20 * g, 40 + 20 * g)
            out_and_experts(1)

        @block.scalar
        def _(act):
            chain = Chain(act, c_act)
            copy = act.copy

            act.dma_start(cst[:, :], consts[:, 0:n_f32]).then_inc(cst_in.sem, 16)
            act.dma_start(consts_in, consts[:, n_f32:n_all]).then_inc(cst_in.sem, 16)
            for i in range(4):
                act.dma_start(x_in[:, i, :], a["x_prompt"][0, 128 * i:128 * i + 128, :]).then_inc(x_loaded.sem, 16)
            act.dma_start(x_in[0:NS, 4, :], a["x_sample"][0]).then_inc(x_loaded.sem, 16)
            act.dma_start(x_in[NS:NS + NM, 4, :], a["meta_tokens"]).then_inc(x_loaded.sem, 16)
            act.dma_start(hgn, a["hg_norm_g"][0].rearrange("h v -> (h v)").partition_broadcast(128)).then_inc(vec_in.sem, 16)
            act.dma_start(tl, a["hg_lb_logits"].rearrange("j (c p) -> p j c", p=128),
                          allow_slow_non_contiguous=True).then_inc(vec_in.sem, 16)
            act.dma_start(fb4[0:4, :], a["fox_forget_bias"].rearrange("o h -> h o"),
                          allow_slow_non_contiguous=True).then_inc(vec_in.sem, 16)
            act.dma_start(rw[:, :, :], a["router_w"].rearrange("(k p) n -> p k n", p=128)).then_inc(vec_in.sem, 16)
            act.dma_start(rbias, a["router_bias"].partition_broadcast(128)).then_inc(vec_in.sem, 16)
            act.dma_start(w_ff[:, :, :], w_in_d[:, :, 3584:3588]).then_inc(vec_in.sem, 16)

            def evac_tile(s, i):
                P, key = TILES[i], ("T", s, i)
                ps = filled(act, key)
                copy(xT[:, :, 128 * i:128 * i + P], ps[:, :].rearrange("p (k t) -> p k t", k=KD)[:, :, 0:P]).then_inc(ps_free.sem(key), 1)

            for i in range(0, NT, 2):
                evac_tile(-1, i)
            act.wait_ge(*pe_full[("T", -1, 3)])
            act.dma_start(ss_, a["state_hgrn2"][0, 0].rearrange("h k v -> k h v")).then_inc(state_in.sem, 16)
            for i in range(NT):
                P = TILES[i]
                copy(hv[0:P, i, :], filled(act, ("v", i))[0:P, 0:512]).then_inc(ps_free.sem(("v", i)), 1)
            for i in range(NT):
                P = TILES[i]
                key = ("g", i)
                act.activation(hgate[0:P, i, :], filled(act, key)[0:P, 0:512], ACT.Exp, scale=-1.0).then_inc(ps_free.sem(key), 1)
                if i == 0:
                    act.wait_ge(*lb_done["max"])
                    act.activation(tl, tl, ACT.Exp).then_inc(lb_e.sem, 1)

            def q_copy(h):
                if h >= 2:
                    last = ("A", 5 * (h - 2) + 4)
                    act.wait_ge(*pe_full[last])
                copy(qk[:, h % 2, 1, 0:TOK], filled(act, ("q", h))[:, 0:TOK]).then_inc(ps_free.sem(("q", h)), 1)

            def f_steps(h):
                b = h % 2
                if h >= 1:
                    act.wait_ge(*b_sb[h - 1])
                act.activation(ft[:, 0, 0:TOK], filled(act, ("f", h))[:, 0:TOK], ACT.Exp, scale=-1.0).then_inc(ps_free.sem(("f", h)), 1)
                act.wait_ge(*f_sig[h])
                act.activation(ft[:, 2, 0:TOK], ft[:, 0, 0:TOK], ACT.Ln).then_inc(f_ln.sem, 1)
                act.wait_ge(*b_sb[h])
                act.mul(bn[:, b, 0, :], bn[:, b, 1, :], -1.0).then_inc(nb_sb.sem, 1)
                act.wait_ge(*nb_sb[h])
                if h >= 2:
                    act.wait_ge(*s_sb[5 * (h - 2) + 4])
                act.activation(qe[:, b, :], bn[:, b, 1, :], ACT.Exp)
                for i, (lo, hi) in enumerate([(128 * i, 128 * i + 128) for i in range(4)]
                                             + [(SEQ, META0), (META0, TOK)]):
                    last = bn[:, b, 1, hi - 1:hi]
                    act.activation(ebl[:, b, i:i + 1], last, ACT.Exp)
                    e = act.activation(kd[:, b, lo:hi], bn[:, b, 0, lo:hi], ACT.Exp, bias=last)
                e.then_inc(eb_sb.sem, 1)

            def decays(u):
                act.wait_ge(*d_sb[u])
                act.activation(gbuf[:, u % 2, :, :], gbuf[:, u % 2, :, :], ACT.Exp).then_inc(de_sb.sem, 1)

            def unit_b(u):
                h, i = units[u]
                P, b = TILES[i], u % 2
                act.wait_ge(*kdT_ps[u])
                if u >= 2:
                    act.wait_ge(*s_ps[u - 2])
                copy(kdT[0:P, b, :], kdT_bank[0:P, :]).then_inc(kdT_sb.sem, 1)
                act.wait_ge(*o_ps[u])
                if u >= 2:
                    act.wait_ge(*og_sb[u - 2])
                st = hstat[0:P, 2 * b:2 * b + 1]
                chain(act.activation(junk[0:P, 0:128], o_bank[0:P, :], ACT.Square, accum_out=st))
                chain(act.activation(st, st, ACT.Ln, scale=1.0 / DH, bias=eps_rms[0:P]))
                act.activation(hstat[0:P, 2 * b + 1:2 * b + 2], st, ACT.Exp, scale=-0.5).then_inc(o_rs.sem, 1)

            def unit_c(u):
                h, i = units[u]
                P = TILES[i]
                act.wait_ge(*ogT_ps[u])
                copy(mixT[:, h, 128 * i:128 * i + P], ogT_bank[:, 0:P]).then_inc(ogT_sb.sem, 1)

            def copy_scaled(dst, key, n, scale):
                act.mul(dst, filled(act, key)[:, 0:n], scale).then_inc(ps_free.sem(key), 1)

            def fk_copy(i):
                P, key = TILES[i], ("fk", i)
                if i == 0:
                    act.wait_ge(*st_hg["all"])
                    act.wait_ge(*og_sb[19])
                    act.wait_ge(*ogT_ps[19])
                if i >= 2:
                    act.wait_ge(*pe_full[("fkt", i - 2)])
                    act.wait_ge(fk_st[i % 2].sem, 16 * (i // 2))
                copy(fks[0:P, i % 2, :], filled(act, key)[0:P, 0:512]).then_inc(ps_free.sem(key), 1)

            for kind, n in HG_ORDER:
                if kind == "q":
                    q_copy(n)
                elif kind == "f":
                    f_steps(n)
                elif kind == "fq":
                    copy_scaled(fq[:, n, :], ("fq", n), TOK, SC_FOX)
                elif kind == "U":
                    if n == 0:
                        decays(0)
                    for m in range(5):
                        u = 5 * n + m
                        if u + 1 < 20:
                            decays(u + 1)
                        if m >= 1:
                            unit_b(u - 1)
                        if m >= 2:
                            unit_c(u - 2)
                elif kind == "flush":
                    u = 5 * n + 4
                    unit_b(u)
                    unit_c(u - 1)
                    unit_c(u)
            fk_copy(0)
            for i in range(1, NT + 1):
                if i < NT:
                    fk_copy(i)
                j, P = i - 1, TILES[i - 1]
                key = ("fkt", j)
                copy(fkT[:, :, 128 * j:128 * j + P],
                          filled(act, key)[:, 0:512].rearrange("p (h t) -> p h t", h=4)[:, :, 0:P]).then_inc(ps_free.sem(key), 1)
            for i in range(NT):
                P, key = TILES[i], ("fv", i)
                copy(fv[0:P, i, :], filled(act, key)[0:P, 0:512]).then_inc(ps_free.sem(key), 1)
            act.wait_ge(*lf_x["x"])
            chain(act.activation(l2[0:4, :], l2[0:4, :], ACT.Exp, scale=-1.0))
            act.activation(l2[0:4, :], l2[0:4, :], ACT.Ln, bias=one[0:4]).then_inc(lf_l.sem, 1)
            for j in range(4):
                key = ("kp", j)
                copy(kpT[:, :, 128 * j:128 * j + 128], filled(act, key)[:, 0:512].rearrange("p (h t) -> p h t", h=4)).then_inc(ps_free.sem(key), 1)

            def att_exp(n):
                kind, _, i = att_units[n]
                nb, P = att_rows(i)
                W, b = 80 + 128 * nb, n % 2
                act.wait_ge(*mx_sb[n])
                dst = probs[0:P, b, 0:W]
                if n >= 2:
                    act.wait_ge(*dg_sb[n - 2])
                if kind == "fox":
                    act.activation(dst, dst, ACT.Exp, bias=nmax[0:P, b:b + 1],
                                              accum_out=rsum[0:P, b:b + 1]).then_inc(ex_sb.sem, 1)
                else:
                    if n >= 2:
                        act.wait_ge(*pe_full[("PT", n - 2)])
                    src = psum[pair_of[("S", n)]][0:P, 432:432 + W]
                    filled(act, ("S", n))
                    act.activation(dst, src, ACT.Exp, bias=nmax[0:P, b:b + 1],
                                              accum_out=rsum[0:P, b:b + 1]).then_inc(ex_sb.sem, 1)

            def att_pt(n):
                nb, P = att_rows(att_units[n][2])
                ps = filled(act, ("PT", n))
                if n >= 2:
                    act.wait_ge(*oT_ps[n - 2])
                copy(pT[:, n % 2, 0:128 * nb].rearrange("p (j t) -> p j t", j=nb)[:, :, 0:P],
                               ps[:, 512:512 + 128 * nb].rearrange("p (j t) -> p j t", j=nb)[:, :, 0:P]).then_inc(pT_a.sem, 1)

            def attention(first, last):
                for n in range(first, last + 1):
                    if n < last:
                        att_exp(n)
                    if n - 1 >= first:
                        att_pt(n - 1)

            attention(0, 20)

            def ln_scale(s, i):
                P, b = TILES[i], i % 2
                act.wait_ge(*r_mv[(s, i)])
                chain(act.activation(lrs[0:P, b, 0:1], lmv[0:P, b, 1:2], ACT.Ln, bias=eps_ln[0:P]))
                act.activation(lrs[0:P, b, 1:2], lrs[0:P, b, 0:1], ACT.Exp, scale=-0.5).then_inc(r_rs.sem, 1)

            def out_and_experts(l):
                for i in range(NT):
                    ln_scale(2 * l, i)
                    if i >= 1 and (i - 1) % 2 == 0:
                        evac_tile(2 * l, i - 1)
                evac_tile(2 * l, NT - 1)
                act.wait_ge(*lg_sb[(l, NT - 1)])
                act.activation(sc_, lg, ACT.Exp, scale=-1.0).then_inc(r_e.sem, 1)

                def rows_copy(e):
                    act.wait_ge(*xgT_ps[(l, e)])
                    if e >= 2:
                        act.wait_ge(*gu_ps[(l, e - 2)])
                    copy(xgT[:, e % 2, 0:4, :], psum[0][:, 0:512].rearrange("p (k n) -> p k n", k=4)).then_inc(xgT_sa.sem, 1)

                rows_copy(0)
                for e in range(NE + 1):
                    if e < NE:
                        act.wait_ge(*gu_ps[(l, e)])
                        if e >= 2:
                            act.wait_ge(*h_sb[(l, e - 2)])
                        lo = 512 * (e % 2)
                        act.activation(eg[:, e % 2, :], psum[1][:, lo:lo + 256], ACT.Exp, scale=-1.0).then_inc(eg_sb.sem, 1)
                    if e + 1 < NE:
                        rows_copy(e + 1)
                    if e >= 1:
                        act.wait_ge(*dn_ps[(l, e - 1)])
                        if e >= 3:
                            act.wait_ge(*y_st[(e - 1) % 2][(l, e - 3)])
                        copy(yb[:, (e - 1) % 2, 0:512], psum[2][:, 0:512]).then_inc(y_sa.sem, 1)
                m = ov[l]
                act.wait_ge(*ix_sb[l])
                count = act.value_load(ovi[0:1, 0:1], min_val=0, max_val=NOV)
                with act.Fori(0, NOV) as b:
                    with act.If(count > b):
                        act.wait_ge(m["gu"], b + 1)
                        act.activation(eg[:, 0, :], psum[1][:, 0:256], ACT.Exp, scale=-1.0).then_inc(m["ex"], 1)
                for i in range(NT):
                    ln_scale(2 * l + 1, i)
                    if l == 0 and i >= 1 and (i - 1) % 2 == 0:
                        evac_tile(1, i - 1)
                if l == 0:
                    evac_tile(1, NT - 1)

            out_and_experts(0)
            for i in range(NT + 1):
                if i < NT:
                    P, b = TILES[i], i % 2
                    ps = filled(act, ("mi", i))
                    if i >= 2:
                        act.wait_ge(*mi_sb[i - 2])
                    act.activation(junk[0:P, 0:QL], ps[0:P, 0:QL], ACT.Square, accum_out=mst[0:P, b, 0:1])
                    chain(act.activation(junk[0:P, 512:512 + KVL], ps[0:P, QL:QL + KVL], ACT.Square, accum_out=mst[0:P, b, 1:2]))
                    act.activation(mst[0:P, b, 2:3], mst[0:P, b, 0:1], ACT.Ln, scale=1.0 / QL, bias=eps_rms[0:P])
                    chain(act.activation(mst[0:P, b, 3:4], mst[0:P, b, 1:2], ACT.Ln, scale=1.0 / KVL, bias=eps_rms[0:P]))
                    act.activation(mst[0:P, b, 0:2], mst[0:P, b, 2:4], ACT.Exp, scale=-0.5).then_inc(mi_a.sem, 1)
                if i >= 1:
                    j, P = i - 1, TILES[i - 1]
                    ps = filled(act, ("mt", j))
                    cs = slice(128 * j, 128 * j + P)
                    copy(cqT[:, :, cs], ps[:, 0:512].rearrange("p (k t) -> p k t", k=4)[:, :, 0:P])
                    copy(ckT[:, :, cs], ps[:, 512:768].rearrange("p (k t) -> p k t", k=2)[:, :, 0:P])
                    copy(peT[:, cs], ps[:, 768:768 + P]).then_inc(ps_free.sem(("mt", j)), 1)
            for j in range(4):
                ps = filled(act, ("pt", j))
                cs = slice(128 * j, 128 * j + 128)
                copy(ckpT[:, :, cs], ps[:, 0:256].rearrange("p (k t) -> p k t", k=2))
                copy(pepT[:, cs], ps[:, 256:384]).then_inc(ps_free.sem(("pt", j)), 1)
            for j in range(NT):
                P, key = TILES[j], ("qt", j)
                act.mul(qpT[:, :, 128 * j:128 * j + P],
                             filled(act, key)[:, 0:512].rearrange("p (k t) -> p k t", k=4)[:, :, 0:P], SC_MLA).then_inc(ps_free.sem(key), 1)
            for g in range(2):
                if g == 1:
                    for n in (38, 39):
                        act.wait_ge(*oT_ps[n])
                for h in range(4):
                    copy_scaled(qnT[:, h, :], ("qn", g, h), TOK, SC_MLA)
                    copy_scaled(knT[:, h, :], ("kn", g, h), TOK, 1.0)
                    copy_scaled(knpT[:, h, :], ("knp", g, h), PAST, 1.0)
                if g == 0:
                    for b in range(2):
                        act.wait_ge(mi_st[b].sem, mi_st[b].total)
                    act.wait_ge(*pe_full[("qt", 4)])
                for j in range(9):
                    P, key = (TILES[j] if j < 5 else 128), ("mv", g, j)
                    copy(mv_[0:P, j, :], filled(act, key)[0:P, 0:512]).then_inc(ps_free.sem(key), 1)
                attention(20 + 20 * g, 40 + 20 * g)
            out_and_experts(1)

        @block.vector
        def _(dve):
            chain = Chain(dve, c_dve)
            tt, ts, stt, copy = dve.tensor_tensor, dve.tensor_scalar, dve.scalar_tensor_tensor, dve.tensor_copy

            def bc(v, n):
                return v.unsqueeze(len(v.shape)).to_broadcast(list(v.shape) + [n])

            dve.memset(eps_rms, RMS_EPS)
            dve.memset(eps_ln, LN_EPS)
            dve.memset(one, 1.0)
            dve.memset(lg, 0.0)
            dve.memset(ft[:, 2, TOK:PAD], 0.0)
            chain(dve.memset(qk[:, :, :, TOK:PAD], 0.0))
            dve.wait_ge(*cst_in["all"])
            copy(cstb[:, :], consts_in)
            copy(identb[:, :], ident)
            copy(iotab[:, :], const("iota")).then_inc(cst_b.sem, 1)

            def evac_tile(s, i):
                P, key = TILES[i], ("T", s, i)
                ps = filled(dve, key)
                copy(xT[:, :, 128 * i:128 * i + P], ps[:, :].rearrange("p (k t) -> p k t", k=KD)[:, :, 0:P]).then_inc(ps_free.sem(key), 1)

            for i in range(1, NT, 2):
                evac_tile(-1, i)
            dve.wait_ge(vec_in.sem, vec_in.total)
            chain(dve.tensor_reduce(mx4, tl.rearrange("p j c -> p c j"), AX, ALU.max))
            tt(tl, tl, mx4.unsqueeze(1).to_broadcast([128, 3, 4]), ALU.subtract).then_inc(lb_done.sem, 1)
            dve.wait_ge(*lb_e["exp"])
            chain(dve.tensor_reduce(se4, tl.rearrange("p j c -> p c j"), AX, ALU.add))
            chain(dve.reciprocal(se4, se4))
            chain(tt(lb, tl[:, 0, :], se4, ALU.mult))
            chain(ts(omlb, lb, -1.0, 1.0, ALU.mult, ALU.add))
            for i in range(NT):
                P, key = TILES[i], ("g", i)
                dve.wait_ge(*ps_free[key])
                chain(ts(hgate[0:P, i, :], hgate[0:P, i, :], 1.0, None, ALU.add))
                chain(dve.reciprocal(hgate[0:P, i, :], hgate[0:P, i, :]))
                tt(hgate[0:P, i, :], hgate[0:P, i, :], hgn[0:P, :], ALU.mult).then_inc(g_sb.sem, 1)

            def f_steps(h):
                b = h % 2
                f0, f1, f2 = (ft[:, n, 0:TOK] for n in range(3))
                dve.wait_ge(*ps_free[("f", h)])
                chain(ts(f1, f0, 1e37, 1.0, ALU.min, ALU.add))
                chain(dve.reciprocal(f1, f1))
                chain(ts(f2, f0, 1e37, omlb[:, h:h + 1], ALU.min, ALU.mult))
                if h >= 2:
                    last = ("A", 5 * (h - 2) + 4)
                    dve.wait_ge(*pe_full[last])
                chain(tt(qk[:, b, 0, 0:TOK], f2, f1, ALU.mult))
                ts(f0, f1, omlb[:, h:h + 1], lb[:, h:h + 1], ALU.mult, ALU.add).then_inc(f_sig.sem, 1)
                dve.wait_ge(*f_ln[h])
                dve.tensor_tensor_scan(bn[:, b, 1, :], reset, ft[:, 2, :], 0.0, ALU.mult, ALU.add).then_inc(b_sb.sem, 1)
                dve.wait_ge(*eb_sb[h])
                dve.wait_ge(*q_sb[h])
                tt(qe[:, b, 0:TOK], qe[:, b, 0:TOK], qk[:, b, 1, 0:TOK], ALU.mult)
                tt(kd[:, b, 0:TOK], kd[:, b, 0:TOK], qk[:, b, 0, 0:TOK], ALU.mult).then_inc(qe_sb.sem, 1)

            def levels(u):
                h, i = units[u]
                dve.wait_ge(*de_sb[u])
                for n, L in enumerate(LEVELS):
                    both, _ = pairs(qk[:, h % 2, 0, 128 * i:128 * i + 128], L)
                    g = gbuf[:, u % 2, n, :].rearrange("p (q s r) -> p q s r", s=2, r=L)
                    last = tt(g, g, both, ALU.mult)
                last.then_inc(gm_sb.sem, 1)

            def unit_a(u):
                _, i = units[u]
                P, n0 = TILES[i], (1 if i == 4 else 0)
                key = ("A", u)
                ps = filled(dve, key)[0:P, 128 * n0:1024].rearrange("p (l t) -> p l t", t=128)[:, :, 0:P]
                m = am[0:P, 128 * n0:1024].rearrange("p (l t) -> p l t", t=128)[:, :, 0:P]
                if u >= 1:
                    dve.wait_ge(*a_sb[u - 1])
                tt(m, ps, lev[0:P, n0:8, 0:P], ALU.mult).then_inc(ps_free.sem(key), 1)
                dve.wait_ge(*ps_free[key])
                if u >= 2:
                    dve.wait_ge(*o_ps[u - 2])
                dve.tensor_reduce(asb[0:P, u % 2, 0:P], m.rearrange("p l t -> p t l"), AX, ALU.add).then_inc(a_sb.sem, 1)

            def unit_b(u):
                h, i = units[u]
                P, b = TILES[i], u % 2
                dve.wait_ge(*s_ps[u])
                if i == 4:
                    dve.wait_ge(*state_in["all"])
                    copy(sp_[:, h, :], s_bank[:, 0:128])
                    last = stt(ss_[:, h, :], ss_[:, h, :], ebl[:, h % 2, 4:5], s_bank[:, 128:256], ALU.mult, ALU.add)
                else:
                    last = stt(sp_[:, h, :], sp_[:, h, :], ebl[:, h % 2, i:i + 1], s_bank[:, 0:128], ALU.mult, ALU.add)
                last.then_inc(s_sb.sem, 1)
                dve.wait_ge(*o_rs[u])
                if u >= 2:
                    dve.wait_ge(*ogT_ps[u - 2])
                dve.wait_ge(*g_sb[i])
                stt(og[0:P, b, :], o_bank[0:P, :], hstat[0:P, 2 * b + 1:2 * b + 2],
                               hgate[0:P, i, 128 * h:128 * h + 128], ALU.mult, ALU.mult).then_inc(og_sb.sem, 1)

            for kind, n in HG_ORDER:
                if kind == "f":
                    f_steps(n)
                elif kind == "U":
                    if n == 0:
                        levels(0)
                    for m in range(5):
                        u = 5 * n + m
                        if u + 1 < 20:
                            levels(u + 1)
                        unit_a(u)
                        if m >= 1:
                            unit_b(u - 1)
                elif kind == "flush":
                    unit_b(5 * n + 4)

            dve.wait_ge(*st_hg["all"])
            dve.wait_ge(*ogT_ps[19])
            for h in range(4):
                copy(sel4[0:4, h, :], ident[0:4, h:h + 1].to_broadcast([4, 128]))
            ps = filled(dve, ("lf",))
            ts(l1[0:4, :], ps[0:4, 0:TOK], fb4[0:4, :], None, ALU.add).then_inc(ps_free.sem(("lf",)), 1)
            dve.wait_ge(*ps_free[("lf",)])
            stt(l2[0:4, :], l1[0:4, :], -1.0, l1[0:4, :], ALU.mult, ALU.max).then_inc(lf_x.sem, 1)
            dve.wait_ge(*lf_l["x"])
            dve.wait_ge(past_in.sem, 48)
            chain(stt(lf[0:4, PAST:PAST + TOK], l1[0:4, :], 0.0, l2[0:4, :], ALU.min, ALU.subtract))
            own, ones = PAST, const("ones")
            scan_of = lambda lo, hi, init: dve.tensor_tensor_scan(
                ff[0:4, lo:hi], ones[0:4, 0:1].to_broadcast([4, hi - lo]), lf[0:4, lo:hi], init, ALU.mult, ALU.subtract)
            scan_of(0, PAST, 0.0)
            chain(scan_of(own + META0, own + TOK, 0.0))
            scan_of(own, own + SEQ, ff[0:4, own + TOK - 1:own + TOK])
            scan_of(own + SEQ, own + META0, ff[0:4, PAST - 1:PAST]).then_inc(lf_sb.sem, 1)

            def att_max(n):
                kind, h, i = att_units[n]
                nb, P = att_rows(i)
                W, b = 80 + 128 * nb, n % 2
                if kind == "fox" and i == 0:
                    k0, k1 = ("nf", h, 0), ("nf", h, 1)
                    ps = filled(dve, k0)
                    copy(nfb[:, 0, 80:592], ps[:, 0:512])
                    copy(nfb[:, 0, 0:80], ps[:, 512:592])
                    copy(nfb[:, 1, 0:80], ps[:, 512:592]).then_inc(ps_free.sem(k0), 1)
                    ps = filled(dve, k1)
                    copy(nfb[:, 1, 80:592], ps[:, 0:512]).then_inc(ps_free.sem(k1), 1)
                    dve.wait_ge(*ps_free[k1])
                    dve.wait_ge(*ps_free[k0])
                key = ("S", n)
                src = filled(dve, key)[0:P, 432:432 + W]
                if n >= 2:
                    dve.wait_ge(*ex_sb[n - 2])
                if kind == "fox":
                    if n >= 2:
                        dve.wait_ge(*pe_full[("PT", n - 2)])
                    dve.tensor_tensor_reduce(probs[0:P, b, 0:W], src, nfb[0:P, int(i == 4), 0:W], 1.0, -3e38,
                                                  ALU.add, ALU.max, amax[0:P, b:b + 1]).then_inc(ps_free.sem(key), 1)
                    dve.wait_ge(*ps_free[key])
                    ts(nmax[0:P, b:b + 1], amax[0:P, b:b + 1], -1.0, None, ALU.mult).then_inc(mx_sb.sem, 1)
                else:
                    dve.tensor_reduce(nmax[0:P, b:b + 1], src, AX, ALU.max, negate=True).then_inc(mx_sb.sem, 1)

            def att_scale(n):
                P, b = TILES[att_units[n][2]], n % 2
                dve.wait_ge(*ex_sb[n])
                if n >= 2:
                    dve.wait_ge(*pe_full[("PT", n - 2)])
                if att_units[n][0] == "mla":
                    dve.reciprocal(rinv[0:P, b:b + 1], rsum[0:P, b:b + 1]).then_inc(ps_free.sem(("S", n)), 1)
                    dve.wait_ge(*ps_free[("S", n)])
                else:
                    chain(dve.reciprocal(rinv[0:P, b:b + 1], rsum[0:P, b:b + 1]))
                ts(diag[0:P, b, 0:P], ident[0:P, 0:P], rinv[0:P, b:b + 1], None, ALU.mult).then_inc(dg_sb.sem, 1)

            def att_own(n):
                P = TILES[att_units[n][2]]
                ps = filled(dve, ("PT", n))
                if n >= 2:
                    dve.wait_ge(*oT_ps[n - 2])
                copy(pT[0:80, n % 2, 512:512 + P], ps[0:80, 0:P]).then_inc(pT_b.sem, 1)

            def att_out(n):
                kind, h, i = att_units[n]
                P = TILES[i]
                dve.wait_ge(*oT_ps[n])
                dst = mixed((4 if kind == "fox" else 0) + h, i)
                copy(dst, psum[pair_of[("PT", n)]][:, 256:256 + P]).then_inc(ps_free.sem(("PT", n)), 1)

            def attention(first, last):
                for n in range(first, last + 2):
                    if n < last:
                        att_max(n)
                    if n - 2 >= first:
                        att_out(n - 2)
                    if first <= n - 1 < last:
                        att_own(n - 1)
                    if n < last:
                        att_scale(n)

            attention(0, 20)

            def layer_norm_tile(s, i):
                l, P, b = s // 2, TILES[i], i % 2
                r, x = rb[0:P, b, :], xr[0:P, b, :]
                dve.wait_ge(*xr_in[b][(s, i, 1 if (s == 0 and i == 4) else 0)])
                if (s, i) > (0, 1):
                    ps_, pi = (s, i - 2) if i >= 2 else (s - 1, 4 if b == 0 else 3)
                    dve.wait_ge(*x_st[b][(ps_, pi)])
                    if ps_ < 3:
                        dve.wait_ge(*pe_full[("T", ps_, pi)])
                if s % 2 == 0:
                    key = ("wo", l, i)
                    stt(r, x, ALPHA, filled(dve, key)[0:P, :], ALU.mult, ALU.add).then_inc(ps_free.sem(key), 1)
                    dve.wait_ge(*ps_free[key])
                else:
                    dve.wait_ge(*yg_in[b][(l, i, 1)])
                    y1, y2 = yg[0:P, 2 * b, :], yg[0:P, 2 * b + 1, :]
                    chain(ts(y1, y1, wts[0:P, 0, i:i + 1], None, ALU.mult))
                    chain(stt(y1, y2, wts[0:P, 1, i:i + 1], y1, ALU.mult, ALU.add))
                    chain(stt(r, x, ALPHA, y1, ALU.mult, ALU.add))
                st = lst[0:P, b, :]
                dve.bn_stats(st[:, 0:6], r[:, 0:512])
                chain(dve.bn_stats(st[:, 6:12], r[:, 512:1024]))
                dve.bn_aggr(lmv[0:P, b, :], st).then_inc(r_mv.sem, 1)
                dve.wait_ge(*lng_in[s])
                dve.wait_ge(*r_rs[(s, i)])
                chain(ts(r, r, lmv[0:P, b, 0:1], lrs[0:P, b, 1:2], ALU.subtract, ALU.mult))
                tt(r, r, lng[0:P, 0, :], ALU.mult).then_inc(r_n.sem, 1)

            def router(l):
                n20 = lambda v: v.rearrange("p i (g j) -> p (i g) j", j=4)
                R = [rtile(n) for n in range(12)]
                S = [r.rearrange("p i e -> p (i e)")[:, 0:20] for r in R]
                f80 = lambda v: v.rearrange("p i e -> p (i e)")
                over_i = lambda v: v.unsqueeze(1).to_broadcast([128, NT, v.shape[1]])
                dve.wait_ge(*r_e[l])
                chain(ts(sc_, sc_, 1.0, None, ALU.add))
                chain(dve.reciprocal(sc_, sc_))
                chain(tt(R[0], sc_, over_i(rbias), ALU.add))
                q = n20(R[0])
                tt(S[1], q[:, :, 0], q[:, :, 1], ALU.max)
                tt(S[2], q[:, :, 0], q[:, :, 1], ALU.min)
                tt(S[3], q[:, :, 2], q[:, :, 3], ALU.max)
                chain(tt(S[4], q[:, :, 2], q[:, :, 3], ALU.min))
                tt(S[5], S[1], S[3], ALU.max)
                tt(S[6], S[1], S[3], ALU.min)
                chain(tt(S[7], S[2], S[4], ALU.max))
                chain(tt(S[6], S[6], S[7], ALU.max))
                g = gs.rearrange("p i e -> p (i e)")
                chain(tt(g, S[5], S[6], ALU.add))
                chain(dve.tensor_reduce(t5a, gs, AX, ALU.max))
                chain(tt(gs2, gs, bc(t5a, 4), ALU.is_equal))
                chain(tt(gs2, gs2, over_i(const("prio4")), ALU.mult))
                chain(dve.tensor_reduce(t5b, gs2, AX, ALU.max))
                chain(tt(gs2, gs2, bc(t5b, 4), ALU.is_equal))
                chain(tt(n20(R[1]), q, bc(gs2.rearrange("p i e -> p (i e)"), 4), ALU.mult))
                chain(ts(gs2, gs2, -NEG, NEG, ALU.mult, ALU.add))
                chain(tt(n20(R[1]), n20(R[1]), bc(gs2.rearrange("p i e -> p (i e)"), 4), ALU.add))
                for c, sel in ((0, sel1), (1, mk)):
                    chain(dve.tensor_reduce(t5a, R[1], AX, ALU.max))
                    chain(tt(R[2], R[1], bc(t5a, NE), ALU.is_equal))
                    chain(tt(R[2], R[2], over_i(const("prio16")), ALU.mult))
                    chain(dve.tensor_reduce(t5b, R[2], AX, ALU.max))
                    chain(tt(sel, R[2], bc(t5b, NE), ALU.is_equal))
                    if c == 0:
                        chain(stt(f80(R[1]), f80(sel), 2 * NEG, f80(R[1]), ALU.mult, ALU.add))
                    chain(tt(sel, sel, bc(const("valid"), NE), ALU.mult))
                    chain(tt(R[3], sel, sc_, ALU.mult))
                    chain(dve.tensor_reduce(wts[:, c, :], R[3], AX, ALU.add))
                chain(copy(R[4], mk))
                chain(tt(mk, mk, sel1, ALU.add))
                copy(maskb[:, :], f80(mk)).then_inc(mk_sb.sem, 1)
                chain(tt(t5a, wts[:, 0, :], wts[:, 1, :], ALU.add))
                chain(ts(t5a, t5a, 1e-37, None, ALU.max))
                chain(dve.reciprocal(t5a, t5a))
                chain(tt(wts, wts, t5a.unsqueeze(1).to_broadcast([128, 2, NT]), ALU.mult))
                key = ("rk", l)
                ps = filled(dve, key)
                copy(f80(R[5]), ps[:, 0:80])
                copy(cnt, ps[:, 80:96]).then_inc(ps_free.sem(key), 1)
                dve.wait_ge(*ps_free[key])
                chain(ts(ovn, cnt, 128.0, None, ALU.is_gt))
                for m in (256.0, 384.0, 512.0):
                    chain(stt(ovn, cnt, m, ovn, ALU.is_gt, ALU.add))
                chain(dve.tensor_tensor_scan(ovend, const("ones")[:, 0:NE], ovn, 0.0, ALU.mult, ALU.add))
                copy(ovi[:, 0:1], ovend[:, NE - 1:NE])
                chain(tt(cnt, ovend, ovn, ALU.subtract))
                chain(ts(cnt, cnt, 128.0, float(NE * 128 - 128), ALU.mult, ALU.add))
                chain(tt(ovn, const("base"), cnt, ALU.subtract))
                chain(ts(R[6], R[5], 128.0, None, ALU.is_lt))
                chain(tt(R[7], R[6], over_i(ovn), ALU.mult))
                chain(tt(R[7], R[7], over_i(cnt), ALU.add))
                chain(tt(R[7], R[7], R[5], ALU.add))
                for c, sel in ((0, sel1), (1, R[4])):
                    chain(tt(R[8], R[7], sel, ALU.mult))
                    chain(dve.tensor_reduce(posf[:, c, :], R[8], AX, ALU.add))
                chain(copy(posi, posf))
                chain(stt(f80(rk1), f80(R[5]), 1.0, f80(mk), ALU.add, ALU.mult))
                chain(ts(rk1, rk1, -1.0, None, ALU.add))
                for e in range(NE):
                    if e >= 2:
                        dve.wait_ge(*oh_us[(l, e - 2)])
                    for i in range(NT):
                        last = ts(oneh[:, e % 2, i, :], iotab[:, :], rk1[:, i, e:e + 1], None, ALU.is_equal)
                    last.then_inc(oh_sb.sem, 1)
                key = ("ix", l)
                ps = filled(dve, key)[:, 0:2 * NE].rearrange("p (e c) -> p e c", c=2)
                chain(copy(R[9].rearrange("p i e -> p (i e)")[:, 0:NE], ps[:, :, 1]))
                stt(R[9].rearrange("p i e -> p (i e)")[:, 0:NE], ps[:, :, 0], 128.0,
                         R[9].rearrange("p i e -> p (i e)")[:, 0:NE], ALU.mult, ALU.add).then_inc(ps_free.sem(key), 1)
                dve.wait_ge(*ps_free[key])
                copy(sloti, R[9].rearrange("p i e -> p (i e)")[:, 0:NE]).then_inc(ix_sb.sem, 1)

            def experts(l):
                def rows_copy(e):
                    dve.wait_ge(*xgT_ps[(l, e)])
                    if e >= 2:
                        dve.wait_ge(*gu_ps[(l, e - 2)])
                    copy(xgT[:, e % 2, 4:8, :], psum[0][:, 512:1024].rearrange("p (k n) -> p k n", k=4)).then_inc(xgT_sd.sem, 1)

                def hidden(e):
                    b, lo = e % 2, 512 * (e % 2)
                    g_, u_ = psum[1][:, lo:lo + 256], psum[1][:, lo + 256:lo + 512]
                    dve.wait_ge(*eg_sb[(l, e)])
                    if e >= 2:
                        dve.wait_ge(*hT_ps[(l, e - 2)])
                    chain(ts(eg[:, b, :], eg[:, b, :], 1.0, None, ALU.add))
                    chain(dve.reciprocal(eg[:, b, :], eg[:, b, :]))
                    chain(tt(eg[:, b, :], g_, eg[:, b, :], ALU.mult))
                    tt(hb[:, b, :], u_, eg[:, b, :], ALU.mult).then_inc(h_sb.sem, 1)

                rows_copy(0)
                for e in range(NE + 1):
                    if e >= 1:
                        dve.wait_ge(*hT_ps[(l, e - 1)])
                        if e >= 3:
                            dve.wait_ge(*dn_ps[(l, e - 3)])
                        copy(hT[:, (e - 1) % 2, :], psum[3][:, 0:256]).then_inc(hT_sb.sem, 1)
                    if e + 1 < NE:
                        rows_copy(e + 1)
                    if e < NE:
                        hidden(e)
                    if e >= 1:
                        dve.wait_ge(*dn_ps[(l, e - 1)])
                        if e >= 3:
                            dve.wait_ge(*y_st[(e - 1) % 2][(l, e - 3)])
                        copy(yb[:, (e - 1) % 2, 512:1024], psum[2][:, 512:1024]).then_inc(y_sd.sem, 1)
                m = ov[l]
                dve.memset(cur[:, 0:1], float(NE * 128))
                chain(dve.memset(cur[:, 1:2], 0.0))
                dve.wait_ge(*y_st[1][(l, NE - 1)])
                dve.wait_ge(*y_st[0][(l, NE - 2)])
                count = dve.value_load(ovi[0:1, 0:1], min_val=0, max_val=NOV)
                with dve.Fori(0, NOV) as b:
                    with dve.If(count > b):
                        steps = [0]

                        def step(ins):
                            steps[0] += 1
                            ins.then_inc(m["cnt"], 1)
                            dve.wait_ge(m["cnt"], b * STEPS + steps[0])

                        STEPS = 10
                        for c in range(2):
                            for i in range(NT):
                                last = ts(oneh[:, c, i, :], iotab[:, :], cur[:, 0:1], posf[:, c, i:i + 1],
                                          ALU.add, ALU.is_equal)
                        last.then_inc(m["oh"], 1)
                        step(ts(ovn, ovend, cur[:, 1:2], None, ALU.is_le))
                        step(dve.tensor_reduce(cur[:, 2:3], ovn, AX, ALU.add))
                        step(ts(ovi[:, 1:2], cur[:, 2:3], float(NE - 1), None, ALU.min))
                        dve.wait_ge(m["ix"], b + 1)
                        step(copy(cur[:, 3:4], psum[3][:, 513:514]))
                        step(stt(cur[:, 3:4], psum[3][:, 512:513], 128.0, cur[:, 3:4], ALU.mult, ALU.add))
                        copy(ovi[:, 2:3], cur[:, 3:4]).then_inc(m["id"], 1)
                        dve.wait_ge(m["tx"], b + 1)
                        copy(xgT[:, 0, :, :], psum[0][:, :].rearrange("p (k n) -> p k n", k=KD)).then_inc(m["xt"], 1)
                        dve.wait_ge(m["ex"], b + 1)
                        step(ts(eg[:, 0, :], eg[:, 0, :], 1.0, None, ALU.add))
                        step(dve.reciprocal(eg[:, 0, :], eg[:, 0, :]))
                        step(tt(eg[:, 0, :], psum[1][:, 0:256], eg[:, 0, :], ALU.mult))
                        tt(hb[:, 0, :], psum[1][:, 256:512], eg[:, 0, :], ALU.mult).then_inc(m["h"], 1)
                        step(ts(cur[:, 0:1], cur[:, 0:1], 128.0, None, ALU.add))
                        step(ts(cur[:, 1:2], cur[:, 1:2], 1.0, None, ALU.add))
                        dve.wait_ge(m["ht"], b + 1)
                        copy(hT[:, 0, :], psum[3][:, 0:256]).then_inc(m["hs"], 1)
                        dve.wait_ge(m["dn"], b + 1)
                        copy(yb[:, 0, :], psum[2][:, :]).then_inc(m["y"], 1)
                        assert steps[0] == STEPS

            def out_and_experts(l):
                for i in range(NT):
                    layer_norm_tile(2 * l, i)
                    if i >= 1:
                        j = i - 1
                        if j % 2 == 1:
                            evac_tile(2 * l, j)
                        logits_copy(l, j)
                logits_copy(l, NT - 1)
                router(l)
                experts(l)
                for i in range(NT):
                    layer_norm_tile(2 * l + 1, i)
                    if l == 0 and i >= 1 and (i - 1) % 2 == 1:
                        evac_tile(1, i - 1)

            def logits_copy(l, i):
                key = ("lg", l, i)
                P = TILES[i]
                copy(lg[0:P, i, :], filled(dve, key)[0:P, 0:NE]).then_inc(ps_free.sem(key), 1)
                dve.wait_ge(*ps_free[key])

            out_and_experts(0)
            rt = lambda P, n: rtmp[0:P, n, :]
            for i in range(NT):
                P, b, key = TILES[i], i % 2, ("mi", i)
                ps = filled(dve, key)
                if i == 0:
                    dve.wait_ge(mg_in.sem, 32)
                dve.wait_ge(*mi_a[i])
                if i >= 1:
                    dve.wait_ge(*mi_sb[i - 1])
                if i >= 2:
                    dve.wait_ge(*pe_full[("mt", i - 2)])
                    dve.wait_ge(mi_st[b].sem, 32 * (i // 2))
                stt(cqb[0:P, b, :], ps[0:P, 0:QL], mst[0:P, b, 0:1], qng[0:P, 0:QL], ALU.mult, ALU.mult)
                stt(cvb[0:P, b, :], ps[0:P, QL:QL + KVL], mst[0:P, b, 1:2], qng[0:P, QL:QL + KVL], ALU.mult, ALU.mult)
                x1, x2 = ps[0:P, 768:800], ps[0:P, 800:832]
                tt(rt(P, 0)[:, 0:32], x1, cos[0:P, i, :], ALU.mult)
                tt(rt(P, 1)[:, 0:32], x2, sin[0:P, i, :], ALU.mult)
                tt(rt(P, 2)[:, 0:32], x1, sin[0:P, i, :], ALU.mult)
                tt(rt(P, 3)[:, 0:32], x2, cos[0:P, i, :], ALU.mult).then_inc(ps_free.sem(key), 1)
                dve.wait_ge(*ps_free[key])
                for lo in (0, 64):
                    tt(kpb[0:P, b, lo:lo + 32], rt(P, 0)[:, 0:32], rt(P, 1)[:, 0:32], ALU.subtract)
                    last = tt(kpb[0:P, b, lo + 32:lo + 64], rt(P, 2)[:, 0:32], rt(P, 3)[:, 0:32], ALU.add)
                last.then_inc(mi_sb.sem, 1)
            dve.wait_ge(*mi_sb[NT - 1])
            for i in range(NT):
                P, b, key = TILES[i], i % 2, ("qp", i)
                ps = filled(dve, key)[0:P, 0:512].rearrange("p (h s d) -> p h s d", h=MH, s=2)
                v = lambda n: rt(P, n).rearrange("p (h d) -> p h d", h=MH)
                cs, sn = (t[0:P, i, :].unsqueeze(1).to_broadcast([P, MH, 32]) for t in (cos, sin))
                if i >= 1:
                    dve.wait_ge(*qp_sb[i - 1])
                if i >= 2:
                    dve.wait_ge(*pe_full[("qt", i - 2)])
                tt(v(0), ps[:, :, 0, :], cs, ALU.mult)
                tt(v(1), ps[:, :, 1, :], sn, ALU.mult)
                tt(v(2), ps[:, :, 0, :], sn, ALU.mult)
                tt(v(3), ps[:, :, 1, :], cs, ALU.mult).then_inc(ps_free.sem(key), 1)
                dve.wait_ge(*ps_free[key])
                out = qpb[0:P, b, :].rearrange("p (h s d) -> p h s d", h=MH, s=2)
                tt(out[:, :, 0, :], v(0), v(1), ALU.subtract)
                tt(out[:, :, 1, :], v(2), v(3), ALU.add).then_inc(qp_sb.sem, 1)
            attention(20, 40)
            attention(40, 60)
            out_and_experts(1)


_INS = ['x_prompt', 'x_sample', 'state_hgrn2', 'cache_fox_k', 'cache_fox_v', 'cache_fox_logf', 'cache_mla_ckv',
        'cache_mla_kpe', 'meta_tokens', 'even_w_in', 'hg_lb_logits', 'hg_norm_g', 'fox_forget_bias', 'even_w_out',
        'mla_w_in', 'mla_q_norm_g', 'mla_kv_norm_g', 'mla_w_uq', 'mla_w_uk', 'mla_w_uv', 'mla_w_out', 'ln_mix_g',
        'ln_mix_b', 'ln_ffn_g', 'ln_ffn_b', 'router_w', 'router_bias', 'moe_w_gate', 'moe_w_up', 'moe_w_down']
_L = NM + SEQ
_OUTS = [(1, SEQ, D), (1, NS, D), (1, 1, HH, DH, DH), (1, 1, _L, FH, DH), (1, 1, _L, FH, DH), (1, 1, _L, FH),
         (1, 1, _L, KVL), (1, 1, _L, ROPE), (1, 1, HH, DH, DH), (1, 1, NS, FH, DH), (1, 1, NS, FH, DH),
         (1, 1, NS, FH), (1, 1, NS, KVL), (1, 1, NS, ROPE)]


def kernel(**inputs):
    import concourse.bacc as _bacc
    from concourse.bass_utils import run_bass_kernel_spmd as _run

    nc = _bacc.Bacc("TRN2", target_bir_lowering=False, num_devices=1)
    blob, where = shape_constants()
    arrays, args = {"shape_constants": blob}, {}
    consts = nc.dram_tensor("shape_constants", blob.shape, F32, kind="ExternalInput").ap()
    for name in _INS:
        x = np.ascontiguousarray(inputs[name])
        arrays[f"in_{name}"] = x
        args[name] = nc.dram_tensor(f"in_{name}", x.shape, mybir.dt.from_np(x.dtype), kind="ExternalInput").ap()
    outs = [nc.dram_tensor(f"out_{i}", s, F32, kind="ExternalOutput").ap() for i, s in enumerate(_OUTS)]
    build_step(nc, where, consts, args, outs)
    r = _run(nc, [arrays], core_ids=[0])
    return tuple(r.results[0][f"out_{i}"] for i in range(len(_OUTS)))
```

```python
from contextlib import ExitStack

import numpy as np

import concourse.bass as bass
from concourse import mybir

F32 = mybir.dt.float32
BF16 = mybir.dt.bfloat16
I32 = mybir.dt.int32
ALU = mybir.AluOpType
ACT = mybir.ActivationFunctionType
AX = mybir.AxisListType.X

D = 1024
KD = D // 128
SEQ, NS, NM, PAST = 512, 64, 16, 512
TILES = [128, 128, 128, 128, NS + NM]
NT = len(TILES)
TOK = sum(TILES)
PAD = 128 * NT
META0 = SEQ + NS
HH, FH, MH = 4, 4, 8
DH = 128
QL, KVL, NOPE, ROPE = 512, 256, 128, 64
NE, DE = 16, 256
ALPHA = 4.0 ** 0.25
LN_EPS, RMS_EPS = 1e-5, 1e-6
LEVELS = [64, 32, 16, 8, 4, 2, 1]
NL = len(LEVELS)
NEG = -1e30
SLOT = 2048
NOV = 9
NSLOTS = (NE + NOV) * 128
UNIT_TILES = [4, 0, 1, 2, 3]
SC_FOX = DH ** -0.5
SC_MLA = (NOPE + ROPE) ** -0.5


def shape_constants():
    s = np.arange(128)[:, None]
    t = np.arange(128)[None, :]
    parts = {}
    parts["ident"] = (s == t).astype(np.float32)
    parts["iota"] = np.broadcast_to(t.astype(np.float32), (128, 128))
    reset = np.ones((128, PAD), np.float32)
    reset[:, 0:SEQ:128] = 0
    reset[:, SEQ] = 0
    reset[:, META0] = 0
    parts["reset"] = reset
    pos = np.zeros((NT, 128), np.float32)
    for i in range(4):
        pos[i] = NM + 128 * i + np.arange(128)
    pos[4, :NS] = PAST + np.arange(NS)
    pos[4, NS:NS + NM] = np.arange(NM)
    inv = np.float32(10000.0) ** (-np.arange(32, dtype=np.float32) / np.float32(32))
    ang = pos[:, :, None] * inv.astype(np.float32)[None, None, :]
    parts["cos"] = np.cos(ang).astype(np.float32).transpose(1, 0, 2).reshape(128, NT * 32)
    parts["sin"] = np.sin(ang).astype(np.float32).transpose(1, 0, 2).reshape(128, NT * 32)
    valid = np.ones((128, NT), np.float32)
    valid[NS + NM:, 4] = 0
    parts["valid"] = valid
    parts["prio4"] = np.broadcast_to(4.0 - np.arange(4), (128, 4))
    parts["prio16"] = np.broadcast_to(16.0 - np.arange(16), (128, 16))
    parts["base"] = np.broadcast_to(128.0 * np.arange(16), (128, 16))
    s3 = s[:, :, None]
    lev = []
    for L in LEVELS:
        lev.append((s // (2 * L) == t // (2 * L)) & (s % (2 * L) < L) & (t % (2 * L) >= L))
    lev.append(s == t)
    parts["lev"] = np.stack(lev, 1).reshape(128, 8 * 128).astype(np.float32)
    unmasked = np.zeros((128, NM + 384))
    parts["m_causal"] = np.concatenate([unmasked, np.where(t <= s, 0, NEG)], 1)
    parts["m_group"] = np.concatenate([unmasked, np.where((s < 64) & (t >= 64), NEG, 0)], 1)
    c80 = np.arange(80)[None, :]
    parts["m_past"] = np.broadcast_to(np.where(s < NS, 0, NEG), (128, PAST))
    same = (s < NS) == (c80 < NS)
    parts["m_own_fox"] = np.where(same & (c80 <= s), 0, NEG)
    parts["m_own_mla"] = np.where(same, 0, NEG)
    parts["before"] = (s < t).astype(np.float32)
    parts["ones"] = np.ones((128, 128), np.float32)
    parts["tok"] = np.stack([np.broadcast_to(np.arange(NT), (128, NT)),
                             np.broadcast_to(s, (128, NT))], 2).reshape(128, 2 * NT)
    where, n = {}, 0
    for name, a in parts.items():
        where[name] = (n, n + a.shape[1])
        n += a.shape[1]
    blob = np.concatenate([np.ascontiguousarray(a, np.float32) for a in parts.values()], 1)
    return blob, where


class Signal:

    def __init__(self, sem, keys, step=1):
        self.sem = sem
        self.at = {k: (n + 1) * step for n, k in enumerate(keys)}
        self.total = len(self.at) * step

    def __getitem__(self, key):
        return self.sem, self.at[key]


class Chain:

    def __init__(self, eng, sem):
        self.eng, self.sem, self.n = eng, sem, 0

    def __call__(self, ins):
        ins.then_inc(self.sem, 1)
        self.n += 1
        self.eng.wait_ge(self.sem, self.n)

    def mark(self, ins):
        ins.then_inc(self.sem, 1)
        self.n += 1
        return self.n

    def wait(self, n):
        self.eng.wait_ge(self.sem, n)


def build_step(nc, const_where, consts, a, o):
    (y_prompt, y_sample, hg_prompt, fk_prompt, fv_prompt, flf_prompt, ckv_prompt, kpe_prompt,
     hg_sample, fk_sample, fv_sample, flf_sample, ckv_sample, kpe_sample) = o

    x_rows = [nc.dram_tensor(f"x_rows{s}", [TOK, D], F32).ap() for s in range(3)]
    y_all = nc.dram_tensor("y_rows", [NSLOTS, D], F32).ap()
    y_rows = [y_all, y_all]

    ctx = ExitStack()
    with ctx:
        def sb(name, shape, dt=F32):
            return ctx.enter_context(nc.sbuf_tensor(name, shape, dt))

        def sem(name):
            return ctx.enter_context(nc.semaphore(name))

        def signal(name, keys, step=1):
            return Signal(sem(name), keys, step)

        n_f32 = const_where["lev"][0]
        n_all = consts.shape[1]
        cst = sb("cst", [128, n_f32])
        cstb = sb("cstb", [128, n_all - n_f32], BF16)
        identb = sb("identb", [128, 128], BF16)
        iotab = sb("iotab", [128, 128], BF16)

        def const(name):
            lo, hi = const_where[name]
            return cst[:, lo:hi] if lo < n_f32 else cstb[:, lo - n_f32:hi - n_f32]

        ident, reset = const("ident"), const("reset")
        cos = const("cos").rearrange("p (i d) -> p i d", i=NT)
        sin = const("sin").rearrange("p (i d) -> p i d", i=NT)
        lev = const("lev").rearrange("p (l t) -> p l t", l=8)
        tok2 = const("tok").rearrange("p (i c) -> p i c", c=2)

        xT = sb("xT", [128, KD, TOK])
        mixT = sb("mixT", [128, 4, TOK])
        ring = sb("ring", [128, 6 * SLOT])
        xr = sb("xr", [128, 2, D])
        rb = sb("rb", [128, 2, D])
        lng = sb("lng", [128, 2, D])
        rw = sb("rw", [128, KD, NE])
        small = sb("small", [128, 768])
        ints = sb("ints", [128, 64], I32)
        ARENA = 22528
        arena = sb("arena", [128, ARENA])

        cursor = [0]

        def col(n):
            c = cursor[0]
            cursor[0] += n
            assert cursor[0] <= 768
            return small[:, c:c + n]

        psum = [ctx.enter_context(nc.psum_tensor(f"pair{p}", [128, 1024], F32)) for p in range(4)]

        class Region:
            def __init__(self, start=0):
                self.n = start

            def take(self, words):
                v = arena[:, self.n:self.n + words]
                self.n += words
                assert self.n <= ARENA, self.n
                return v

        r0 = Region()
        fq = r0.take(4 * TOK).rearrange("p (h t) -> p h t", h=4)
        KCOL = NM + TOK
        fkT = r0.take(4 * KCOL).rearrange("p (h t) -> p h t", h=4)
        hg_start = r0.n
        hv = r0.take(NT * 512).rearrange("p (i n) -> p i n", i=NT)
        hgate = r0.take(NT * 512).rearrange("p (i n) -> p i n", i=NT)
        qk = r0.take(2 * 2 * PAD).rearrange("p (b s t) -> p b s t", b=2, s=2)
        bn = r0.take(2 * 2 * PAD).rearrange("p (b s t) -> p b s t", b=2, s=2)
        x_in = arena[:, r0.n:r0.n + NT * D].rearrange("p (i n) -> p i n", i=NT)
        qe = r0.take(2 * PAD).rearrange("p (b t) -> p b t", b=2)
        kd = r0.take(2 * PAD).rearrange("p (b t) -> p b t", b=2)
        gbuf = r0.take(2 * NL * 128).rearrange("p (b l t) -> p b l t", b=2, l=NL)
        am = lng[:, 0, :]
        junk = lng[:, 1, :]
        asb = r0.take(2 * 128).rearrange("p (b t) -> p b t", b=2)
        kdT = r0.take(2 * 128).rearrange("p (b t) -> p b t", b=2)
        og = r0.take(2 * 128).rearrange("p (b t) -> p b t", b=2)
        sp_ = r0.take(4 * 128).rearrange("p (h t) -> p h t", h=4)
        ss_ = r0.take(4 * 128).rearrange("p (h t) -> p h t", h=4)
        ft = rb[:, :, :].rearrange("p b n -> p (b n)")[:, 0:3 * PAD].rearrange("p (b t) -> p b t", b=3)
        hgn = xr[:, 0, 0:512]
        consts_in = arena[:, 0:n_all - n_f32]
        r1 = Region(hg_start)
        fv = r1.take(NT * 512).rearrange("p (i n) -> p i n", i=NT)
        kpT = r1.take(4 * PAST).rearrange("p (h t) -> p h t", h=4)
        vp = r1.take(4 * 512).rearrange("p (j n) -> p j n", j=4)
        fks = r1.take(2 * 512).rearrange("p (b n) -> p b n", b=2)
        kps = r1.take(4 * 512).rearrange("p (b n) -> p b n", b=4)
        nfb = r1.take(2 * 592).rearrange("p (s t) -> p s t", s=2)
        lf = r1.take(PAST + TOK)
        ff = r1.take(PAST + TOK)
        l1, l2 = xr[:, 1, 0:TOK], r1.take(TOK)
        sel4 = r1.take(4 * 128).rearrange("p (h t) -> p h t", h=4)
        ATT = 2 * 592 + 2 * 128 + 2 * 640
        r1.n = max(r1.n, ARENA - ATT)
        probs = [r1.take(592), r1.take(592), rb[:, 0, 0:592]]
        diag = [r1.take(128), r1.take(128), rb[:, 1, 0:128]]
        pT = r1.take(2 * 640).rearrange("p (b t) -> p b t", b=2)
        r2 = Region()
        cqT = r2.take(4 * TOK).rearrange("p (k t) -> p k t", k=4)
        ckT = r2.take(2 * TOK).rearrange("p (k t) -> p k t", k=2)
        ckpT = r2.take(2 * PAST).rearrange("p (k t) -> p k t", k=2)
        peT, pepT = r2.take(KCOL), r2.take(PAST)
        qpT = r2.take(4 * TOK).rearrange("p (k t) -> p k t", k=4)
        qnT = r2.take(4 * TOK).rearrange("p (k t) -> p k t", k=4)
        knT = r2.take(4 * KCOL).rearrange("p (k t) -> p k t", k=4)
        knpT = r2.take(4 * PAST).rearrange("p (k t) -> p k t", k=4)
        r3 = Region(r2.n)
        mv_ = r2.take(9 * 512).rearrange("p (j n) -> p j n", j=9)
        assert r2.n <= ARENA - ATT
        cqb = r3.take(2 * 512).rearrange("p (b n) -> p b n", b=2)
        cvb = r3.take(2 * 256).rearrange("p (b n) -> p b n", b=2)
        kpb = r3.take(2 * 128).rearrange("p (b n) -> p b n", b=2)
        qpb = r3.take(2 * 512).rearrange("p (b n) -> p b n", b=2)
        assert r3.n <= r2.n
        r3 = Region(r2.n - 4608 - 4 * PAST)
        pst = r3.take(4 * 384).rearrange("p (b n) -> p b n", b=4)
        rtmp = arena[:, ARENA - ATT:ARENA - ATT + 1024].rearrange("p (b n) -> p b n", b=4)
        qng = arena[:, ARENA - ATT + 1024:ARENA - ATT + 1024 + 768]
        r4 = Region()
        wexp = r4.take(6 * SLOT)
        xg = r4.take(2 * D).rearrange("p (b n) -> p b n", b=2)
        xgT = r4.take(2 * D).rearrange("p (b k n) -> p b k n", b=2, k=KD)
        yb = r4.take(2 * D).rearrange("p (b n) -> p b n", b=2)
        eg = r4.take(2 * 256).rearrange("p (b n) -> p b n", b=2)
        hb = r4.take(2 * 256).rearrange("p (b n) -> p b n", b=2)
        hT = r4.take(2 * 256).rearrange("p (b n) -> p b n", b=2)
        oneh = r4.take(2 * 5 * 64).bitcast(BF16).rearrange("p (b i t) -> p b i t", b=2, i=NT)
        r5 = Region()
        yg = r5.take(2 * NT * D).rearrange("p (i c n) -> p i c n", i=NT, c=2)
        wdiag = r5.take(2 * NT * 128).rearrange("p (i c t) -> p i c t", i=NT, c=2)
        adiag = r5.take(128)
        x_far = [mixT[:, :, :].rearrange("p k t -> p (k t)")[:, n * D:n * D + D] for n in range(2)]
        x_far.append(r4.take(D))

        def residual(s, i):
            return x_far[i - 2] if s % 2 == 1 and i >= 2 else xr[:, i % 2, :]


        lb, omlb, tl = col(4), col(4), col(12).rearrange("p (j c) -> p j c", j=3)
        mx4, se4 = col(4), col(4)
        one, neg_half = col(1), col(2)
        ebl = col(12).rearrange("p (b c) -> p b c", b=2)
        hstat = col(4)
        fb4 = col(1)
        amax, nmax, rsum, rinv = col(3), col(3), col(3), col(3)
        lst = col(24).rearrange("p (b c) -> p b c", b=2)
        lmv = col(4).rearrange("p (b c) -> p b c", b=2)
        lrs = col(4).rearrange("p (b c) -> p b c", b=2)
        mst = col(8).rearrange("p (b c) -> p b c", b=2)
        rbias = col(16)
        lg = col(NT * NE).rearrange("p (i e) -> p i e", i=NT)
        sc_ = col(NT * NE).rearrange("p (i e) -> p i e", i=NT)
        mk = col(NT * NE).rearrange("p (i e) -> p i e", i=NT)
        sel1 = col(NT * NE).rearrange("p (i e) -> p i e", i=NT)
        gs = col(NT * 4).rearrange("p (i e) -> p i e", i=NT)
        gs2 = col(NT * 4).rearrange("p (i e) -> p i e", i=NT)
        t5a, t5b = col(NT), col(NT)
        wts = col(2 * NT).rearrange("p (c i) -> p c i", c=2)
        posf = col(2 * NT).rearrange("p (c i) -> p c i", c=2)
        rk1 = col(NT * NE).rearrange("p (i e) -> p i e", i=NT)
        cnt, ovn, ovend = col(16), col(16), col(16)
        cur = col(4)
        assert r4.n <= ARENA - 800
        RW = arena[:, ARENA - 800:ARENA]

        def rtile(n):
            return RW[:, n * 80:(n + 1) * 80].rearrange("p (i e) -> p i e", i=NT)

        maskb = sb("maskb", [128, NT * NE], BF16)
        posi = ints[:, 0:10].rearrange("p (c i) -> p c i", c=2)
        sloti = ints[:, 16:32]
        ovi = ints[:, 32:36]

        order = {0: [], 1: [], 2: [], 3: []}
        pair_of = {}
        alt = [0]

        def ticket(key, pair=None):
            if pair is None:
                pair = alt[0] % 2
                alt[0] += 1
            order[pair].append(key)
            pair_of[key] = pair

        lo_k, hi_k, all_k = range(0, KD // 2), range(KD // 2, KD), range(KD)
        BETWEEN = {15: ("fq", 2, hi_k), 16: ("fq", 3, lo_k), 17: ("fq", 3, hi_k), 18: ("lf", 0, all_k)}
        for h in range(HH - 1):
            BETWEEN[5 * h] = ("f", h + 1, lo_k)
            BETWEEN[5 * h + 1] = ("f", h + 1, hi_k)
            BETWEEN[5 * h + 2] = ("q", h + 1, lo_k)
            BETWEEN[5 * h + 3] = ("q", h + 1, hi_k)
            BETWEEN[5 * h + 4] = ("fq", h, all_k if h < 2 else lo_k)
        units = [(h, i) for h in range(HH) for i in UNIT_TILES]
        fox_units = [("fox", h, i) for h in range(FH) for i in range(NT)]
        mla_units = [("mla", h, i) for h in range(MH) for i in range(NT)]
        att_units = fox_units + mla_units
        for i in range(NT):
            ticket(("T", -1, i))
        ticket(("f", 0))
        for i in range(NT):
            ticket(("v", i))
        ticket(("q", 0))
        for i in range(NT):
            ticket(("g", i))
        for u in range(len(units)):
            if u in BETWEEN and KD - 1 in BETWEEN[u][2]:
                ticket(BETWEEN[u][:2], 0)
            ticket(("A", u), 2)
        ticket(("fk", 0), 0)
        alt[0] = 1
        for i in range(1, NT + 1):
            if i < NT:
                ticket(("fk", i))
            ticket(("fkt", i - 1))
        for i in range(NT):
            ticket(("fv", i))
        for j in range(4):
            ticket(("kp", j))
        for n, (_, h, i) in enumerate(fox_units):
            if i == 0:
                ticket(("nf", h, 0))
                ticket(("nf", h, 1))
            ticket(("S", n))
            ticket(("PT", n), 2 + n % 2)

        IX_GROUPS = [range(e, e + 2) for e in range(0, NE, 2)]
        LAST_IX = len(IX_GROUPS) - 1

        def plan_out(l):
            for i in range(NT):
                ticket(("wo", l, i))
                ticket(("T", 2 * l, i), 2)
                ticket(("lg", l, i), 3)
            ticket(("rk", l), 0)
            for g in range(len(IX_GROUPS)):
                ticket(("ix", l, g), 3)
            for i in range(NT):
                ticket(("cb", l, i))

        plan_out(0)
        for i in range(NT):
            ticket(("T", 1, i), 2)
        alt[0] = 0
        for i in range(NT):
            ticket(("mi", i))
            ticket(("mt", i), 2)
        for j in range(4):
            ticket(("pt", j), 3)
        for i in range(NT):
            ticket(("qp", i))
            ticket(("qt", i), 2)
        for g in range(2):
            for h in range(4):
                ticket(("qn", g, h))
                ticket(("kn", g, h))
                ticket(("knp", g, h))
            for j in range(9):
                ticket(("mv", g, j))
            for n in range(20 + 20 * g, 40 + 20 * g):
                ticket(("S", n))
                ticket(("PT", n), 2 + n % 2)
        plan_out(1)

        kdT_bank, o_bank = psum[1][:, 0:128], psum[1][:, 512:640]
        s_bank, ogT_bank = psum[3][:, 0:256], psum[3][:, 512:640]

        class Pairs:

            def __init__(self, what):
                self.of = [signal(f"pair{p}_{what}", order[p]) for p in range(4)]

            def sem(self, key):
                return self.of[pair_of[key]].sem

            def __getitem__(self, key):
                return self.of[pair_of[key]][key]

        pe_full = Pairs("full")
        ps_free = Pairs("free")
        before = {}
        for p in range(4):
            for prev, k in zip(order[p], order[p][1:]):
                before[k] = prev

        def claim(pe, key):
            if key in before:
                pe.wait_ge(*ps_free[before[key]])
            return psum[pair_of[key]]

        def filled(eng, key):
            eng.wait_ge(*pe_full[key])
            return psum[pair_of[key]]

        class Written:

            def __init__(self, key_of):
                self.key_of = key_of

            def __getitem__(self, k):
                return ps_free[self.key_of(k)]

        id_in = signal("identity_loaded", ["all"], 16)
        cst_in = signal("constants_loaded", ["all"], 32)
        cst_b = signal("constants_ready", ["dve"])
        lbl_in = signal("lower_bound_logits_loaded", ["all"], 16)
        vec_in = signal("vectors_loaded", ["all"], 16 * 5)
        state_in = signal("states_loaded", ["all"], 16)
        past_in = signal("past_fox_loaded", ["all"], 48)
        pastm_in = signal("past_mla_loaded", ["all"], 48)
        mg_in = signal("mla_gains_loaded", ["all"], 32)
        x_loaded = [signal(f"x_loaded{i}", ["all"], 32 if i == 4 else 16) for i in range(NT)]
        evac = Written(lambda k: k)
        lb_done = signal("lower_bound_logits_ready", ["max"])
        lb_e = signal("lower_bound_exps_ready", ["exp"])
        v_sb = Written(lambda i: ("v", i))
        g_exp = signal("gate_exp_written", list(range(NT)))
        g_sb = signal("gate_written", list(range(NT)))
        q_sb = Written(lambda h: ("q", h))
        f_exp = signal("f_exp_written", list(range(HH)))
        f_sig = signal("f_written", list(range(HH)))
        f_ln = signal("log_f_written", list(range(HH)))
        b_sb = signal("b_written", list(range(HH)))
        nb_sb = signal("minus_b_written", list(range(HH)))
        eb_sb = signal("exp_b_written", list(range(HH)))
        qe_sb = signal("decayed_q_k_written", list(range(HH)))
        d_sb = signal("decay_exponents_written", list(range(20)))
        de_sb = signal("decays_written", list(range(20)))
        gm_sb = signal("decayed_levels_written", list(range(20)))
        a_sb = signal("A_written", list(range(20)))
        kdT_ps = signal("kd_transposed", list(range(20)))
        kdT_sb = signal("kdT_written", list(range(20)))
        o_ps = signal("o_in_psum", list(range(20)))
        s_ps = signal("S_in_psum", list(range(20)))
        s_sb = signal("S_written", list(range(20)))
        o_ms = signal("o_mean_squares_ready", list(range(20)))
        o_rs = signal("o_rms_ready", list(range(20)))
        og_sb = signal("gated_o_written", list(range(20)))
        ogT_ps = signal("gated_o_transposed", list(range(20)))
        ogT_sb = signal("mixed_hg_written", list(range(20)))
        zero_st = signal("overflow_rows_zeroed", ["all"], 16 * NOV)
        st_hg = signal("hg_states_stored", ["all"], 32)
        fk_st = [signal(f"fox_k_stored{b}", [(i, p) for i in range(b, NT, 2)
                                             for p in range(2 if i == 4 else 1)], 16) for b in range(2)]
        fv_st = signal("fox_v_stored", ["all"], 16 * 6)
        fq_sb = Written(lambda h: ("fq", h))
        fk_sb = Written(lambda i: ("fk", i))
        fkt_sb = Written(lambda i: ("fkt", i))
        fv_sb = Written(lambda i: ("fv", i))
        lf_x = signal("forget_logit_written", ["x"])
        lf_l = signal("forget_log_written", ["x"])
        lf_sb = signal("forget_sums_written", ["x"])
        lf_st = signal("logf_stored", ["all"], 48)
        kp_sb = Written(lambda j: ("kp", j))
        N_ATT = len(att_units)
        mx_sb = signal("row_max_ready", list(range(N_ATT)))
        ex_fox = signal("fox_probs_written", list(range(len(fox_units))))

        class Exps:

            def __getitem__(self, n):
                return ex_fox[n] if att_units[n][0] == "fox" else ps_free[("S", n)]

        ex_sb = Exps()
        dg_sb = signal("row_scale_written", list(range(N_ATT)))
        pT_a = signal("pT_blocks_written", list(range(N_ATT)))
        pT_b = signal("pT_own_written", list(range(N_ATT)))
        oT_ps = signal("oT_in_psum", list(range(N_ATT)))
        lnk = [(s, i) for s in range(4) for i in range(NT)]
        xr_in = [signal(f"residual_loaded{i}", [(s, i, c) for s in range(4)
                                                for c in range(2 if (s == 0 and i == 4) else 1)], 16)
                 for i in range(NT)]
        wd_sb = signal("weight_diagonals_written", [0, 1])
        r_mv = signal("ln_stats_ready", lnk)
        r_rs = signal("ln_scale_ready", lnk)
        r_sb = signal("ln_written", lnk)
        x_st = [signal(f"rows_stored{b}", [(s, i) for s in range(4) for i in range(b, NT, 2)], 16)
                for b in range(2)]
        lng_in = signal("ln_params_loaded", list(range(4)), 32)
        lg_sb = Written(lambda k: ("lg", *k))
        r_e = signal("router_exp_written", [0, 1])
        mk_sb = signal("expert_mask_written", [0, 1])
        rt_sb = signal("router_done", [0, 1])
        oh_sb = signal("onehots_written", [(l, e) for l in range(2) for e in range(NE)])
        ix_sb = signal("slot_tokens_written", [(l, g) for l in range(2) for g in range(len(IX_GROUPS))])
        mi_ms = signal("mla_mean_squares_ready", list(range(NT)))
        mi_a = signal("mla_rms_ready", list(range(NT)))
        mi_sb = signal("mla_latents_written", list(range(NT)))
        mt_sb = Written(lambda i: ("mt", i))
        mi_st = [signal(f"mla_stored{b}", [(i, c) for i in range(b, NT, 2)
                                           for c in range(4 if i == 4 else 2)], 16) for b in range(2)]
        pt_sb = Written(lambda j: ("pt", j))
        qp_sb = signal("q_rope_written", list(range(NT)))
        qt_sb = Written(lambda i: ("qt", i))
        qn_sb = Written(lambda k: ("qn", *k))
        kn_sb = Written(lambda k: ("kn", *k))
        knp_sb = Written(lambda k: ("knp", *k))
        mvs_sb = Written(lambda k: ("mv", *k))
        ALLE = [(l, e) for l in range(2) for e in range(NE)]
        we_in = [signal(f"expert_weights_loaded{b}", [le for le in ALLE if le[1] % 4 == b], 48)
                 for b in range(4)]
        xg_in = [signal(f"expert_rows_loaded{b}", [le for le in ALLE if le[1] % 2 == b], 16) for b in range(2)]
        xgT_ps = signal("expert_rows_transposed", ALLE)
        xgT_sa = signal("expert_rowsT_written_act", ALLE)
        xgT_sd = signal("expert_rowsT_written_dve", ALLE)
        gu_ps = signal("gate_up_in_psum", ALLE)
        eg_sb = signal("gate_exp_ready", ALLE)
        h_sb = signal("hidden_written", ALLE)
        hT_ps = signal("hidden_transposed", ALLE)
        hT_sb = signal("hiddenT_written", ALLE)
        dn_ps = signal("down_in_psum", ALLE)
        y_sa = signal("expert_out_written_act", ALLE)
        y_sd = signal("expert_out_written_dve", ALLE)
        y_st = [signal(f"expert_out_stored{b}", [le for le in ALLE if le[1] % 2 == b], 16) for b in range(2)]
        yg_in = [signal(f"token_rows_gathered{i}", [0, 1], 32) for i in range(NT)]
        c_dve, c_act, c_pool = sem("dve_steps"), sem("act_steps"), sem("pool_steps")
        ov = [{k: sem(f"ov_{k}{l}") for k in ("cnt", "oh", "ix", "id", "xg", "tx", "xt", "w", "gu", "ex",
                                              "h", "ht", "hs", "dn", "y", "st", "turn")} for l in range(2)]

        w_in_d = a["even_w_in"][0].rearrange("(k p) n -> p k n", p=128)
        mi_d = a["mla_w_in"][0].rearrange("(k p) n -> p k n", p=128)
        items = []

        def item(name, slot, nslots, src, last):
            k, n = src.shape[1], src.shape[2]
            view = ring[:, slot * SLOT:slot * SLOT + k * n].rearrange("p (k n) -> p k n", k=k)
            items.append((name, slot, nslots, src, last, view))

        for name, c, slot, last in (("f", 1, 0, ("f", 3)), ("v", 2, 2, ("v", 4)), ("q", 0, 4, ("q", 3)),
                                    ("g", 3, 2, ("g", 4)), ("fq", 4, 2, ("fq", 3)), ("fk", 5, 0, ("fk", 4)),
                                    ("fv", 6, 4, ("fv", 4))):
            item(name, slot, 2, w_in_d[:, :, 512 * c:512 * c + 512], last)
        wo_d = [a[n][0].rearrange("(k p) n -> p k n", p=128) for n in ("even_w_out", "mla_w_out")]
        item(("wo", 0, 0), 2, 2, wo_d[0][:, :, 0:512], ("wo", 0, 4))
        item(("wo", 0, 1), 0, 2, wo_d[0][:, :, 512:1024], ("wo", 0, 4))
        n_items0 = len(items)
        item("mi0", 0, 2, mi_d[:, :, 0:512], ("mi", 4))
        item("mi1", 2, 2, mi_d[:, :, 512:832], ("mi", 4))
        item("uk", 4, 1, a["mla_w_uk"][0].rearrange("(k p) h d -> p k (h d)", p=128), ("knp", 1, 3))
        item("uv", 5, 1, a["mla_w_uv"][0].rearrange("(k p) h d -> p k (h d)", p=128), ("mv", 1, 8))
        item("uq", 0, 3, a["mla_w_uq"][0].rearrange("(k p) n -> p k n", p=128), ("qn", 1, 3))
        item(("wo", 1, 0), 3, 2, wo_d[1][:, :, 0:512], ("wo", 1, 4))
        item(("wo", 1, 1), 0, 2, wo_d[1][:, :, 512:1024], ("wo", 1, 4))
        w_in = [signal(f"weights_loaded{s}", [it[0] for it in items if it[1] == s], 16) for s in range(6)]
        w_ff = sb("w_ff", [128, KD, 4])

        def weights(pe, name):
            it = next(x for x in items if x[0] == name)
            pe.wait_ge(*w_in[it[1]][name])
            return it[5]

        def earlier_users(n):
            _, slot, ns, *_ = items[n]
            out = []
            for m in range(n - 1, -1, -1):
                if items[m][1] < slot + ns and slot < items[m][1] + items[m][2]:
                    out.append(items[m][4])
            return out

        def token_halves(view):
            return view.rearrange("p (s t) -> p s t", s=2)[:, :, 0:TOK // 2]

        def expert_place(e):
            base = (ring if e % 4 < 2 else wexp)[:, (e % 2) * 3 * SLOT:(e % 2) * 3 * SLOT + 3 * SLOT]
            gu = base[:, 0:2 * SLOT].rearrange("p (k n) -> p k n", k=KD)
            dn = base[:, 2 * SLOT:3 * SLOT].rearrange("p (k n) -> p k n", k=2)
            return gu, dn

        gate_d = a["moe_w_gate"].rearrange("l e (k p) n -> (l e) p k n", p=128)
        up_d = a["moe_w_up"].rearrange("l e (k p) n -> (l e) p k n", p=128)
        down_d = a["moe_w_down"].rearrange("l e (k p) n -> (l e) p k n", p=128)

        def mixed(k, i):
            src = mixT[:, k, :] if k < 4 else xT[:, k, :]
            return src[:, 128 * i:128 * i + TILES[i]]

        def att_rows(i):
            return (4 if i == 4 else i + 1), TILES[i], (0 if i == 4 else NS)

        def score_parts(i):
            if i == 4:
                return 432, [(432, 80), (512, PAST)]
            n = NM + 128 * (i + 1)
            return (512, [(512, n)]) if n <= 512 else (512 - n // 2, [(512 - n // 2, n // 2), (512, n // 2)])

        def row_dst(i, prompt, sample):
            if i < 4:
                return [((0, 128), prompt[NM + 128 * i:NM + 128 * i + 128, :])]
            return [((0, NS), sample[:, :]), ((NS, NS + NM), prompt[0:NM, :])]

        def pairs(view, L):
            part = list(view.ap[0])
            both = bass.AP(view.tensor, view.offset, [part, [2 * L, 64 // L], [PAD + L, 2], [1, L]])
            mid = bass.AP(view.tensor, view.offset + L - 1, [part, [2 * L, 64 // L], [PAD, 2], [0, L]])
            return both, mid

        block = ctx.enter_context(nc.Block())

        @block.sync
        def _(sp):
            def load_item(n):
                name, slot, _, src, _, view = items[n]
                for last in earlier_users(n):
                    sp.wait_ge(*pe_full[last])
                sp.dma_start(view, src).then_inc(w_in[slot].sem, 16)

            def load_expert(l, e):
                gu, dn = expert_place(e)
                s = we_in[e % 4].sem
                sp.dma_start(gu[:, :, 0:DE], gate_d[l * NE + e]).then_inc(s, 16)
                sp.dma_start(gu[:, :, DE:2 * DE], up_d[l * NE + e]).then_inc(s, 16)
                sp.dma_start(dn, down_d[l * NE + e]).then_inc(s, 16)

            for i in (0, 2):
                sp.dma_start(x_in[:, i, :], a["x_prompt"][0, 128 * i:128 * i + 128, :]).then_inc(x_loaded[i].sem, 16)
            sp.dma_start(x_in[0:NS, 4, :], a["x_sample"][0]).then_inc(x_loaded[4].sem, 16)
            sp.dma_start(x_in[NS:NS + NM, 4, :], a["meta_tokens"]).then_inc(x_loaded[4].sem, 16)
            for n in range(n_items0):
                load_item(n)
            for l in range(2):
                last_att = 19 if l == 0 else N_ATT - 1
                sp.wait_ge(*oT_ps[last_att])
                if l == 0:
                    sp.wait_ge(*fv_st["all"])
                    for b in range(2):
                        sp.wait_ge(fk_st[b].sem, fk_st[b].total)
                    sp.wait_ge(*st_hg["all"])
                    sp.wait_ge(*lf_st["all"])
                else:
                    for b in range(2):
                        sp.wait_ge(mi_st[b].sem, mi_st[b].total)
                load_expert(l, 2)
                load_expert(l, 3)
                sp.wait_ge(*pe_full[("wo", l, 4)])
                load_expert(l, 0)
                load_expert(l, 1)
                for e in range(NE):
                    if e + 4 < NE:
                        sp.wait_ge(*dn_ps[(l, e)])
                        load_expert(l, e + 4)
                    sp.wait_ge(*y_sa[(l, e)])
                    sp.wait_ge(*y_sd[(l, e)])
                    sp.dma_start(y_rows[l][128 * e:128 * e + 128, :], yb[:, e % 2, :]).then_inc(y_st[e % 2].sem, 16)
                    if l == 0 and e == 13:
                        for n in range(n_items0, n_items0 + 4):
                            load_item(n)
                mk = ov[l]
                sp.wait_ge(*ix_sb[(l, LAST_IX)])
                count = sp.value_load(ovi[0:1, 0:1], min_val=0, max_val=NOV)
                with sp.Fori(0, NOV) as b:
                    with sp.If(count > b):
                        sp.wait_ge(*dn_ps[(l, 14)])
                        sp.wait_ge(mk["id"], b + 1)
                        sp.sem_inc(mk["turn"], 1)
                        ex = sp.value_load(ovi[0:1, 1:2], min_val=0, max_val=NE - 1)
                        gu, dn = expert_place(2)
                        le = ex + l * NE
                        sp.dma_start(gu[:, :, 0:DE], gate_d[bass.ds(le, 1)].rearrange("o p k n -> p (o k) n")
                                     ).then_inc(mk["w"], 16)
                        sp.dma_start(gu[:, :, DE:2 * DE], up_d[bass.ds(le, 1)].rearrange("o p k n -> p (o k) n")
                                     ).then_inc(mk["w"], 16)
                        sp.dma_start(dn, down_d[bass.ds(le, 1)].rearrange("o p k n -> p (o k) n")
                                     ).then_inc(mk["w"], 16)
                        sp.wait_ge(mk["y"], b + 1)
                        sp.dma_start(y_rows[l][bass.ds(b * 128 + NE * 128, 128), :], yb[:, 0, :]
                                     ).then_inc(mk["st"], 16)
                        sp.wait_ge(mk["st"], b * 16 + 16)
                        sp.sem_inc(mk["turn"], 1)
                if l == 0:
                    for n in range(n_items0 + 4, len(items)):
                        load_item(n)
            for s in (st_hg, fv_st, lf_st, *fk_st, *mi_st, *x_st, *y_st):
                sp.wait_ge(s.sem, s.total)

        @block.gpsimd
        def _(pool):
            zrow = xr[:, 1, :]
            chain = Chain(pool, c_pool)
            chain(pool.memset(zrow, 0.0))
            chain(pool.memset(neg_half, -0.5))

            def inverse_root(dst, src, eps, done):
                P, n = src.shape
                chain(pool.tensor_scalar(src, src, eps, None, ALU.add))
                pool.tensor_tensor(dst, src, neg_half[0:P, 0:n], ALU.pow).then_inc(done.sem, 1)

            xf = [a["x_prompt"][0], a["x_sample"][0], a["meta_tokens"]]
            st_hg_dst = [hg_prompt[0, 0].rearrange("h k v -> k h v"), hg_sample[0, 0].rearrange("h k v -> k h v")]

            def o_scale(u):
                P, b = TILES[units[u][1]], u % 2
                pool.wait_ge(*o_ms[u])
                inverse_root(hstat[0:P, 2 * b + 1:2 * b + 2], hstat[0:P, 2 * b:2 * b + 1], RMS_EPS, o_rs)

            for u, (h, i) in enumerate(units):
                if i == 4:
                    pool.wait_ge(*nb_sb[h])
                    pool.wait_ge(*b_sb[h])
                if u >= 2:
                    pool.wait_ge(*pe_full[("A", u - 2)])
                for n, L in enumerate(LEVELS):
                    both, mid = pairs(bn[:, h % 2, 0, 128 * i:128 * i + 128], L)
                    dst = gbuf[:, u % 2, n, :].rearrange("p (q s r) -> p q s r", s=2, r=L)
                    last = pool.tensor_tensor(dst, both, mid, ALU.subtract)
                last.then_inc(d_sb.sem, 1)
                if u >= 3:
                    o_scale(u - 3)
                if u == 4:
                    for n in range(NOV):
                        pool.dma_start(y_all[128 * (NE + n):128 * (NE + n) + 128, :], zrow).then_inc(zero_st.sem, 16)
            for u in range(17, 20):
                o_scale(u)
            pool.wait_ge(*s_sb[19])
            pool.dma_start(st_hg_dst[0], sp_).then_inc(st_hg.sem, 16)
            pool.dma_start(st_hg_dst[1], ss_).then_inc(st_hg.sem, 16)
            pool.wait_ge(st_hg.sem, 32)
            pool.wait_ge(*og_sb[19])
            pool.wait_ge(*ogT_ps[19])
            pool.dma_start(vp, a["cache_fox_v"][0, 0].rearrange("(j p) h d -> p j (h d)", p=128)).then_inc(past_in.sem, 16)
            pool.dma_start(kps, a["cache_fox_k"][0, 0].rearrange("(j p) h d -> p j (h d)", p=128)).then_inc(past_in.sem, 16)
            pool.dma_start(lf[0:4, 0:PAST], a["cache_fox_logf"][0, 0].rearrange("t h -> h t"),
                           allow_slow_non_contiguous=True).then_inc(past_in.sem, 16)

            def store_rows(i, tile, prompt, sample, sm):
                for (lo, hi), dst in row_dst(i, prompt, sample):
                    pool.dma_start(dst, tile[lo:hi, :]).then_inc(sm, 16)

            k2 = [fk_prompt[0, 0].rearrange("t h d -> t (h d)"), fk_sample[0, 0].rearrange("t h d -> t (h d)")]
            v2 = [fv_prompt[0, 0].rearrange("t h d -> t (h d)"), fv_sample[0, 0].rearrange("t h d -> t (h d)")]
            for i in range(NT):
                pool.wait_ge(*fk_sb[i])
                store_rows(i, fks[:, i % 2, :], k2[0], k2[1], fk_st[i % 2].sem)
            for i in range(NT):
                pool.wait_ge(*fv_sb[i])
                store_rows(i, fv[:, i, :], v2[0], v2[1], fv_st.sem)
            pool.wait_ge(*lf_sb["x"])
            fp = flf_prompt[0, 0].rearrange("t h -> h t")
            pool.dma_start(fp[:, NM:NM + SEQ], lf[0:4, PAST:PAST + SEQ], allow_slow_non_contiguous=True).then_inc(lf_st.sem, 16)
            pool.dma_start(fp[:, 0:NM], lf[0:4, PAST + META0:PAST + TOK], allow_slow_non_contiguous=True).then_inc(lf_st.sem, 16)
            pool.dma_start(flf_sample[0, 0].rearrange("t h -> h t"), lf[0:4, PAST + SEQ:PAST + META0],
                           allow_slow_non_contiguous=True).then_inc(lf_st.sem, 16)

            def load_residual(s, i):
                b, dst, sm = i % 2, residual(s, i), xr_in[i].sem
                if s % 2 == 1 and i >= 2:
                    pool.wait_ge(*pe_full[("wo", s // 2, 4)])
                elif i >= 2:
                    pool.wait_ge(*r_mv[(s, i - 2)])
                elif s > 0:
                    pool.wait_ge(*r_mv[(s - 1, i if s == 2 else 4 - b)])
                if s == 0 and i < 4:
                    pool.dma_start(dst, xf[0][128 * i:128 * i + 128, :]).then_inc(sm, 16)
                elif s == 0:
                    pool.dma_start(dst[0:NS], xf[1][:, :]).then_inc(sm, 16)
                    pool.dma_start(dst[NS:NS + NM], xf[2][:, :]).then_inc(sm, 16)
                else:
                    pool.wait_ge(*x_st[b][(s - 1, i)])
                    pool.dma_start(dst[0:TILES[i]], x_rows[s - 1][128 * i:128 * i + TILES[i], :]).then_inc(sm, 16)

            def load_ln_params(s):
                gn, bnm = (("ln_mix_g", "ln_mix_b"), ("ln_ffn_g", "ln_ffn_b"))[s % 2]
                if s > 0:
                    pool.wait_ge(*r_sb[(s - 1, 4)])
                pool.dma_start(lng[:, 0, :], a[gn][s // 2].partition_broadcast(128)).then_inc(lng_in.sem, 16)
                pool.dma_start(lng[:, 1, :], a[bnm][s // 2].partition_broadcast(128)).then_inc(lng_in.sem, 16)

            def layer_norm_rows(s):
                if s % 2 == 0:
                    load_ln_params(s)
                    load_residual(s, 0)
                    load_residual(s, 1)
                for i in range(NT):
                    P, b = TILES[i], i % 2
                    pool.wait_ge(*r_mv[(s, i)])
                    inverse_root(lrs[0:P, b, 1:2], lmv[0:P, b, 1:2], LN_EPS, r_rs)
                    if i + 3 < NT and s % 2 == 1:
                        gather_rows(s // 2, i + 3)
                    pool.wait_ge(*r_sb[(s, i)])
                    t = rb[:, i % 2, :]
                    if s < 3:
                        pool.dma_start(x_rows[s][128 * i:128 * i + P, :], t[0:P, :]).then_inc(x_st[i % 2].sem, 16)
                    elif i < 4:
                        pool.dma_start(y_prompt[0, 128 * i:128 * i + 128, :], t).then_inc(x_st[i % 2].sem, 16)
                    else:
                        pool.dma_start(y_sample[0], t[0:NS, :]).then_inc(x_st[i % 2].sem, 16)
                    if i + 2 < NT and s % 2 == 0:
                        load_residual(s, i + 2)

            def gather_rows(l, i):
                P = TILES[i]
                for c in range(2):
                    pool.indirect_dma_start(
                        yg[0:P, i, c, :], None, y_rows[l],
                        bass.IndirectOffsetOnAxis(ap=posi[0:P, c, i:i + 1], axis=0)).then_inc(yg_in[i].sem, 16)

            def experts(l):
                for b in range(2):
                    last = (2 * l, 4 if b == 0 else 3)
                    pool.wait_ge(*x_st[b][last])
                for e in range(NE):
                    for g in range(len(IX_GROUPS)):
                        if e == IX_GROUPS[g][0]:
                            pool.wait_ge(*ix_sb[(l, g)])
                    if e >= 2:
                        pool.wait_ge(*xgT_ps[(l, e - 2)])
                    if e == 3:
                        load_ln_params(2 * l + 1)
                        for i in range(NT):
                            load_residual(2 * l + 1, i)
                    pool.indirect_dma_start(
                        xg[:, e % 2, :], None, x_rows[2 * l],
                        bass.IndirectOffsetOnAxis(ap=sloti[:, e:e + 1], axis=0)).then_inc(xg_in[e % 2].sem, 16)
                m = ov[l]
                pool.wait_ge(*xgT_ps[(l, NE - 1)])
                count = pool.value_load(ovi[0:1, 0:1], min_val=0, max_val=NOV)
                with pool.Fori(0, NOV) as b:
                    with pool.If(count > b):
                        pool.wait_ge(m["id"], b + 1)
                        pool.sem_inc(m["turn"], 1)
                        pool.indirect_dma_start(xg[:, 0, :], None, x_rows[2 * l],
                                                bass.IndirectOffsetOnAxis(ap=ovi[:, 2:3], axis=0)
                                                ).then_inc(m["xg"], 16)
                        pool.wait_ge(m["xg"], b * 16 + 16)
                        pool.wait_ge(m["st"], b * 16 + 16)
                pool.wait_ge(*zero_st["all"])
                for b in range(2):
                    pool.wait_ge(y_st[b].sem, (l + 1) * 16 * (NE // 2))
                for i in range(3):
                    gather_rows(l, i)

            pool.wait_ge(*zero_st["all"])
            pool.wait_ge(*g_sb[4])
            layer_norm_rows(0)
            experts(0)
            layer_norm_rows(1)
            pool.dma_start(qng[:, 0:QL], a["mla_q_norm_g"][0].partition_broadcast(128)).then_inc(mg_in.sem, 16)
            pool.dma_start(qng[:, QL:QL + KVL], a["mla_kv_norm_g"][0].partition_broadcast(128)).then_inc(mg_in.sem, 16)
            pool.dma_start(pst[:, :, 0:256], a["cache_mla_ckv"][0, 0].rearrange("(j p) n -> p j n", p=128)).then_inc(pastm_in.sem, 16)
            for c in range(2):
                pool.dma_start(pst[:, :, 256 + 64 * c:320 + 64 * c],
                               a["cache_mla_kpe"][0, 0].rearrange("(j p) n -> p j n", p=128)).then_inc(pastm_in.sem, 16)
            for i in range(NT):
                P, b = TILES[i], i % 2
                pool.wait_ge(*mi_ms[i])
                inverse_root(mst[0:P, b, 2:4], mst[0:P, b, 0:2], RMS_EPS, mi_a)
                pool.wait_ge(*mi_sb[i])
                store_rows(i, cvb[:, i % 2, :], ckv_prompt[0, 0], ckv_sample[0, 0], mi_st[i % 2].sem)
                store_rows(i, kpb[:, i % 2, 0:ROPE], kpe_prompt[0, 0], kpe_sample[0, 0], mi_st[i % 2].sem)
            layer_norm_rows(2)
            experts(1)
            layer_norm_rows(3)

        @block.tensor
        def _(pe):
            def transpose_tile(s, i, src):
                P = TILES[i]
                ps = claim(pe, ("T", s, i))
                for k in range(KD):
                    last = pe.transpose(ps[:, 128 * k:128 * k + P], src[0:P, 128 * k:128 * k + 128], ident[0:P, 0:P])
                last.then_inc(pe_full.sem(("T", s, i)), 1)

            def to_tokens(key, i, w, n, chunks=KD, src=None, sl=None):
                P = TILES[i]
                ps = claim(pe, key)
                for k in range(chunks):
                    last = pe.matmul(ps[0:P, 0:n], xT[:, k, 128 * i:128 * i + P], w[:, k, :],
                                     start=(k == 0), stop=(k == chunks - 1))
                last.then_inc(pe_full.sem(key), 1)

            def to_features(key, w, src, ncol):
                ps = claim(pe, key)
                chunks = src.shape[1]
                n = ncol if ncol <= 512 else ncol // 2
                for s in range(ncol // n):
                    for k in range(chunks):
                        last = pe.matmul(ps[0:w.shape[2], 512 * s:512 * s + n], w[:, k, :], src[:, k, n * s:n * s + n],
                                         start=(k == 0), stop=(k == chunks - 1))
                last.then_inc(pe_full.sem(key), 1)

            pe.wait_ge(*id_in["all"])
            for i in range(NT):
                pe.wait_ge(*x_loaded[i]["all"])
                transpose_tile(-1, i, x_in[:, i, :])
            pe.wait_ge(*evac[("T", -1, 4)])
            pe.wait_ge(*evac[("T", -1, 3)])
            for head0, nm in (("f", "v"), ("q", "g")):
                to_features((head0, 0), weights(pe, head0)[:, :, 0:128], xT, TOK)
                w = weights(pe, nm)
                for i in range(NT):
                    to_tokens((nm, i), i, w, 512)

            def unit_a(u):
                h, i = units[u]
                P, c0 = TILES[i], 128 * i
                pe.wait_ge(*gm_sb[u])
                ps = claim(pe, ("A", u))
                n0 = 1 if i == 4 else 0
                for n in range(n0, NL):
                    pe.matmul(ps[0:P, 128 * n:128 * n + P], gbuf[:, u % 2, n, 0:P], gbuf[:, u % 2, n, 0:P],
                              start=True, stop=True)
                pe.matmul(ps[0:P, 896:896 + P], qk[:, h % 2, 0, c0:c0 + P], qk[:, h % 2, 1, c0:c0 + P],
                               start=True, stop=True).then_inc(pe_full.sem(("A", u)), 1)

            def unit_b(u):
                h, i = units[u]
                P, c0, hc = TILES[i], 128 * i, slice(128 * h, 128 * h + 128)
                pe.wait_ge(*qe_sb[h])
                if u > 0:
                    pe.wait_ge(*kdT_sb[u - 1])
                pe.transpose(kdT_bank[0:P, :], kd[:, h % 2, c0:c0 + P], ident).then_inc(kdT_ps.sem, 1)
                pe.wait_ge(*a_sb[u])
                if u > 0:
                    pe.wait_ge(*og_sb[u - 1])
                    pe.wait_ge(*s_sb[u - 1])
                oo = o_bank
                if i == 4:
                    pe.wait_ge(*state_in["all"])
                    pe.matmul(oo[NS:P, :], asb[0:P, u % 2, NS:P], hv[0:P, i, hc], start=True, stop=True)
                    pe.matmul(oo[0:NS, :], asb[0:P, u % 2, 0:NS], hv[0:P, i, hc], start=True, stop=False)
                    last = pe.matmul(oo[0:NS, :], qe[:, h % 2, SEQ:META0], ss_[:, h, :], start=False, stop=True)
                else:
                    pe.matmul(oo[0:P, :], asb[0:P, u % 2, 0:P], hv[0:P, i, hc], start=True, stop=False)
                    last = pe.matmul(oo[0:P, :], qe[:, h % 2, c0:c0 + P], sp_[:, h, :], start=False, stop=True)
                last.then_inc(o_ps.sem, 1)
                pe.wait_ge(*kdT_sb[u])
                if i == 4:
                    pe.matmul(s_bank[:, 0:128], kdT[NS:NS + NM, u % 2, :], hv[NS:NS + NM, 4, hc], start=True, stop=True)
                    last = pe.matmul(s_bank[:, 128:256], kdT[0:NS, u % 2, :], hv[0:NS, 4, hc], start=True, stop=True)
                else:
                    last = pe.matmul(s_bank[:, 0:128], kdT[0:P, u % 2, :], hv[0:P, i, hc], start=True, stop=True)
                last.then_inc(s_ps.sem, 1)

            def unit_c(u):
                P = TILES[units[u][1]]
                pe.wait_ge(*og_sb[u])
                if u > 0:
                    pe.wait_ge(*ogT_sb[u - 1])
                pe.transpose(ogT_bank[:, 0:P], og[0:P, u % 2, :], ident[0:P, 0:P]).then_inc(ogT_ps.sem, 1)

            def fk_step(i):
                to_tokens(("fk", i), i, weights(pe, "fk"), 512)

            def project(kind, n, ks):
                key = (kind, n)
                w = w_ff if kind == "lf" else weights(pe, kind)[:, :, 128 * n:128 * n + 128]
                ps = claim(pe, key) if 0 in ks else psum[pair_of[key]]
                for k in ks:
                    for s in range(2):
                        n = TOK // 2
                        last = pe.matmul(ps[0:w.shape[2], 512 * s:512 * s + n], w[:, k, :], xT[:, k, n * s:n * s + n],
                                         start=(k == 0), stop=(k == KD - 1))
                if KD - 1 in ks:
                    last.then_inc(pe_full.sem(key), 1)

            pe.wait_ge(*v_sb[4])
            pe.wait_ge(*ps_free[("g", 4)])
            pe.wait_ge(*ps_free[("g", 3)])
            for u in range(len(units)):
                if u == 18:
                    pe.wait_ge(vec_in.sem, vec_in.total)
                if u in BETWEEN:
                    project(*BETWEEN[u])
                unit_a(u)
                if u >= 1:
                    unit_b(u - 1)
                if u >= 2:
                    unit_c(u - 2)
            fk_step(0)
            unit_b(19)
            unit_c(18)
            unit_c(19)

            pe.wait_ge(*kdT_sb[19])
            pe.wait_ge(*og_sb[19])
            for i in range(1, NT + 1):
                if i < NT:
                    fk_step(i)
                j = i - 1
                P = TILES[j]
                pe.wait_ge(*fk_sb[j])
                ps = claim(pe, ("fkt", j))
                for h in range(4):
                    last = pe.transpose(ps[:, 128 * h:128 * h + P], fks[0:P, j % 2, 128 * h:128 * h + 128], ident[0:P, 0:P])
                last.then_inc(pe_full.sem(("fkt", j)), 1)
            w = weights(pe, "fv")
            for i in range(NT):
                to_tokens(("fv", i), i, w, 512)
            pe.wait_ge(past_in.sem, 48)
            for j in range(4):
                ps = claim(pe, ("kp", j))
                for h in range(4):
                    last = pe.transpose(ps[:, 128 * h:128 * h + 128], kps[:, j, 128 * h:128 * h + 128], ident)
                last.then_inc(pe_full.sem(("kp", j)), 1)

            def att_scores(n):
                kind, h, i = att_units[n]
                nb, P, k0 = att_rows(i)
                W, c0 = 128 * nb, 128 * i
                ps = claim(pe, ("S", n))
                start, parts = score_parts(i)
                hh, r = h % 4, slice(64 * (h % 2), 64 * (h % 2) + 64)
                if kind == "fox":
                    lq, keys, past = [fq[:, h, c0:c0 + P]], [fkT[:, h, :]], [kpT[:, h, :]]
                    m_own, m_diag = const("m_own_fox"), const("m_causal")
                else:
                    lq = [qnT[:, hh, c0:c0 + P], qpT[r, h // 2, c0:c0 + P]]
                    keys, past = [knT[:, hh, :], peT[r, :]], [knpT[:, hh, :], pepT[r, :]]
                    m_own, m_diag = const("m_own_mla"), const("m_group")
                done = 0
                for lo, cols in parts:
                    if i < 4:
                        ks = [k_[:, done:done + cols] for k_ in keys]
                        first = NM + 512 - (NM + W) + done
                        mask = m_diag[:, first:first + cols]
                    elif done == 0:
                        ks, mask = [k_[:, NM + 512:NM + TOK] for k_ in keys], m_own
                    else:
                        ks, mask = past, const("m_past")
                    for c, (q_, k_) in enumerate(zip(lq, ks)):
                        pe.matmul(ps[0:P, lo:lo + cols], q_, k_, start=(c == 0), stop=False)
                    last = pe.matmul(ps[0:P, lo:lo + cols], identb[0:P, 0:P], mask[0:P, :], start=False, stop=True)
                    done += cols
                last.then_inc(pe_full.sem(("S", n)), 1)

            def att_transpose(n):
                _, _, i = att_units[n]
                nb, P, k0 = att_rows(i)
                pe.wait_ge(*ex_sb[n])
                pe.wait_ge(*dg_sb[n])
                ps = claim(pe, ("PT", n))
                d = diag[n % 3][0:P, 0:P]
                pe.matmul(ps[k0:80, 0:P], probs[n % 3][0:P, k0:80], d, start=True, stop=True)
                for j in range(nb):
                    last = pe.matmul(ps[:, 512 + 128 * j:512 + 128 * j + P],
                                     probs[n % 3][0:P, 80 + 128 * j:208 + 128 * j], d, start=True, stop=True)
                last.then_inc(pe_full.sem(("PT", n)), 1)

            def att_values(n):
                kind, h, i = att_units[n]
                nb, P, k0 = att_rows(i)
                pe.wait_ge(*pT_a[n])
                pe.wait_ge(*pT_b[n])
                out = psum[pair_of[("PT", n)]][:, 256:256 + P]
                if kind == "fox":
                    hc = slice(128 * h, 128 * h + 128)
                    vo, vb = fv[k0:80, 4, hc], [(vp if i == 4 else fv)[:, j, hc] for j in range(nb)]
                else:
                    hc = slice(128 * (h % 4), 128 * (h % 4) + 128)
                    vo, vb = mv_[k0:80, 4, hc], [mv_[:, (5 + j) if i == 4 else j, hc] for j in range(nb)]
                pe.matmul(out, vo, pT[k0:80, n % 2, 512:512 + P], start=True, stop=False)
                for j in range(nb):
                    last = pe.matmul(out, vb[j], pT[:, n % 2, 128 * j:128 * j + P], start=False, stop=(j == nb - 1))
                last.then_inc(oT_ps.sem, 1)

            def attention(first, last):
                for n in range(first, last + 3):
                    if n < last:
                        kind, h, i = att_units[n]
                        if kind == "fox" and i == 0:
                            for s in range(2):
                                ps = claim(pe, ("nf", h, s))
                                lo = 512 - 512 * s
                                if s == 0:
                                    pe.matmul(ps[:, 0:512], sel4[0:4, h, :], ff[0:4, 512:1024], start=True, stop=True)
                                    m = pe.matmul(ps[:, 512:592], sel4[0:4, h, :], ff[0:4, 1024:PAST + TOK], start=True, stop=True)
                                else:
                                    m = pe.matmul(ps[:, 0:512], sel4[0:4, h, :], ff[0:4, 0:512], start=True, stop=True)
                                m.then_inc(pe_full.sem(("nf", h, s)), 1)
                        att_scores(n)
                    if n - 3 >= first:
                        att_values(n - 3)
                    if first <= n - 2 < last:
                        att_transpose(n - 2)

            pe.wait_ge(*lf_sb["x"])
            pe.wait_ge(*fq_sb[3])
            pe.wait_ge(*fkt_sb[4])
            pe.wait_ge(*kp_sb[3])
            pe.wait_ge(*fv_sb[4])
            pe.wait_ge(*ogT_sb[19])
            pe.wait_ge(*s_sb[19])
            attention(0, 20)

            def out_and_experts(l):
                w0, w1 = weights(pe, ("wo", l, 0)), weights(pe, ("wo", l, 1))
                lastn = 19 if l == 0 else N_ATT - 1
                pe.wait_ge(*ps_free[("PT", lastn)])
                pe.wait_ge(*ps_free[("PT", lastn - 1)])
                for i in range(NT):
                    P = TILES[i]
                    ps = claim(pe, ("wo", l, i))
                    for half, w in ((0, w0), (1, w1)):
                        for k in range(KD):
                            last = pe.matmul(ps[0:P, 512 * half:512 * half + 512], mixed(k, i), w[:, k, :],
                                             start=(k == 0), stop=(k == KD - 1))
                        if half == 0 and i >= 2:
                            router_logits(l, i - 2)
                    last.then_inc(pe_full.sem(("wo", l, i)), 1)
                    if i >= 1:
                        normed_tile(l, i - 1)
                router_logits(l, NT - 2)
                normed_tile(l, NT - 1)
                router_logits(l, NT - 1)
                pe.wait_ge(*mk_sb[l])
                ps = claim(pe, ("rk", l))
                for i in range(NT):
                    m = maskb[:, NE * i:NE * i + NE]
                    for j in range(i):
                        pe.matmul(ps[:, NE * i:NE * i + NE], const("ones"), maskb[:, NE * j:NE * j + NE],
                                  start=(j == 0), stop=False)
                    pe.matmul(ps[:, NE * i:NE * i + NE], const("before"), m, start=(i == 0), stop=True)
                for j in range(NT):
                    last = pe.matmul(ps[:, 80:96], const("ones"), maskb[:, NE * j:NE * j + NE],
                                     start=(j == 0), stop=(j == NT - 1))
                last.then_inc(pe_full.sem(("rk", l)), 1)
                slot_tokens(l, 0)
                slot_tokens(l, 1)
                pe.wait_ge(*ps_free[("rk", l)])
                pe.wait_ge(*ps_free[("lg", l, 4)])
                pe.wait_ge(*ps_free[("T", 2 * l, 4)])
                experts(l)

            def slot_tokens(l, g):
                ps = claim(pe, ("ix", l, g))
                for e in IX_GROUPS[g]:
                    pe.wait_ge(*oh_sb[(l, e)])
                    for i in range(NT):
                        last = pe.matmul(ps[:, 512 + 2 * e:514 + 2 * e], oneh[:, e % 2, i, :], tok2[:, i, :],
                                         start=(i == 0), stop=(i == NT - 1))
                last.then_inc(pe_full.sem(("ix", l, g)), 1)

            def combine(l, i):
                P, s = TILES[i], 2 * l + 1
                ps = claim(pe, ("cb", l, i))
                pe.wait_ge(*wd_sb[l])
                pe.wait_ge(*xr_in[i][(s, i, 0)])
                pe.wait_ge(*yg_in[i][l])
                for half in (slice(0, 512), slice(512, 1024)):
                    pe.matmul(ps[0:P, half], adiag[0:P, 0:P], residual(s, i)[0:P, half], start=True, stop=False)
                    pe.matmul(ps[0:P, half], wdiag[0:P, i, 0, 0:P], yg[0:P, i, 0, half], start=False, stop=False)
                    last = pe.matmul(ps[0:P, half], wdiag[0:P, i, 1, 0:P], yg[0:P, i, 1, half], start=False, stop=True)
                last.then_inc(pe_full.sem(("cb", l, i)), 1)

            def normed_tile(l, i):
                pe.wait_ge(*r_sb[(2 * l, i)])
                transpose_tile(2 * l, i, rb[:, i % 2, :])

            def router_logits(l, i):
                P = TILES[i]
                pe.wait_ge(*evac[("T", 2 * l, i)])
                ps = claim(pe, ("lg", l, i))
                for k in range(KD):
                    last = pe.matmul(ps[0:P, 0:NE], xT[:, k, 128 * i:128 * i + P], rw[:, k, :],
                                     start=(k == 0), stop=(k == KD - 1))
                last.then_inc(pe_full.sem(("lg", l, i)), 1)

            def prev(le):
                n = ALLE.index(le)
                return ALLE[n - 1] if n else None

            def rows_t(l, e):
                pe.wait_ge(*xg_in[e % 2][(l, e)])
                if e > 0:
                    pe.wait_ge(*xgT_sa[(l, e - 1)])
                    pe.wait_ge(*xgT_sd[(l, e - 1)])
                for k in range(KD):
                    last = pe.transpose(psum[0][:, 128 * k:128 * k + 128], xg[:, e % 2, 128 * k:128 * k + 128], ident)
                last.then_inc(xgT_ps.sem, 1)

            def gate_up(l, e):
                pe.wait_ge(*we_in[e % 4][(l, e)])
                pe.wait_ge(*xgT_sa[(l, e)])
                pe.wait_ge(*xgT_sd[(l, e)])
                if e >= 2:
                    pe.wait_ge(*h_sb[(l, e - 2)])
                gu, _ = expert_place(e)
                bank = psum[1][:, 512 * (e % 2):512 * (e % 2) + 512]
                for k in range(KD):
                    last = pe.matmul(bank, xgT[:, e % 2, k, :], gu[:, k, :], start=(k == 0), stop=(k == KD - 1))
                last.then_inc(gu_ps.sem, 1)

            def hidden_t(l, e):
                pe.wait_ge(*h_sb[(l, e)])
                if e > 0:
                    pe.wait_ge(*hT_sb[(l, e - 1)])
                for k in range(2):
                    last = pe.transpose(psum[3][:, 128 * k:128 * k + 128], hb[:, e % 2, 128 * k:128 * k + 128], ident)
                last.then_inc(hT_ps.sem, 1)

            def down(l, e):
                pe.wait_ge(*hT_sb[(l, e)])
                if e > 0:
                    pe.wait_ge(*y_sa[(l, e - 1)])
                    pe.wait_ge(*y_sd[(l, e - 1)])
                _, dn = expert_place(e)
                for half in range(2):
                    for k in range(2):
                        last = pe.matmul(psum[2][:, 512 * half:512 * half + 512], hT[:, e % 2, 128 * k:128 * k + 128],
                                         dn[:, k, 512 * half:512 * half + 512], start=(k == 0), stop=(k == 1))
                last.then_inc(dn_ps.sem, 1)

            def experts(l):
                rows_t(l, 0)
                for e in range(NE + 1):
                    if e < NE:
                        gate_up(l, e)
                    if 1 <= e < LAST_IX:
                        slot_tokens(l, e + 1)
                    if e >= 1:
                        hidden_t(l, e - 1)
                    if e + 1 < NE:
                        rows_t(l, e + 1)
                    if e >= 1:
                        down(l, e - 1)
                m = ov[l]
                pe.wait_ge(*y_sa[(l, NE - 1)])
                pe.wait_ge(*y_sd[(l, NE - 1)])
                pe.wait_ge(*ix_sb[(l, LAST_IX)])
                count = pe.value_load(ovi[0:1, 0:1], min_val=0, max_val=NOV)
                with pe.Fori(0, NOV) as b:
                    with pe.If(count > b):
                        pe.wait_ge(m["oh"], b + 1)
                        for c in range(2):
                            for i in range(NT):
                                last = pe.matmul(psum[3][:, 512:514], oneh[:, c, i, :], tok2[:, i, :],
                                                 start=(c == 0 and i == 0), stop=(c == 1 and i == NT - 1))
                        last.then_inc(m["ix"], 1)
                        pe.wait_ge(m["xg"], b * 16 + 16)
                        for k in range(KD):
                            last = pe.transpose(psum[0][:, 128 * k:128 * k + 128], xg[:, 0, 128 * k:128 * k + 128], ident)
                        last.then_inc(m["tx"], 1)
                        pe.wait_ge(m["xt"], b + 1)
                        pe.wait_ge(m["w"], b * 48 + 48)
                        gu, dn = expert_place(2)
                        for k in range(KD):
                            last = pe.matmul(psum[1][:, 0:512], xgT[:, 0, k, :], gu[:, k, :], start=(k == 0), stop=(k == KD - 1))
                        last.then_inc(m["gu"], 1)
                        pe.wait_ge(m["h"], b + 1)
                        for k in range(2):
                            last = pe.transpose(psum[3][:, 128 * k:128 * k + 128], hb[:, 0, 128 * k:128 * k + 128], ident)
                        last.then_inc(m["ht"], 1)
                        pe.wait_ge(m["hs"], b + 1)
                        for half in range(2):
                            for k in range(2):
                                last = pe.matmul(psum[2][:, 512 * half:512 * half + 512], hT[:, 0, 128 * k:128 * k + 128],
                                                 dn[:, k, 512 * half:512 * half + 512], start=(k == 0), stop=(k == 1))
                        last.then_inc(m["dn"], 1)

            out_and_experts(0)
            for i in range(NT + 1):
                if i < NT:
                    combine(0, i)
                if i >= 1:
                    pe.wait_ge(*r_sb[(1, i - 1)])
                    transpose_tile(1, i - 1, rb[:, (i - 1) % 2, :])
            wq, wkv = weights(pe, "mi0"), weights(pe, "mi1")

            def latents_t(i):
                P = TILES[i]
                pe.wait_ge(*mi_sb[i])
                ps = claim(pe, ("mt", i))
                for k in range(4):
                    pe.transpose(ps[:, 128 * k:128 * k + P], cqb[0:P, i % 2, 128 * k:128 * k + 128], ident[0:P, 0:P])
                for k in range(2):
                    pe.transpose(ps[:, 512 + 128 * k:512 + 128 * k + P], cvb[0:P, i % 2, 128 * k:128 * k + 128], ident[0:P, 0:P])
                pe.transpose(ps[:, 768:768 + P], kpb[0:P, i % 2, :], ident[0:P, 0:P]).then_inc(pe_full.sem(("mt", i)), 1)

            for i in range(NT):
                P = TILES[i]
                pe.wait_ge(*evac[("T", 1, i)])
                ps = claim(pe, ("mi", i))
                for w, lo, n in ((wq, 0, 512), (wkv, 512, 320)):
                    for k in range(KD):
                        last = pe.matmul(ps[0:P, lo:lo + n], xT[:, k, 128 * i:128 * i + P], w[:, k, :],
                                         start=(k == 0), stop=(k == KD - 1))
                last.then_inc(pe_full.sem(("mi", i)), 1)
                if i >= 1:
                    latents_t(i - 1)
            latents_t(NT - 1)
            pe.wait_ge(pastm_in.sem, 48)
            for j in range(4):
                ps = claim(pe, ("pt", j))
                for k in range(3):
                    last = pe.transpose(ps[:, 128 * k:128 * k + 128], pst[:, j, 128 * k:128 * k + 128], ident)
                last.then_inc(pe_full.sem(("pt", j)), 1)
            uq = weights(pe, "uq")

            def rope_t(i):
                P = TILES[i]
                pe.wait_ge(*qp_sb[i])
                ps = claim(pe, ("qt", i))
                for k in range(4):
                    last = pe.transpose(ps[:, 128 * k:128 * k + P], qpb[0:P, i % 2, 128 * k:128 * k + 128], ident[0:P, 0:P])
                last.then_inc(pe_full.sem(("qt", i)), 1)

            for i in range(NT):
                P = TILES[i]
                pe.wait_ge(*mt_sb[i])
                ps = claim(pe, ("qp", i))
                for k in range(4):
                    rope_cols = uq[:, k, :].rearrange("p (h n) -> p h n", h=MH)[:, :, NOPE:NOPE + ROPE]
                    last = pe.matmul(ps[0:P, 0:512], cqT[:, k, 128 * i:128 * i + P], rope_cols,
                                     start=(k == 0), stop=(k == 3))
                last.then_inc(pe_full.sem(("qp", i)), 1)
                if i >= 1:
                    rope_t(i - 1)
            rope_t(NT - 1)
            uk, uv = weights(pe, "uk"), weights(pe, "uv")
            pe.wait_ge(*pt_sb[3])
            for g in range(2):
                for h in range(4):
                    hd = 4 * g + h
                    to_features(("qn", g, h), uq[:, :, 192 * hd:192 * hd + 128], cqT, TOK)
                    to_features(("kn", g, h), uk[:, :, 128 * hd:128 * hd + 128], ckT, TOK)
                    to_features(("knp", g, h), uk[:, :, 128 * hd:128 * hd + 128], ckpT, PAST)
                for j in range(9):
                    ps = claim(pe, ("mv", g, j))
                    P = TILES[j] if j < 5 else 128
                    src = ckT[:, :, 128 * j:128 * j + P] if j < 5 else ckpT[:, :, 128 * (j - 5):128 * (j - 5) + 128]
                    for k in range(2):
                        last = pe.matmul(ps[0:P, 0:512], src[:, k, :], uv[:, k, 512 * g:512 * g + 512],
                                         start=(k == 0), stop=(k == 1))
                    last.then_inc(pe_full.sem(("mv", g, j)), 1)
                pe.wait_ge(*qt_sb[4])
                pe.wait_ge(*mvs_sb[(g, 8)])
                pe.wait_ge(*qn_sb[(g, 3)])
                pe.wait_ge(*kn_sb[(g, 3)])
                pe.wait_ge(*knp_sb[(g, 3)])
                attention(20 + 20 * g, 40 + 20 * g)
            out_and_experts(1)
            for i in range(NT):
                combine(1, i)

        @block.scalar
        def _(act):
            chain = Chain(act, c_act)
            copy = act.copy

            act.dma_start(cst[:, 0:128], consts[:, 0:128]).then_inc(id_in.sem, 16)
            for i in (1, 3):
                act.dma_start(x_in[:, i, :], a["x_prompt"][0, 128 * i:128 * i + 128, :]).then_inc(x_loaded[i].sem, 16)
            act.dma_start(tl, a["hg_lb_logits"].rearrange("j (c p) -> p j c", p=128),
                          allow_slow_non_contiguous=True).then_inc(lbl_in.sem, 16)
            act.dma_start(cst[:, 128:n_f32], consts[:, 128:n_f32]).then_inc(cst_in.sem, 16)
            act.dma_start(consts_in, consts[:, n_f32:n_all]).then_inc(cst_in.sem, 16)
            act.dma_start(hgn, a["hg_norm_g"][0].rearrange("h v -> (h v)").partition_broadcast(128)).then_inc(vec_in.sem, 16)
            act.dma_start(fb4[0:4, :], a["fox_forget_bias"].rearrange("o h -> h o"),
                          allow_slow_non_contiguous=True).then_inc(vec_in.sem, 16)
            act.dma_start(rw[:, :, :], a["router_w"].rearrange("(k p) n -> p k n", p=128)).then_inc(vec_in.sem, 16)
            act.dma_start(rbias, a["router_bias"].partition_broadcast(128)).then_inc(vec_in.sem, 16)
            act.dma_start(w_ff[:, :, :], w_in_d[:, :, 3584:3588]).then_inc(vec_in.sem, 16)

            def evac_tile(s, i):
                P, key = TILES[i], ("T", s, i)
                ps = filled(act, key)
                copy(xT[:, :, 128 * i:128 * i + P], ps[:, :].rearrange("p (k t) -> p k t", k=KD)[:, :, 0:P]).then_inc(ps_free.sem(key), 1)

            for i in range(0, NT, 2):
                evac_tile(-1, i)
            act.wait_ge(*pe_full[("T", -1, 3)])
            act.dma_start(ss_, a["state_hgrn2"][0, 0].rearrange("h k v -> k h v")).then_inc(state_in.sem, 16)
            act.wait_ge(*lb_done["max"])
            act.activation(tl, tl, ACT.Exp).then_inc(lb_e.sem, 1)

            def q_copy(h):
                if h >= 2:
                    last = ("A", 5 * (h - 2) + 4)
                    act.wait_ge(*pe_full[last])
                copy(token_halves(qk[:, h % 2, 1, 0:TOK]), token_halves(filled(act, ("q", h)))).then_inc(ps_free.sem(("q", h)), 1)

            def f_exp(h):
                if h >= 1:
                    act.wait_ge(*b_sb[h - 1])
                act.activation(token_halves(ft[:, 0, 0:TOK]), token_halves(filled(act, ("f", h))), ACT.Exp, scale=-1.0).then_inc(ps_free.sem(("f", h)), 1)

            def f_log(h):
                act.wait_ge(*f_sig[h])
                act.activation(ft[:, 2, 0:TOK], ft[:, 0, 0:TOK], ACT.Ln).then_inc(f_ln.sem, 1)

            def b_steps(h):
                b = h % 2
                act.wait_ge(*b_sb[h])
                act.mul(bn[:, b, 0, :], bn[:, b, 1, :], -1.0).then_inc(nb_sb.sem, 1)
                act.wait_ge(*nb_sb[h])
                if h >= 2:
                    act.wait_ge(*s_sb[5 * (h - 2) + 4])
                act.activation(qe[:, b, :], bn[:, b, 1, :], ACT.Exp)
                for i, (lo, hi) in enumerate([(128 * i, 128 * i + 128) for i in range(4)]
                                             + [(SEQ, META0), (META0, TOK)]):
                    last = bn[:, b, 1, hi - 1:hi]
                    act.activation(ebl[:, b, i:i + 1], last, ACT.Exp)
                    e = act.activation(kd[:, b, lo:hi], bn[:, b, 0, lo:hi], ACT.Exp, bias=last)
                e.then_inc(eb_sb.sem, 1)

            def decays(u):
                act.wait_ge(*d_sb[u])
                act.activation(gbuf[:, u % 2, :, :], gbuf[:, u % 2, :, :], ACT.Exp).then_inc(de_sb.sem, 1)

            def unit_b(u):
                h, i = units[u]
                P, b = TILES[i], u % 2
                act.wait_ge(*kdT_ps[u])
                if u >= 2:
                    act.wait_ge(*s_ps[u - 2])
                copy(kdT[0:P, b, :], kdT_bank[0:P, :]).then_inc(kdT_sb.sem, 1)
                act.wait_ge(*o_ps[u])
                if u >= 2:
                    act.wait_ge(*og_sb[u - 2])
                st = hstat[0:P, 2 * b:2 * b + 1]
                act.activation(junk[0:P, 0:128], o_bank[0:P, :], ACT.Square, scale=DH ** -0.5, accum_out=st).then_inc(o_ms.sem, 1)

            def unit_c(u):
                h, i = units[u]
                P = TILES[i]
                act.wait_ge(*ogT_ps[u])
                copy(mixT[:, h, 128 * i:128 * i + P], ogT_bank[:, 0:P]).then_inc(ogT_sb.sem, 1)

            def copy_scaled(dst, key, n, scale):
                ps = filled(act, key)
                src = ps[:, 0:n] if n <= 512 else token_halves(ps)
                act.mul(dst if n <= 512 else token_halves(dst), src, scale).then_inc(ps_free.sem(key), 1)

            def fk_copy(i):
                P, key = TILES[i], ("fk", i)
                if i == 0:
                    act.wait_ge(*st_hg["all"])
                    act.wait_ge(*og_sb[19])
                    act.wait_ge(*ogT_ps[19])
                if i >= 2:
                    act.wait_ge(*pe_full[("fkt", i - 2)])
                    act.wait_ge(fk_st[i % 2].sem, 16 * (i // 2))
                copy(fks[0:P, i % 2, :], filled(act, key)[0:P, 0:512]).then_inc(ps_free.sem(key), 1)

            f_exp(0)
            for i in range(NT):
                P = TILES[i]
                copy(hv[0:P, i, :], filled(act, ("v", i))[0:P, 0:512]).then_inc(ps_free.sem(("v", i)), 1)
                if i == 1:
                    f_log(0)
            q_copy(0)
            b_steps(0)
            decays(0)
            for i in range(NT):
                P, key = TILES[i], ("g", i)
                act.activation(hgate[0:P, i, :], filled(act, key)[0:P, 0:512], ACT.Exp, scale=-1.0).then_inc(ps_free.sem(key), 1)
            for u in range(20):
                h, m = u // 5, u % 5
                if u + 1 < 20:
                    decays(u + 1)
                if u in BETWEEN and BETWEEN[u][0] == "fq" and KD - 1 in BETWEEN[u][2]:
                    n = BETWEEN[u][1]
                    copy_scaled(fq[:, n, :], ("fq", n), TOK, SC_FOX)
                if u >= 1:
                    unit_b(u - 1)
                if u >= 2:
                    unit_c(u - 2)
                if h + 1 < HH:
                    if m == 1:
                        f_exp(h + 1)
                    elif m == 2:
                        f_log(h + 1)
                    elif m == 3:
                        q_copy(h + 1)
                        b_steps(h + 1)
            unit_b(19)
            unit_c(18)
            unit_c(19)
            fk_copy(0)
            for i in range(1, NT + 1):
                if i < NT:
                    fk_copy(i)
                j, P = i - 1, TILES[i - 1]
                key = ("fkt", j)
                ps = filled(act, key)[:, 0:512].rearrange("p (h t) -> p h t", h=4)
                if j == 4:
                    copy(fkT[:, :, 0:NM], ps[:, :, NS:P])
                copy(fkT[:, :, NM + 128 * j:NM + 128 * j + P], ps[:, :, 0:P]).then_inc(ps_free.sem(key), 1)
            for i in range(NT):
                P, key = TILES[i], ("fv", i)
                copy(fv[0:P, i, :], filled(act, key)[0:P, 0:512]).then_inc(ps_free.sem(key), 1)
            act.wait_ge(*lf_x["x"])
            chain(act.activation(l2[0:4, :], l2[0:4, :], ACT.Exp, scale=-1.0))
            act.activation(l2[0:4, :], l2[0:4, :], ACT.Ln, bias=one[0:4]).then_inc(lf_l.sem, 1)
            for j in range(4):
                key = ("kp", j)
                copy(kpT[:, :, 128 * j:128 * j + 128], filled(act, key)[:, 0:512].rearrange("p (h t) -> p h t", h=4)).then_inc(ps_free.sem(key), 1)

            def att_exp(n):
                kind, _, i = att_units[n]
                nb, P, k0 = att_rows(i)
                W, b = 80 + 128 * nb, n % 3
                act.wait_ge(*mx_sb[n])
                dst = probs[b][0:P, k0:W]
                if n >= 3:
                    act.wait_ge(*dg_sb[n - 3])
                if kind == "fox":
                    act.activation(dst, dst, ACT.Exp, bias=nmax[0:P, b:b + 1],
                                              accum_out=rsum[0:P, b:b + 1]).then_inc(ex_fox.sem, 1)
                else:
                    act.wait_ge(*pe_full[("PT", n - 3)])
                    start, _ = score_parts(i)
                    src = psum[pair_of[("S", n)]][0:P, start:start + W - k0]
                    filled(act, ("S", n))
                    act.activation(dst, src, ACT.Exp, bias=nmax[0:P, b:b + 1],
                                              accum_out=rsum[0:P, b:b + 1]).then_inc(ps_free.sem(("S", n)), 1)

            def att_pt(n):
                nb, P, _ = att_rows(att_units[n][2])
                ps = filled(act, ("PT", n))
                if n >= 2:
                    act.wait_ge(*oT_ps[n - 2])
                copy(pT[:, n % 2, 0:128 * nb].rearrange("p (j t) -> p j t", j=nb)[:, :, 0:P],
                               ps[:, 512:512 + 128 * nb].rearrange("p (j t) -> p j t", j=nb)[:, :, 0:P]).then_inc(pT_a.sem, 1)

            def attention(first, last):
                for n in range(first, last + 2):
                    if n < last:
                        att_exp(n)
                    if n - 2 >= first:
                        att_pt(n - 2)

            attention(0, 20)

            def out_and_experts(l):
                for i in range(NT):
                    evac_tile(2 * l, i)
                act.wait_ge(*lg_sb[(l, NT - 1)])
                act.activation(sc_, lg, ACT.Exp, scale=-1.0).then_inc(r_e.sem, 1)

                def rows_copy(e):
                    act.wait_ge(*xgT_ps[(l, e)])
                    if e >= 2:
                        act.wait_ge(*gu_ps[(l, e - 2)])
                    copy(xgT[:, e % 2, 0:4, :], psum[0][:, 0:512].rearrange("p (k n) -> p k n", k=4)).then_inc(xgT_sa.sem, 1)

                rows_copy(0)
                for e in range(NE + 1):
                    if e < NE:
                        act.wait_ge(*gu_ps[(l, e)])
                        if e >= 2:
                            act.wait_ge(*h_sb[(l, e - 2)])
                        lo = 512 * (e % 2)
                        act.activation(eg[:, e % 2, :], psum[1][:, lo:lo + 256], ACT.Exp, scale=-1.0).then_inc(eg_sb.sem, 1)
                    if e + 1 < NE:
                        rows_copy(e + 1)
                    if e >= 1:
                        act.wait_ge(*dn_ps[(l, e - 1)])
                        if e >= 3:
                            act.wait_ge(*y_st[(e - 1) % 2][(l, e - 3)])
                        copy(yb[:, (e - 1) % 2, 0:512], psum[2][:, 0:512]).then_inc(y_sa.sem, 1)
                m = ov[l]
                act.wait_ge(*ix_sb[(l, LAST_IX)])
                count = act.value_load(ovi[0:1, 0:1], min_val=0, max_val=NOV)
                with act.Fori(0, NOV) as b:
                    with act.If(count > b):
                        act.wait_ge(m["gu"], b + 1)
                        act.activation(eg[:, 0, :], psum[1][:, 0:256], ACT.Exp, scale=-1.0).then_inc(m["ex"], 1)
                act.mul(adiag, ident, ALPHA)
                for i in range(NT):
                    for c in range(2):
                        last = act.mul(wdiag[:, i, c, :], ident, wts[:, c, i:i + 1])
                last.then_inc(wd_sb.sem, 1)
                if l == 0:
                    for i in range(NT):
                        evac_tile(1, i)

            out_and_experts(0)
            for i in range(NT + 1):
                if i < NT:
                    P, b = TILES[i], i % 2
                    ps = filled(act, ("mi", i))
                    if i >= 2:
                        act.wait_ge(*mi_sb[i - 2])
                    if i >= 1:
                        act.wait_ge(*mi_ms[i - 1])
                    act.activation(junk[0:P, 0:QL], ps[0:P, 0:QL], ACT.Square, scale=QL ** -0.5, accum_out=mst[0:P, b, 0:1])
                    act.activation(junk[0:P, 512:512 + KVL], ps[0:P, QL:QL + KVL], ACT.Square, scale=KVL ** -0.5,
                                   accum_out=mst[0:P, b, 1:2]).then_inc(mi_ms.sem, 1)
                if i >= 1:
                    j, P = i - 1, TILES[i - 1]
                    ps = filled(act, ("mt", j))
                    cs = slice(128 * j, 128 * j + P)
                    copy(cqT[:, :, cs], ps[:, 0:512].rearrange("p (k t) -> p k t", k=4)[:, :, 0:P])
                    copy(ckT[:, :, cs], ps[:, 512:768].rearrange("p (k t) -> p k t", k=2)[:, :, 0:P])
                    if j == 4:
                        copy(peT[:, 0:NM], ps[:, 768 + NS:768 + P])
                    copy(peT[:, NM + 128 * j:NM + 128 * j + P], ps[:, 768:768 + P]).then_inc(ps_free.sem(("mt", j)), 1)
            for j in range(4):
                ps = filled(act, ("pt", j))
                cs = slice(128 * j, 128 * j + 128)
                copy(ckpT[:, :, cs], ps[:, 0:256].rearrange("p (k t) -> p k t", k=2))
                copy(pepT[:, cs], ps[:, 256:384]).then_inc(ps_free.sem(("pt", j)), 1)
            for j in range(NT):
                P, key = TILES[j], ("qt", j)
                act.mul(qpT[:, :, 128 * j:128 * j + P],
                             filled(act, key)[:, 0:512].rearrange("p (k t) -> p k t", k=4)[:, :, 0:P], SC_MLA).then_inc(ps_free.sem(key), 1)
            for g in range(2):
                if g == 1:
                    for n in (38, 39):
                        act.wait_ge(*oT_ps[n])
                for h in range(4):
                    copy_scaled(qnT[:, h, :], ("qn", g, h), TOK, SC_MLA)
                    copy(knT[:, h, 0:NM], filled(act, ("kn", g, h))[:, 512 + META0 - TOK // 2:512 + TOK // 2])
                    copy_scaled(knT[:, h, NM:KCOL], ("kn", g, h), TOK, 1.0)
                    copy_scaled(knpT[:, h, :], ("knp", g, h), PAST, 1.0)
                if g == 0:
                    for b in range(2):
                        act.wait_ge(mi_st[b].sem, mi_st[b].total)
                    act.wait_ge(*pe_full[("qt", 4)])
                for j in range(9):
                    P, key = (TILES[j] if j < 5 else 128), ("mv", g, j)
                    copy(mv_[0:P, j, :], filled(act, key)[0:P, 0:512]).then_inc(ps_free.sem(key), 1)
                attention(20 + 20 * g, 40 + 20 * g)
            out_and_experts(1)

        @block.vector
        def _(dve):
            chain = Chain(dve, c_dve)
            tt, ts, stt, copy = dve.tensor_tensor, dve.tensor_scalar, dve.scalar_tensor_tensor, dve.tensor_copy

            def bc(v, n):
                return v.unsqueeze(len(v.shape)).to_broadcast(list(v.shape) + [n])

            dve.memset(one, 1.0)
            dve.memset(lg, 0.0)
            dve.memset(ft[:, 2, TOK:PAD], 0.0)
            chain(dve.memset(qk[:, :, :, TOK:PAD], 0.0))
            def evac_tile(s, i):
                P, key = TILES[i], ("T", s, i)
                ps = filled(dve, key)
                copy(xT[:, :, 128 * i:128 * i + P], ps[:, :].rearrange("p (k t) -> p k t", k=KD)[:, :, 0:P]).then_inc(ps_free.sem(key), 1)

            for i in range(1, NT, 2):
                evac_tile(-1, i)
            dve.wait_ge(*lbl_in["all"])
            chain(dve.tensor_reduce(mx4, tl.rearrange("p j c -> p c j"), AX, ALU.max))
            tt(tl, tl, mx4.unsqueeze(1).to_broadcast([128, 3, 4]), ALU.subtract).then_inc(lb_done.sem, 1)
            dve.wait_ge(*lb_e["exp"])
            chain(dve.tensor_reduce(se4, tl.rearrange("p j c -> p c j"), AX, ALU.add))
            chain(dve.reciprocal(se4, se4))
            chain(tt(lb, tl[:, 0, :], se4, ALU.mult))
            chain(ts(omlb, lb, -1.0, 1.0, ALU.mult, ALU.add))

            def gate(i):
                P, key = TILES[i], ("g", i)
                dve.wait_ge(*ps_free[key])
                chain(ts(hgate[0:P, i, :], hgate[0:P, i, :], 1.0, None, ALU.add))
                chain(dve.reciprocal(hgate[0:P, i, :], hgate[0:P, i, :]))
                tt(hgate[0:P, i, :], hgate[0:P, i, :], hgn[0:P, :], ALU.mult).then_inc(g_sb.sem, 1)

            def f_steps(h):
                b = h % 2
                f0, f1, f2 = (ft[:, n, 0:TOK] for n in range(3))
                dve.wait_ge(*ps_free[("f", h)])
                chain(ts(f1, f0, 1e37, 1.0, ALU.min, ALU.add))
                chain(dve.reciprocal(f1, f1))
                chain(ts(f2, f0, 1e37, omlb[:, h:h + 1], ALU.min, ALU.mult))
                if h >= 2:
                    last = ("A", 5 * (h - 2) + 4)
                    dve.wait_ge(*pe_full[last])
                chain(tt(qk[:, b, 0, 0:TOK], f2, f1, ALU.mult))
                ts(f0, f1, omlb[:, h:h + 1], lb[:, h:h + 1], ALU.mult, ALU.add).then_inc(f_sig.sem, 1)

            def b_scan(h):
                b = h % 2
                dve.wait_ge(*f_ln[h])
                dve.tensor_tensor_scan(bn[:, b, 1, :], reset, ft[:, 2, :], 0.0, ALU.mult, ALU.add).then_inc(b_sb.sem, 1)

            def decayed(h):
                b = h % 2
                dve.wait_ge(*eb_sb[h])
                dve.wait_ge(*q_sb[h])
                tt(qe[:, b, 0:TOK], qe[:, b, 0:TOK], qk[:, b, 1, 0:TOK], ALU.mult)
                tt(kd[:, b, 0:TOK], kd[:, b, 0:TOK], qk[:, b, 0, 0:TOK], ALU.mult).then_inc(qe_sb.sem, 1)

            def levels(u):
                h, i = units[u]
                dve.wait_ge(*de_sb[u])
                for n, L in enumerate(LEVELS):
                    both, _ = pairs(qk[:, h % 2, 0, 128 * i:128 * i + 128], L)
                    g = gbuf[:, u % 2, n, :].rearrange("p (q s r) -> p q s r", s=2, r=L)
                    last = tt(g, g, both, ALU.mult)
                last.then_inc(gm_sb.sem, 1)

            def unit_a(u):
                _, i = units[u]
                P, n0 = TILES[i], (1 if i == 4 else 0)
                key = ("A", u)
                ps = filled(dve, key)[0:P, 128 * n0:1024].rearrange("p (l t) -> p l t", t=128)[:, :, 0:P]
                m = am[0:P, 128 * n0:1024].rearrange("p (l t) -> p l t", t=128)[:, :, 0:P]
                if u >= 1:
                    dve.wait_ge(*a_sb[u - 1])
                tt(m, ps, lev[0:P, n0:8, 0:P], ALU.mult).then_inc(ps_free.sem(key), 1)
                dve.wait_ge(*ps_free[key])
                if u >= 2:
                    dve.wait_ge(*o_ps[u - 2])
                dve.tensor_reduce(asb[0:P, u % 2, 0:P], m.rearrange("p l t -> p t l"), AX, ALU.add).then_inc(a_sb.sem, 1)

            def unit_b(u):
                h, i = units[u]
                P, b = TILES[i], u % 2
                dve.wait_ge(*s_ps[u])
                if i == 4:
                    dve.wait_ge(*state_in["all"])
                    copy(sp_[:, h, :], s_bank[:, 0:128])
                    last = stt(ss_[:, h, :], ss_[:, h, :], ebl[:, h % 2, 4:5], s_bank[:, 128:256], ALU.mult, ALU.add)
                else:
                    last = stt(sp_[:, h, :], sp_[:, h, :], ebl[:, h % 2, i:i + 1], s_bank[:, 0:128], ALU.mult, ALU.add)
                last.then_inc(s_sb.sem, 1)
                dve.wait_ge(*o_rs[u])
                if u >= 2:
                    dve.wait_ge(*ogT_ps[u - 2])
                dve.wait_ge(*g_sb[i])
                stt(og[0:P, b, :], o_bank[0:P, :], hstat[0:P, 2 * b + 1:2 * b + 2],
                               hgate[0:P, i, 128 * h:128 * h + 128], ALU.mult, ALU.mult).then_inc(og_sb.sem, 1)

            f_steps(0)
            dve.wait_ge(*cst_in["all"])
            copy(cstb[:, :], consts_in)
            copy(identb[:, :], ident)
            copy(iotab[:, :], const("iota")).then_inc(cst_b.sem, 1)
            b_scan(0)
            decayed(0)
            levels(0)
            dve.wait_ge(vec_in.sem, vec_in.total)
            for i in range(NT):
                gate(i)
            for u in range(20):
                h, m = u // 5, u % 5
                if h + 1 < HH:
                    if m == 2:
                        f_steps(h + 1)
                    elif m == 3:
                        b_scan(h + 1)
                    elif m == 4:
                        decayed(h + 1)
                if u == 19:
                    dve.wait_ge(*zero_st["all"])
                    ps = filled(dve, ("lf", 0))
                    ts(token_halves(l1[0:4, :]), token_halves(ps[0:4, :]), fb4[0:4, :], None, ALU.add).then_inc(ps_free.sem(("lf", 0)), 1)
                if u + 1 < 20:
                    levels(u + 1)
                unit_a(u)
                if u >= 1:
                    unit_b(u - 1)
            unit_b(19)

            dve.wait_ge(*st_hg["all"])
            dve.wait_ge(*ogT_ps[19])
            for h in range(4):
                copy(sel4[0:4, h, :], ident[0:4, h:h + 1].to_broadcast([4, 128]))
            dve.wait_ge(*ps_free[("lf", 0)])
            stt(l2[0:4, :], l1[0:4, :], -1.0, l1[0:4, :], ALU.mult, ALU.max).then_inc(lf_x.sem, 1)
            dve.wait_ge(*lf_l["x"])
            dve.wait_ge(past_in.sem, 48)
            chain(stt(lf[0:4, PAST:PAST + TOK], l1[0:4, :], 0.0, l2[0:4, :], ALU.min, ALU.subtract))
            own, ones = PAST, const("ones")
            scan_of = lambda lo, hi, init: dve.tensor_tensor_scan(
                ff[0:4, lo:hi], ones[0:4, 0:1].to_broadcast([4, hi - lo]), lf[0:4, lo:hi], init, ALU.mult, ALU.subtract)
            scan_of(0, PAST, 0.0)
            chain(scan_of(own + META0, own + TOK, 0.0))
            scan_of(own, own + SEQ, ff[0:4, own + TOK - 1:own + TOK])
            scan_of(own + SEQ, own + META0, ff[0:4, PAST - 1:PAST]).then_inc(lf_sb.sem, 1)

            def att_max(n):
                kind, h, i = att_units[n]
                nb, P, k0 = att_rows(i)
                W, b = 80 + 128 * nb, n % 3
                if kind == "fox" and i == 0:
                    own_key, past_key = ("nf", h, 0), ("nf", h, 1)
                    ps = filled(dve, own_key)
                    copy(nfb[:, 0, 80:592], ps[:, 0:512])
                    copy(nfb[:, 0, 0:80], ps[:, 512:592])
                    copy(nfb[:, 1, 0:80], ps[:, 512:592]).then_inc(ps_free.sem(own_key), 1)
                    ps = filled(dve, past_key)
                    copy(nfb[:, 1, 80:592], ps[:, 0:512]).then_inc(ps_free.sem(past_key), 1)
                    dve.wait_ge(*ps_free[past_key])
                    dve.wait_ge(*ps_free[own_key])
                key = ("S", n)
                start, _ = score_parts(i)
                src = filled(dve, key)[0:P, start:start + W - k0]
                if n >= 3:
                    dve.wait_ge(*ex_sb[n - 3])
                if kind == "fox":
                    if n >= 3:
                        dve.wait_ge(*pe_full[("PT", n - 3)])
                    dve.tensor_tensor_reduce(probs[b][0:P, k0:W], src, nfb[0:P, int(i == 4), k0:W], 1.0, -3e38,
                                                  ALU.add, ALU.max, amax[0:P, b:b + 1]).then_inc(ps_free.sem(key), 1)
                    dve.wait_ge(*ps_free[key])
                    ts(nmax[0:P, b:b + 1], amax[0:P, b:b + 1], -1.0, None, ALU.mult).then_inc(mx_sb.sem, 1)
                else:
                    dve.tensor_reduce(nmax[0:P, b:b + 1], src, AX, ALU.max, negate=True).then_inc(mx_sb.sem, 1)

            def att_scale(n):
                P, b = TILES[att_units[n][2]], n % 3
                dve.wait_ge(*ex_sb[n])
                if n >= 3:
                    dve.wait_ge(*pe_full[("PT", n - 3)])
                chain(dve.reciprocal(rinv[0:P, b:b + 1], rsum[0:P, b:b + 1]))
                ts(diag[b][0:P, 0:P], ident[0:P, 0:P], rinv[0:P, b:b + 1], None, ALU.mult).then_inc(dg_sb.sem, 1)

            def att_own(n):
                _, P, k0 = att_rows(att_units[n][2])
                ps = filled(dve, ("PT", n))
                if n >= 2:
                    dve.wait_ge(*oT_ps[n - 2])
                copy(pT[k0:80, n % 2, 512:512 + P], ps[k0:80, 0:P]).then_inc(pT_b.sem, 1)

            def att_out(n):
                kind, h, i = att_units[n]
                P = TILES[i]
                dve.wait_ge(*oT_ps[n])
                dst = mixed((4 if kind == "fox" else 0) + h, i)
                copy(dst, psum[pair_of[("PT", n)]][:, 256:256 + P]).then_inc(ps_free.sem(("PT", n)), 1)

            def attention(first, last):
                for n in range(first, last + 3):
                    if n < last:
                        att_max(n)
                    if n - 3 >= first:
                        att_out(n - 3)
                    if first <= n - 2 < last:
                        att_own(n - 2)
                    if first <= n - 1 < last:
                        att_scale(n - 1)

            attention(0, 20)

            def layer_norm_tile(s, i):
                l, P, b = s // 2, TILES[i], i % 2
                r, src = rb[0:P, b, :], rb[0:P, b, :]
                if (s, i) > (0, 1):
                    ps_, pi = (s, i - 2) if i >= 2 else (s - 1, 4 if b == 0 else 3)
                    dve.wait_ge(*x_st[b][(ps_, pi)])
                    if ps_ < 3:
                        dve.wait_ge(*pe_full[("T", ps_, pi)])
                if s % 2 == 0:
                    key = ("wo", l, i)
                    dve.wait_ge(*xr_in[i][(s, i, 1 if (s == 0 and i == 4) else 0)])
                    stt(r, xr[0:P, b, :], ALPHA, filled(dve, key)[0:P, :], ALU.mult, ALU.add).then_inc(ps_free.sem(key), 1)
                    dve.wait_ge(*ps_free[key])
                else:
                    key = ("cb", l, i)
                    src = filled(dve, key)[0:P, :]
                st = lst[0:P, b, :]
                dve.bn_stats(st[:, 0:6], src[:, 0:512])
                chain(dve.bn_stats(st[:, 6:12], src[:, 512:1024]))
                dve.bn_aggr(lmv[0:P, b, :], st).then_inc(r_mv.sem, 1)
                dve.wait_ge(*lng_in[s])
                dve.wait_ge(*r_mv[(s, i)])
                centred = stt(r, src, lmv[0:P, b, 0:1], lng[0:P, 0, :], ALU.subtract, ALU.mult)
                if s % 2 == 1:
                    centred.then_inc(ps_free.sem(key), 1)
                    dve.wait_ge(*ps_free[key])
                else:
                    chain(centred)
                dve.wait_ge(*r_rs[(s, i)])
                stt(r, r, lrs[0:P, b, 1:2], lng[0:P, 1, :], ALU.mult, ALU.add).then_inc(r_sb.sem, 1)

            R = [rtile(n) for n in range(10)]
            f80 = lambda v: v.rearrange("p i e -> p (i e)")
            over_i = lambda v: v.unsqueeze(1).to_broadcast([128, NT, v.shape[1]])

            def router(l):
                n20 = lambda v: v.rearrange("p i (g j) -> p (i g) j", j=4)
                S = [f80(r)[:, 0:20] for r in R]
                dve.wait_ge(*r_e[l])
                chain(ts(sc_, sc_, 1.0, None, ALU.add))
                chain(dve.reciprocal(sc_, sc_))
                chain(tt(R[0], sc_, over_i(rbias), ALU.add))
                q = n20(R[0])
                tt(S[1], q[:, :, 0], q[:, :, 1], ALU.max)
                tt(S[2], q[:, :, 0], q[:, :, 1], ALU.min)
                tt(S[3], q[:, :, 2], q[:, :, 3], ALU.max)
                chain(tt(S[4], q[:, :, 2], q[:, :, 3], ALU.min))
                tt(S[5], S[1], S[3], ALU.max)
                tt(S[6], S[1], S[3], ALU.min)
                chain(tt(S[7], S[2], S[4], ALU.max))
                chain(tt(S[6], S[6], S[7], ALU.max))
                g = gs.rearrange("p i e -> p (i e)")
                chain(tt(g, S[5], S[6], ALU.add))
                chain(dve.tensor_reduce(t5a, gs, AX, ALU.max))
                chain(tt(gs2, gs, bc(t5a, 4), ALU.is_equal))
                chain(tt(gs2, gs2, over_i(const("prio4")), ALU.mult))
                chain(dve.tensor_reduce(t5b, gs2, AX, ALU.max))
                chain(tt(gs2, gs2, bc(t5b, 4), ALU.is_equal))
                chain(tt(n20(R[1]), q, bc(gs2.rearrange("p i e -> p (i e)"), 4), ALU.mult))
                chain(ts(gs2, gs2, -NEG, NEG, ALU.mult, ALU.add))
                chain(tt(n20(R[1]), n20(R[1]), bc(gs2.rearrange("p i e -> p (i e)"), 4), ALU.add))
                for c, sel in ((0, sel1), (1, mk)):
                    chain(dve.tensor_reduce(t5a, R[1], AX, ALU.max))
                    chain(tt(R[2], R[1], bc(t5a, NE), ALU.is_equal))
                    chain(tt(R[2], R[2], over_i(const("prio16")), ALU.mult))
                    chain(dve.tensor_reduce(t5b, R[2], AX, ALU.max))
                    chain(tt(sel, R[2], bc(t5b, NE), ALU.is_equal))
                    if c == 0:
                        chain(stt(f80(R[1]), f80(sel), 2 * NEG, f80(R[1]), ALU.mult, ALU.add))
                    chain(tt(sel, sel, bc(const("valid"), NE), ALU.mult))
                chain(copy(R[4], mk))
                chain(tt(mk, mk, sel1, ALU.add))
                copy(maskb[:, :], f80(mk)).then_inc(mk_sb.sem, 1)
                key = ("rk", l)
                ps = filled(dve, key)
                stt(f80(rk1), ps[:, 0:80], 1.0, f80(mk), ALU.add, ALU.mult)
                copy(f80(R[5]), ps[:, 0:80])
                copy(cnt, ps[:, 80:96]).then_inc(ps_free.sem(key), 1)
                dve.wait_ge(*ps_free[key])
                for g in range(2):
                    onehots(l, g)
                    slot_tokens(l, g)

            def slots_and_weights(l):
                for c, sel in ((0, sel1), (1, R[4])):
                    chain(tt(R[3], sel, sc_, ALU.mult))
                    chain(dve.tensor_reduce(wts[:, c, :], R[3], AX, ALU.add))
                chain(tt(t5a, wts[:, 0, :], wts[:, 1, :], ALU.add))
                chain(ts(t5a, t5a, 1e-37, None, ALU.max))
                chain(dve.reciprocal(t5a, t5a))
                chain(tt(wts, wts, t5a.unsqueeze(1).to_broadcast([128, 2, NT]), ALU.mult))
                chain(ts(ovn, cnt, 128.0, None, ALU.is_gt))
                for m in (256.0, 384.0, 512.0):
                    chain(stt(ovn, cnt, m, ovn, ALU.is_gt, ALU.add))
                chain(dve.tensor_tensor_scan(ovend, const("ones")[:, 0:NE], ovn, 0.0, ALU.mult, ALU.add))
                copy(ovi[:, 0:1], ovend[:, NE - 1:NE])
                chain(tt(cnt, ovend, ovn, ALU.subtract))
                chain(ts(cnt, cnt, 128.0, float(NE * 128 - 128), ALU.mult, ALU.add))
                chain(tt(ovn, const("base"), cnt, ALU.subtract))
                chain(ts(R[6], R[5], 128.0, None, ALU.is_lt))
                chain(tt(R[7], R[6], over_i(ovn), ALU.mult))
                chain(tt(R[7], R[7], over_i(cnt), ALU.add))
                chain(tt(R[7], R[7], R[5], ALU.add))
                for c, sel in ((0, sel1), (1, R[4])):
                    chain(tt(R[8], R[7], sel, ALU.mult))
                    chain(dve.tensor_reduce(posf[:, c, :], R[8], AX, ALU.add))
                chain(copy(posi, posf))

            def onehots(l, g):
                for e in IX_GROUPS[g]:
                    for i in range(NT):
                        last = ts(oneh[:, e % 2, i, :], iotab[:, :], 1.0, rk1[:, i, e:e + 1], ALU.add, ALU.is_equal)
                    last.then_inc(oh_sb.sem, 1)

            def slot_tokens(l, g):
                slotf, group = f80(R[9])[:, 0:NE], IX_GROUPS[g]
                key, es = ("ix", l, g), slice(group[0], group[-1] + 1)
                ps = filled(dve, key)[:, 512:512 + 2 * NE].rearrange("p (e c) -> p e c", c=2)
                chain(copy(slotf[:, es], ps[:, es, 1]))
                stt(slotf[:, es], ps[:, es, 0], 128.0, slotf[:, es], ALU.mult, ALU.add).then_inc(ps_free.sem(key), 1)
                dve.wait_ge(*ps_free[key])
                copy(sloti[:, es], slotf[:, es]).then_inc(ix_sb.sem, 1)

            def experts(l):
                def rows_copy(e):
                    dve.wait_ge(*xgT_ps[(l, e)])
                    if e >= 2:
                        dve.wait_ge(*gu_ps[(l, e - 2)])
                    copy(xgT[:, e % 2, 4:8, :], psum[0][:, 512:1024].rearrange("p (k n) -> p k n", k=4)).then_inc(xgT_sd.sem, 1)

                def hidden(e):
                    b, lo = e % 2, 512 * (e % 2)
                    g_, u_ = psum[1][:, lo:lo + 256], psum[1][:, lo + 256:lo + 512]
                    dve.wait_ge(*eg_sb[(l, e)])
                    if e >= 2:
                        dve.wait_ge(*hT_ps[(l, e - 2)])
                    chain(ts(eg[:, b, :], eg[:, b, :], 1.0, None, ALU.add))
                    chain(dve.reciprocal(eg[:, b, :], eg[:, b, :]))
                    chain(tt(eg[:, b, :], g_, eg[:, b, :], ALU.mult))
                    tt(hb[:, b, :], u_, eg[:, b, :], ALU.mult).then_inc(h_sb.sem, 1)

                rows_copy(0)
                for e in range(NE + 1):
                    if e >= 1:
                        dve.wait_ge(*hT_ps[(l, e - 1)])
                        if e >= 3:
                            dve.wait_ge(*dn_ps[(l, e - 3)])
                        copy(hT[:, (e - 1) % 2, :], psum[3][:, 0:256]).then_inc(hT_sb.sem, 1)
                    if e + 1 < NE:
                        rows_copy(e + 1)
                    if e < NE:
                        hidden(e)
                    if 1 <= e < LAST_IX:
                        slot_tokens(l, e + 1)
                    if e < LAST_IX - 1:
                        onehots(l, e + 2)
                    if e == 3:
                        slots_and_weights(l)
                    if e >= 1:
                        dve.wait_ge(*dn_ps[(l, e - 1)])
                        if e >= 3:
                            dve.wait_ge(*y_st[(e - 1) % 2][(l, e - 3)])
                        copy(yb[:, (e - 1) % 2, 512:1024], psum[2][:, 512:1024]).then_inc(y_sd.sem, 1)
                m = ov[l]
                dve.memset(cur[:, 0:1], float(NE * 128))
                chain(dve.memset(cur[:, 1:2], 0.0))
                dve.wait_ge(*y_st[1][(l, NE - 1)])
                dve.wait_ge(*y_st[0][(l, NE - 2)])
                count = dve.value_load(ovi[0:1, 0:1], min_val=0, max_val=NOV)
                with dve.Fori(0, NOV) as b:
                    with dve.If(count > b):
                        steps = [0]

                        def step(ins):
                            steps[0] += 1
                            ins.then_inc(m["cnt"], 1)
                            dve.wait_ge(m["cnt"], b * STEPS + steps[0])

                        STEPS = 10
                        for c in range(2):
                            for i in range(NT):
                                last = ts(oneh[:, c, i, :], iotab[:, :], cur[:, 0:1], posf[:, c, i:i + 1],
                                          ALU.add, ALU.is_equal)
                        last.then_inc(m["oh"], 1)
                        step(ts(ovn, ovend, cur[:, 1:2], None, ALU.is_le))
                        step(dve.tensor_reduce(cur[:, 2:3], ovn, AX, ALU.add))
                        step(ts(ovi[:, 1:2], cur[:, 2:3], float(NE - 1), None, ALU.min))
                        dve.wait_ge(m["ix"], b + 1)
                        step(copy(cur[:, 3:4], psum[3][:, 513:514]))
                        step(stt(cur[:, 3:4], psum[3][:, 512:513], 128.0, cur[:, 3:4], ALU.mult, ALU.add))
                        copy(ovi[:, 2:3], cur[:, 3:4]).then_inc(m["id"], 1)
                        dve.wait_ge(m["tx"], b + 1)
                        copy(xgT[:, 0, :, :], psum[0][:, :].rearrange("p (k n) -> p k n", k=KD)).then_inc(m["xt"], 1)
                        dve.wait_ge(m["ex"], b + 1)
                        step(ts(eg[:, 0, :], eg[:, 0, :], 1.0, None, ALU.add))
                        step(dve.reciprocal(eg[:, 0, :], eg[:, 0, :]))
                        step(tt(eg[:, 0, :], psum[1][:, 0:256], eg[:, 0, :], ALU.mult))
                        tt(hb[:, 0, :], psum[1][:, 256:512], eg[:, 0, :], ALU.mult).then_inc(m["h"], 1)
                        step(ts(cur[:, 0:1], cur[:, 0:1], 128.0, None, ALU.add))
                        step(ts(cur[:, 1:2], cur[:, 1:2], 1.0, None, ALU.add))
                        dve.wait_ge(m["ht"], b + 1)
                        copy(hT[:, 0, :], psum[3][:, 0:256]).then_inc(m["hs"], 1)
                        dve.wait_ge(m["dn"], b + 1)
                        copy(yb[:, 0, :], psum[2][:, :]).then_inc(m["y"], 1)
                        assert steps[0] == STEPS

            def out_and_experts(l):
                for i in range(NT):
                    if i >= 2:
                        logits_copy(l, i - 2)
                    layer_norm_tile(2 * l, i)
                logits_copy(l, NT - 2)
                logits_copy(l, NT - 1)
                router(l)
                experts(l)
                for i in range(NT):
                    layer_norm_tile(2 * l + 1, i)

            def logits_copy(l, i):
                key = ("lg", l, i)
                P = TILES[i]
                copy(lg[0:P, i, :], filled(dve, key)[0:P, 0:NE]).then_inc(ps_free.sem(key), 1)
                dve.wait_ge(*ps_free[key])

            out_and_experts(0)
            rt = lambda P, n: rtmp[0:P, n, :]
            for i in range(NT):
                P, b, key = TILES[i], i % 2, ("mi", i)
                ps = filled(dve, key)
                if i == 0:
                    dve.wait_ge(mg_in.sem, 32)
                dve.wait_ge(*mi_a[i])
                if i >= 1:
                    dve.wait_ge(*mi_sb[i - 1])
                if i >= 2:
                    dve.wait_ge(*pe_full[("mt", i - 2)])
                    dve.wait_ge(mi_st[b].sem, 32 * (i // 2))
                stt(cqb[0:P, b, :], ps[0:P, 0:QL], mst[0:P, b, 2:3], qng[0:P, 0:QL], ALU.mult, ALU.mult)
                stt(cvb[0:P, b, :], ps[0:P, QL:QL + KVL], mst[0:P, b, 3:4], qng[0:P, QL:QL + KVL], ALU.mult, ALU.mult)
                x1, x2 = ps[0:P, 768:800], ps[0:P, 800:832]
                tt(rt(P, 0)[:, 0:32], x1, cos[0:P, i, :], ALU.mult)
                tt(rt(P, 1)[:, 0:32], x2, sin[0:P, i, :], ALU.mult)
                tt(rt(P, 2)[:, 0:32], x1, sin[0:P, i, :], ALU.mult)
                tt(rt(P, 3)[:, 0:32], x2, cos[0:P, i, :], ALU.mult).then_inc(ps_free.sem(key), 1)
                dve.wait_ge(*ps_free[key])
                for lo in (0, 64):
                    tt(kpb[0:P, b, lo:lo + 32], rt(P, 0)[:, 0:32], rt(P, 1)[:, 0:32], ALU.subtract)
                    last = tt(kpb[0:P, b, lo + 32:lo + 64], rt(P, 2)[:, 0:32], rt(P, 3)[:, 0:32], ALU.add)
                last.then_inc(mi_sb.sem, 1)
            dve.wait_ge(*mi_sb[NT - 1])
            for i in range(NT):
                P, b, key = TILES[i], i % 2, ("qp", i)
                ps = filled(dve, key)[0:P, 0:512].rearrange("p (h s d) -> p h s d", h=MH, s=2)
                v = lambda n: rt(P, n).rearrange("p (h d) -> p h d", h=MH)
                cs, sn = (t[0:P, i, :].unsqueeze(1).to_broadcast([P, MH, 32]) for t in (cos, sin))
                if i >= 1:
                    dve.wait_ge(*qp_sb[i - 1])
                if i >= 2:
                    dve.wait_ge(*pe_full[("qt", i - 2)])
                tt(v(0), ps[:, :, 0, :], cs, ALU.mult)
                tt(v(1), ps[:, :, 1, :], sn, ALU.mult)
                tt(v(2), ps[:, :, 0, :], sn, ALU.mult)
                tt(v(3), ps[:, :, 1, :], cs, ALU.mult).then_inc(ps_free.sem(key), 1)
                dve.wait_ge(*ps_free[key])
                out = qpb[0:P, b, :].rearrange("p (h s d) -> p h s d", h=MH, s=2)
                tt(out[:, :, 0, :], v(0), v(1), ALU.subtract)
                tt(out[:, :, 1, :], v(2), v(3), ALU.add).then_inc(qp_sb.sem, 1)
            attention(20, 40)
            attention(40, 60)
            out_and_experts(1)


_INS = ['x_prompt', 'x_sample', 'state_hgrn2', 'cache_fox_k', 'cache_fox_v', 'cache_fox_logf', 'cache_mla_ckv',
        'cache_mla_kpe', 'meta_tokens', 'even_w_in', 'hg_lb_logits', 'hg_norm_g', 'fox_forget_bias', 'even_w_out',
        'mla_w_in', 'mla_q_norm_g', 'mla_kv_norm_g', 'mla_w_uq', 'mla_w_uk', 'mla_w_uv', 'mla_w_out', 'ln_mix_g',
        'ln_mix_b', 'ln_ffn_g', 'ln_ffn_b', 'router_w', 'router_bias', 'moe_w_gate', 'moe_w_up', 'moe_w_down']
_L = NM + SEQ
_OUTS = [(1, SEQ, D), (1, NS, D), (1, 1, HH, DH, DH), (1, 1, _L, FH, DH), (1, 1, _L, FH, DH), (1, 1, _L, FH),
         (1, 1, _L, KVL), (1, 1, _L, ROPE), (1, 1, HH, DH, DH), (1, 1, NS, FH, DH), (1, 1, NS, FH, DH),
         (1, 1, NS, FH), (1, 1, NS, KVL), (1, 1, NS, ROPE)]


def kernel(**inputs):
    import concourse.bacc as _bacc
    from concourse.bass_utils import run_bass_kernel_spmd as _run

    nc = _bacc.Bacc("TRN2", target_bir_lowering=False, num_devices=1)
    blob, where = shape_constants()
    arrays, args = {"shape_constants": blob}, {}
    consts = nc.dram_tensor("shape_constants", blob.shape, F32, kind="ExternalInput").ap()
    for name in _INS:
        x = np.ascontiguousarray(inputs[name])
        arrays[f"in_{name}"] = x
        args[name] = nc.dram_tensor(f"in_{name}", x.shape, mybir.dt.from_np(x.dtype), kind="ExternalInput").ap()
    outs = [nc.dram_tensor(f"out_{i}", s, F32, kind="ExternalOutput").ap() for i, s in enumerate(_OUTS)]
    build_step(nc, where, consts, args, outs)
    r = _run(nc, [arrays], core_ids=[0])
    return tuple(r.results[0][f"out_{i}"] for i in range(len(_OUTS)))
```
